# Optimizing a Trainium2 kernel written in Bass

```python
import math
import jax, jax.numpy as jnp
from jax import lax
import numpy as np

D_MODEL = 1024
BATCH = 1
SEQ = 512
DEPTH = 1
DEC_BATCH = 1
DEC_SEQ = 1024
PAST_LEN = 128

HEAD_DIM = 64
N_HEADS = D_MODEL // HEAD_DIM
A_HEADS = N_HEADS // 2
A_KV_HEADS = 2
A_GROUP = A_HEADS // A_KV_HEADS
A_RADIUS = 128
B_HEADS = N_HEADS - A_HEADS
B_DILATIONS = ((128, 1), (512, 4), (2048, 16))
A_WIDTH = A_HEADS * HEAD_DIM
A_KV_WIDTH = A_KV_HEADS * HEAD_DIM
B_WIDTH = B_HEADS * HEAD_DIM
MIX_WIDTH = A_WIDTH + B_WIDTH
IN_WIDTH = A_WIDTH + 2 * A_KV_WIDTH + 3 * B_WIDTH
N_EXPERTS = 16
N_GROUPS = 4
EXPERTS_PER_GROUP = N_EXPERTS // N_GROUPS
TOP_K = 2
D_EXPERT = 256
D_SHARED = 256
DEEPNORM_ALPHA = (2 * DEPTH) ** 0.25
DEEPNORM_BETA = (8 * DEPTH) ** -0.25
LN_EPS = 1e-5
RMS_EPS = 1e-6

kernel_name = "hybrid_bidir_window_dilated_moe_encoder"

def alibi_slopes():
    h = jnp.arange(1, N_HEADS + 1, dtype=jnp.float32)
    return jnp.exp2(-8.0 * h / N_HEADS)

def layer_norm(x, g, b):
    xf = x.astype(jnp.float32)
    mu = xf.mean(-1, keepdims=True)
    var = jnp.square(xf - mu).mean(-1, keepdims=True)
    return ((xf - mu) * lax.rsqrt(var + LN_EPS) * g.astype(jnp.float32) + b.astype(jnp.float32)).astype(x.dtype)

def rms_norm(x, g):
    xf = x.astype(jnp.float32)
    ms = jnp.square(xf).mean(-1, keepdims=True)
    return (xf * lax.rsqrt(ms + RMS_EPS) * g.astype(jnp.float32)).astype(x.dtype)

def banded_attention(q, k, v, radius, slopes, dist_scale, sink=None):
    bsz, L, G, R, hd = q.shape
    blk = radius
    nb = -(-L // blk)
    Lp = nb * blk
    qb = jnp.pad(q, ((0, 0), (0, Lp - L), (0, 0), (0, 0), (0, 0))).reshape(bsz, nb, blk, G, R, hd).astype(jnp.float32)
    padk = ((0, 0), (blk, Lp - L + blk), (0, 0), (0, 0))
    kp = jnp.pad(k, padk).reshape(bsz, nb + 2, blk, G, hd).astype(jnp.float32)
    vp = jnp.pad(v, padk).reshape(bsz, nb + 2, blk, G, hd).astype(jnp.float32)

    def band(t):
        return jnp.concatenate([t[:, :-2], t[:, 1:-1], t[:, 2:]], axis=2)

    kb, vb = band(kp), band(vp)
    s = jnp.einsum('bnqgrd,bnkgd->bngrqk', qb, kb) * (hd ** -0.5)
    qpos = jnp.arange(nb)[:, None] * blk + jnp.arange(blk)[None, :]
    kpos = (jnp.arange(nb)[:, None] - 1) * blk + jnp.arange(3 * blk)[None, :]
    rel = kpos[:, None, :] - qpos[:, :, None]
    valid = (jnp.abs(rel) <= radius) & (kpos[:, None, :] >= 0) & (kpos[:, None, :] < L)
    dist = jnp.abs(rel).astype(jnp.float32) * dist_scale
    s = s - slopes.astype(jnp.float32)[None, None, :, :, None, None] * dist[None, :, None, None]
    s = jnp.where(valid[None, :, None, None], s, -jnp.inf)
    m = s.max(-1)
    if sink is not None:
        sk = sink.astype(jnp.float32)[None, None, :, :, None]
        m = jnp.maximum(m, sk)
    p = jnp.exp(s - m[..., None])
    denom = p.sum(-1)
    if sink is not None:
        denom = denom + jnp.exp(sk - m)
    o = jnp.einsum('bngrqk,bnkgd->bnqgrd', p, vb) / jnp.transpose(denom, (0, 1, 4, 2, 3))[..., None]
    o = o.reshape(bsz, Lp, G, R, hd)[:, :L]
    lse = jnp.transpose(m + jnp.log(denom), (0, 1, 4, 2, 3)).reshape(bsz, Lp, G, R)[:, :L]
    return o, lse

def dilated_attention(q, k, v, slopes):
    bsz, L, H, hd = q.shape
    outs, lses = [], []
    for window, d in B_DILATIONS:
        Ld = L // d

        def strided(t):
            return t.reshape(bsz, Ld, d, H, hd).transpose(0, 2, 1, 3, 4).reshape(bsz * d, Ld, H, hd)

        o, lse = banded_attention(strided(q)[:, :, :, None], strided(k), strided(v),
                                  (window // 2) // d, slopes[:, None], float(d))
        outs.append(o.reshape(bsz, d, Ld, H, hd).transpose(0, 2, 1, 3, 4).reshape(bsz, L, H, hd))
        lses.append(lse.reshape(bsz, d, Ld, H).transpose(0, 2, 1, 3).reshape(bsz, L, H))
    w = jax.nn.softmax(jnp.stack(lses, 0), axis=0)
    return jnp.einsum('cblh,cblhd->blhd', w, jnp.stack(outs, 0))

def mixer(x, w_in, sink, norm_a, norm_b, w_out):
    bsz, L, _ = x.shape
    proj = x @ w_in
    cuts = [A_WIDTH, A_WIDTH + A_KV_WIDTH, A_WIDTH + 2 * A_KV_WIDTH,
            A_WIDTH + 2 * A_KV_WIDTH + B_WIDTH, A_WIDTH + 2 * A_KV_WIDTH + 2 * B_WIDTH]
    qa, ka, va, qb, kb, vb = jnp.split(proj, cuts, axis=-1)
    slopes = alibi_slopes()
    oa, _ = banded_attention(qa.reshape(bsz, L, A_KV_HEADS, A_GROUP, HEAD_DIM),
                             ka.reshape(bsz, L, A_KV_HEADS, HEAD_DIM),
                             va.reshape(bsz, L, A_KV_HEADS, HEAD_DIM),
                             A_RADIUS, slopes[0::2].reshape(A_KV_HEADS, A_GROUP), 1.0,
                             sink.reshape(A_KV_HEADS, A_GROUP))
    ob = dilated_attention(qb.reshape(bsz, L, B_HEADS, HEAD_DIM), kb.reshape(bsz, L, B_HEADS, HEAD_DIM),
                           vb.reshape(bsz, L, B_HEADS, HEAD_DIM), slopes[1::2])
    oa = rms_norm(oa.reshape(bsz, L, A_WIDTH).astype(x.dtype), norm_a)
    ob = rms_norm(ob.reshape(bsz, L, B_WIDTH).astype(x.dtype), norm_b)
    return jnp.concatenate([oa, ob], axis=-1) @ w_out

def moe(x, w_router, router_bias, w_gate, w_up, w_down, ws_gate, ws_up, ws_down):
    shp = x.shape
    xt = x.reshape(-1, shp[-1])
    scores = jax.nn.sigmoid((xt @ w_router).astype(jnp.float32))
    biased = scores + router_bias.astype(jnp.float32)
    group_score = lax.top_k(biased.reshape(-1, N_GROUPS, EXPERTS_PER_GROUP), TOP_K)[0].sum(-1)
    sel_group = jnp.argmax(group_score, axis=-1)
    in_group = (jnp.arange(N_EXPERTS) // EXPERTS_PER_GROUP)[None, :] == sel_group[:, None]
    _, idx = lax.top_k(jnp.where(in_group, biased, -jnp.inf), TOP_K)
    sel = jnp.take_along_axis(scores, idx, axis=-1)
    sel = sel / sel.sum(-1, keepdims=True)
    gates = (jax.nn.one_hot(idx, N_EXPERTS, dtype=jnp.float32) * sel[..., None]).sum(1)
    h = jax.nn.silu(jnp.einsum('nd,edf->nef', xt, w_gate)) * jnp.einsum('nd,edf->nef', xt, w_up)
    h = h * gates[..., None].astype(h.dtype)
    y = jnp.einsum('nef,efd->nd', h, w_down)
    shared = (jax.nn.silu(xt @ ws_gate) * (xt @ ws_up)) @ ws_down
    return (y + shared).reshape(shp)

def trunk(x, w_in, sink_a, norm_a, norm_b, w_out, ln1_g, ln1_b, w_router, router_bias,
          w_gate, w_up, w_down, ws_gate, ws_up, ws_down, ln2_g, ln2_b):
    for l in range(DEPTH):
        x = layer_norm(DEEPNORM_ALPHA * x + mixer(x, w_in[l], sink_a[l], norm_a[l], norm_b[l], w_out[l]),
                       ln1_g[l], ln1_b[l])
        x = layer_norm(DEEPNORM_ALPHA * x + moe(x, w_router, router_bias, w_gate[l], w_up[l], w_down[l],
                                                 ws_gate[l], ws_up[l], ws_down[l]),
                       ln2_g[l], ln2_b[l])
    return x

def setup_inputs(seed: int = 0) -> dict:
    key = jax.random.key(seed)
    ks = jax.random.split(key, 22)
    nrm = jax.random.normal
    f32 = jnp.float32
    col_scale = jnp.concatenate([
        jnp.ones((A_WIDTH + A_KV_WIDTH,), f32),
        jnp.full((A_KV_WIDTH,), DEEPNORM_BETA, f32),
        jnp.ones((2 * B_WIDTH,), f32),
        jnp.full((B_WIDTH,), DEEPNORM_BETA, f32)])
    return {
        "x_prompt": nrm(ks[0], (BATCH, SEQ, D_MODEL), f32),
        "x_sample": nrm(ks[1], (DEC_BATCH, DEC_SEQ, D_MODEL), f32),
        "w_in": nrm(ks[2], (DEPTH, D_MODEL, IN_WIDTH), f32) * D_MODEL ** -0.5 * col_scale,
        "sink_a": nrm(ks[3], (DEPTH, A_HEADS), f32),
        "norm_a": 1.0 + 0.02 * nrm(ks[4], (DEPTH, A_WIDTH), f32),
        "norm_b": 1.0 + 0.02 * nrm(ks[5], (DEPTH, B_WIDTH), f32),
        "w_out": nrm(ks[6], (DEPTH, MIX_WIDTH, D_MODEL), f32) * MIX_WIDTH ** -0.5 * DEEPNORM_BETA,
        "ln1_g": 1.0 + 0.02 * nrm(ks[7], (DEPTH, D_MODEL), f32),
        "ln1_b": 0.02 * nrm(ks[8], (DEPTH, D_MODEL), f32),
        "w_router": nrm(ks[9], (D_MODEL, N_EXPERTS), f32) * D_MODEL ** -0.5,
        "router_bias": 0.01 * nrm(ks[10], (N_EXPERTS,), f32),
        "w_gate": nrm(ks[11], (DEPTH, N_EXPERTS, D_MODEL, D_EXPERT), f32) * D_MODEL ** -0.5,
        "w_up": nrm(ks[12], (DEPTH, N_EXPERTS, D_MODEL, D_EXPERT), f32) * D_MODEL ** -0.5,
        "w_down": nrm(ks[13], (DEPTH, N_EXPERTS, D_EXPERT, D_MODEL), f32) * D_EXPERT ** -0.5 * DEEPNORM_BETA,
        "ws_gate": nrm(ks[14], (DEPTH, D_MODEL, D_SHARED), f32) * D_MODEL ** -0.5,
        "ws_up": nrm(ks[15], (DEPTH, D_MODEL, D_SHARED), f32) * D_MODEL ** -0.5,
        "ws_down": nrm(ks[16], (DEPTH, D_SHARED, D_MODEL), f32) * D_SHARED ** -0.5 * DEEPNORM_BETA,
        "ln2_g": 1.0 + 0.02 * nrm(ks[17], (DEPTH, D_MODEL), f32),
        "ln2_b": 0.02 * nrm(ks[18], (DEPTH, D_MODEL), f32),
    }

def reference(x_prompt, x_sample, w_in, sink_a, norm_a, norm_b, w_out, ln1_g, ln1_b, w_router, router_bias,
              w_gate, w_up, w_down, ws_gate, ws_up, ws_down, ln2_g, ln2_b):
    y_prompt = trunk(x_prompt, w_in, sink_a, norm_a, norm_b, w_out, ln1_g, ln1_b, w_router, router_bias,
                     w_gate, w_up, w_down, ws_gate, ws_up, ws_down, ln2_g, ln2_b)
    y_sample = trunk(x_sample, w_in, sink_a, norm_a, norm_b, w_out, ln1_g, ln1_b, w_router, router_bias,
                     w_gate, w_up, w_down, ws_gate, ws_up, ws_down, ln2_g, ln2_b)
    return (y_prompt, y_sample)


_drawn_inputs = setup_inputs


def setup_inputs(seed=0):
    import zlib

    import numpy as np

    out = dict(_drawn_inputs(seed))
    spreads = {}
    factors = {}
    for name, (base, spread) in spreads.items():
        noise = np.random.default_rng([zlib.crc32(name.encode()), seed]).standard_normal(out[name].shape)
        drawn = base * np.exp(spread * noise) if base else spread * noise
        out[name] = __import__('jax').numpy.asarray(drawn.astype(out[name].dtype))
    for name, factor in factors.items():
        out[name] = (out[name] * factor).astype(out[name].dtype)
    return out
```

```python
import numpy as np
import concourse.bass as bass
from concourse import mybir
from contextlib import ExitStack

FP32 = mybir.dt.float32
I32 = mybir.dt.int32
U32 = mybir.dt.uint32
ALU = mybir.AluOpType
ACT = mybir.ActivationFunctionType
AX = mybir.AxisListType

P = 128
D = 1024
KD = D // P
SEQS = ((0, 512), (512, 1024))
TOKENS = 1536
TILES = TOKENS // P
GROUPS = TOKENS // 512
HD = 64
PAIRS = 4
OW = HD + 2
NE = 16
NGRP = 4
DE = 256
ALPHA = 2.0 ** 0.25
LN_EPS = 1e-5
RMS_EPS = 1e-6
A_RADIUS = 128
B_RADIUS = 64
SLOT_TILES = 2 * TILES + NE
QA0, KA0, VA0, QB0, KB0, VB0 = 0, 512, 640, 768, 1280, 1792
UNITS = 72
BIG = 3.0e38


def constants():
    h = np.arange(1, 17, dtype=np.float32)
    slopes = np.exp2(-8.0 * h / 16).astype(np.float32)
    p = np.arange(P)[:, None]
    hd8 = np.float32(8.0)

    def table(step, ok, slope, mult=None):
        t = -slope * np.abs(step).astype(np.float32)
        if mult is not None:
            t = t + np.log(np.maximum(mult, 1)).astype(np.float32)
        return np.where(ok, hd8 * t, np.float32(-1e37)).astype(np.float32)

    rel_a = np.arange(384)[None, :] - 128 - p
    rel_1 = np.arange(256)[None, :] - 64 - p
    rel_2 = np.arange(384)[None, :] - 128 - p
    mult2 = (np.abs(rel_2) <= B_RADIUS).astype(np.float32) + (rel_2 % 4 == 0)
    tab_a = np.stack([np.stack([table(rel_a, np.abs(rel_a) <= A_RADIUS, slopes[0::2][i + 4 * half])
                                for half in range(2)], 1) for i in range(PAIRS)])
    tab_1 = np.stack([np.stack([table(rel_1, np.abs(rel_1) <= B_RADIUS, slopes[1::2][2 * i + half])
                                for half in range(2)], 1) for i in range(PAIRS)])
    tab_2 = np.stack([np.stack([table(4 * rel_2, mult2 > 0, slopes[1::2][2 * i + half], mult2)
                                for half in range(2)], 1) for i in range(PAIRS)])
    row = np.zeros((P, 512), np.float32)
    row[:, 0:128] = np.eye(P)
    row[:, 128:256] = np.arange(P)[:, None] < np.arange(P)[None, :]
    row[:, 256:384] = np.arange(P)[None, :]
    row[:, 384:384 + SLOT_TILES] = np.arange(SLOT_TILES)[None, :]
    row[:, 428:428 + TILES] = np.arange(TILES)[None, :] * P + np.arange(P)[:, None]
    row[:, 444:448] = 3 - np.arange(4)[None, :]
    return {"tab_a": tab_a, "tab_1": tab_1, "tab_2": tab_2, "const": row}


def encoder_layer(nc, x, w_in, sink, norm_a, norm_b, w_out, ln1_g, ln1_b, w_router, router_bias,
                  w_gate, w_up, w_down, ws_gate, ws_up, ws_down, ln2_g, ln2_b,
                  tab_a, tab_1, tab_2, const, out):
    vb_d = nc.dram_tensor("vb_scratch", (TOKENS, 512), FP32, kind="Internal").ap()
    o_d = nc.dram_tensor("o_scratch", (TOKENS, 3 * PAIRS * 2 * OW), FP32, kind="Internal").ap()
    x1_d = nc.dram_tensor("x1_scratch", (TOKENS, D), FP32, kind="Internal").ap()
    y_d = nc.dram_tensor("y_scratch", (SLOT_TILES * P, D), FP32, kind="Internal").ap()

    ctx = ExitStack()
    with ctx:
        ARENA = 52700
        arena = ctx.enter_context(nc.sbuf_tensor("arena", [P, ARENA], FP32))

        def place(at, *dims):
            n = int(np.prod(dims))
            v = arena[:, at:at + n]
            if len(dims) == 2:
                v = v.rearrange("p (a b) -> p a b", b=dims[1])
            if len(dims) == 3:
                v = v.rearrange("p (a b c) -> p a b c", b=dims[1], c=dims[2])
            assert at + n <= ARENA
            return v, at + n

        cst, at = place(0, 512)
        ident, tri, iota_p = cst[:, 0:128], cst[:, 128:256], cst[:, 256:384]
        iota_j, token_id = cst[:, 384:384 + SLOT_TILES], cst[:, 428:428 + TILES]
        rank0 = cst[:, 444:448]
        logits, at = place(at, TILES, NE)
        w_rt, at = place(at, KD, NE)
        rbias, at = place(at, NE)
        nsink, at = place(at, 8)
        gains, at = place(at, KD)
        minus_half, at = place(at, 1)
        ones, at = place(at, P)
        r1 = at
        w_v, at = place(r1, KD, 640)
        xin, at = place(at, 2, D)
        xts, at = place(at, 2, KD, P)
        vst, at = place(at, 2, 512)
        r2 = at
        w_o, at = place(r1, KD, D)
        ln1g, at = place(at, D)
        ln1b, at = place(at, D)
        assert at <= r2
        xT, r3 = place(r2, KD, TOKENS)
        base, _ = place(r2, TILES, D)
        ws_gu, at = place(r3, KD, 2 * DE)
        ws_d, r4 = place(at, 2, D)
        Va, at = place(r4, TILES, P)
        V1, at = place(at, 14, P)
        V2, at = place(at, TILES, P)
        ost = [None] * 3
        for k in range(3):
            ost[k], at = place(at, TILES, 2, OW)
        QA, at = place(at, TOKENS)
        KA, at = place(at, TOKENS)
        QB, at = place(at, TOKENS)
        KB, at = place(at, TOKENS)
        wqa, at = place(at, KD, P)
        wqb, at = place(at, KD, P)
        wkb, at = place(at, KD, P)
        tA, at = place(at, 2, 384)
        t1, at = place(at, 2, 256)
        t2, at = place(at, 2, 384)
        prob, at = place(at, 2, 384)
        probT, at = place(at, 2, 384)
        wka = ost[0].rearrange("p a b c -> p (a b c)")[:, 0:1024].rearrange("p (k c) -> p k c", c=P)
        odt, at = place(r4, 2, 3 * PAIRS * 2 * OW)
        xr, at = place(at, 2, D)
        om, at = place(at, 2, D)
        oTs, at = place(at, 2, KD, P)
        res, at = place(at, D)
        x1s, at = place(at, 2, D)
        x1T, at = place(at, 2, KD, P)
        eg, at = place(at, 2, DE)
        hid, at = place(at, 2, DE)
        hTs, at = place(at, 2, 2, P)
        junk, at = place(at, 512)
        junk2, at = place(at, 512)
        mD, at = place(at, 4, 8)
        mM, at = place(at, 2, 8)
        mL, at = place(at, 3, 8)
        mR, at = place(at, 2, 8)
        mW, at = place(at, 3, 8)
        ssq, at = place(at, 2, 2)
        rms, at = place(at, 2, 2)
        bst, at = place(at, 2, 6)
        mv, at = place(at, 2, 2)
        rstd, at = place(at, 2, 1)
        c_end = at
        score, at = place(c_end, TILES, NE)
        rank, at = place(at, TILES, NE)
        cmp_, at = place(at, TILES, NE)
        bia, at = place(at, TILES, NE)
        gsc, at = place(at, TILES, NGRP)
        grank, at = place(at, TILES, NGRP)
        gcmp, at = place(at, TILES, NGRP)
        msk, at = place(at, TILES + 1, NE)
        msc, at = place(at, TILES, NE)
        slot, at = place(at, TILES, NE)
        den, at = place(at, TILES)
        two, at = place(at, TILES, 2)
        gate, at = place(at, TILES, 2)
        tend, at = place(at, NE)
        ntil, at = place(at, NE)
        cmpj, at = place(at, SLOT_TILES, NE)
        ej, at = place(at, SLOT_TILES)
        rq, at = place(at, 2, TILES * 2)
        oneB, at = place(at, 2 * TILES, SLOT_TILES)
        d_end = at
        oneA, at = place(r4, 2 * TILES, P)
        assert at <= r4 + 2 * 3 * PAIRS * 2 * OW
        wx_gu, at = [None, None], 0
        wx_d = [None, None]
        for k, start in enumerate((r1, r3)):
            wx_gu[k] = arena[:, start:start + KD * 512]
            wx_d[k] = arena[:, start + KD * 512:start + KD * 512 + 2 * D]
        slot_words = r3 - r1
        xg, at = place(r4 + 3200, 2, D)
        xgT, at = place(at, 2, KD, P)
        sg, at = place(at, 2, DE)
        hx, at = place(at, 2, DE)
        hxT, at = place(at, 2, 2, P)
        ysb, at = place(at, 2, D)
        assert at <= c_end
        y1, at = place(r4, 2, D)
        y2, at = place(at, 2, D)
        zb, at = place(at, 2, D)
        ob, at = place(at, 2, D)
        ln2g, at = place(at, D)
        ln2b, at = place(at, D)
        bst2, at = place(at, 2, 2, 6)
        mv2, at = place(at, 2, 2)
        rstd2, at = place(at, 2, 1)
        nmr2, at = place(at, 2, 1)
        gcol, at = place(at, 2, 2)
        assert at <= c_end

        zeros, _ = place(ARENA - 512, 512)
        assert max(d_end, c_end) <= ARENA - 512

        def isb(name, *shape):
            return ctx.enter_context(nc.sbuf_tensor(name, list(shape), I32))

        two_i = isb("two_i", P, TILES, 2)
        rq_i = isb("rq_i", P, 2, TILES * 2)
        idtab = isb("idtab", P, SLOT_TILES + 2)
        ntil_i = isb("ntil_i", P, NE)
        tend_i = isb("tend_i", P, NE)
        ej_i = isb("ej_i", P, 4, SLOT_TILES)
        pairs_i = isb("pairs_i", P, 2)
        idc = isb("idc", P, 2)
        idy = isb("idy", P, 2, 2)

        bank = [ctx.enter_context(nc.psum_tensor(f"bank{b}", [P, 512], FP32)) for b in range(8)]

        names = """c_loaded wv_loaded wk_loaded wa_loaded wb_loaded x_ld0 x_ld1 xt_made xts_ready
            xT_ready v_made v_ready vb_st0 vb_st1 proj_made proj_ready ta_loaded t1_loaded t2_loaded
            v1_loaded v2_loaded qk_made biased exp_done pT_made pT_ready pv_made o_ready
            oA_st o1_st o2_st wo_loaded ws_loaded wr_loaded wo_scaled od_ld0 od_ld1 xr_ld0 xr_ld1
            x1_st0 x1_st1 op_made x1T_made hT_made dn_made lg_made oT_made gu_made
            x1T_ready hT_ready merge_exp squares lg_ready oT_ready gexp_done sinks_ready
            res_done x1_ready base_done merge_need merged om_ready h_ready ln_var rms_var
            ln_rstd rms_rstd lgexp_done cum_need cum_made id_need idm_made table_ready
            we_even we_odd ids_col g_ld0 g_ld1 xgT_made xgT_ready gx_made sg_ready hx_ready hxT_made
            hxT_ready dx_made ya_ready yb_ready y_st0 y_st1 cols_ready ye_ld0 ye_ld1 ln2_loaded
            z_sum z_var z_rstd z_nmr z_norm z_gain fin_ready out_st0 out_st1 zfree msum base_all y_zeroed units_begun gathers_begun
            ones_ready""".split()
        S = {n: ctx.enter_context(nc.semaphore(n)) for n in names}
        block = ctx.enter_context(nc.Block())

        kinds = []
        for half in range(2):
            hp = slice(HD * half, HD * half + HD)
            for s0, L in SEQS:
                for j in range(L // P):
                    k0, k1 = max(0, P * (j - 1)), min(L, P * (j + 2))
                    off = k0 - P * (j - 1)
                    kinds.append((0, half, s0 // P + j, QA[hp, s0 + P * j:s0 + P * j + P],
                                  KA[hp, s0 + k0:s0 + k1], k1 - k0, tA[:, half, off:off + k1 - k0],
                                  [(P, Va[:, (s0 + k0) // P + c, hp]) for c in range((k1 - k0) // P)]))
        for half in range(2):
            hp = slice(HD * half, HD * half + HD)
            for s0, L in SEQS:
                nb = L // P
                for j in range(nb):
                    k0, k1 = max(0, P * j - B_RADIUS), min(L, P * (j + 1) + B_RADIUS)
                    off = k0 - (P * j - B_RADIUS)
                    vt = 0 if s0 == 0 else 5
                    rows = [(64 if m in (0, nb) else P) for m in (j, j + 1)]
                    kinds.append((1, half, s0 // P + j, QB[hp, s0 + P * j:s0 + P * j + P],
                                  KB[hp, s0 + k0:s0 + k1], k1 - k0, t1[:, half, off:off + k1 - k0],
                                  [(r, V1[0:r, vt + m, hp]) for r, m in zip(rows, (j, j + 1))]))
        for half in range(2):
            hp = slice(HD * half, HD * half + HD)
            for s0, L in SEQS:
                qs = QB[hp, s0:s0 + L].rearrange("c (s r) -> c r s", r=4)
                ks = KB[hp, s0:s0 + L].rearrange("c (s r) -> c r s", r=4)
                nb = L // 512
                for r in range(4):
                    for b in range(nb):
                        off = P * (1 - b)
                        kinds.append((2, half, s0 // P + r * nb + b, qs[:, r, P * b:P * b + P],
                                      ks[:, r, :], L // 4, t2[:, half, off:off + L // 4],
                                      [(P, V2[:, s0 // P + r * nb + c, hp]) for c in range(nb)]))
        assert len(kinds) == UNITS

        def proj_plan():
            plan = {}
            for n in range(48):
                plan.setdefault(n * 20 // 48, []).append((n // 8, n % 8))
            for n in range(24):
                plan.setdefault(26 + n * 40 // 24, []).append((6 + n // 8, n % 8))
            return plan

        PLAN = proj_plan()
        GROUP_END = {g: max(s for s, ms in PLAN.items() if any(m[0] == g for m in ms)) for g in range(9)}

        def pslot(n):
            return bank[6 + n % 2]

        @block.sync
        def _(sp):
            x_t = x.rearrange("(t p) d -> t p d", p=P)
            out_t = out.rearrange("(t p) d -> t p d", p=P)
            x1_t = x1_d.rearrange("(t p) d -> t p d", p=P)
            vb_t = vb_d.rearrange("(t p) d -> t p d", p=P)
            od_t = o_d.rearrange("(t p) d -> t p d", p=P)
            w_cols = w_in.rearrange("(k p) c -> p k c", p=P)
            x_ld, vb_st = (S["x_ld0"], S["x_ld1"]), (S["vb_st0"], S["vb_st1"])

            sp.dma_start(xin[:, 0, :], x_t[0]).then_inc(x_ld[0], 16)
            sp.dma_start(cst, const).then_inc(S["c_loaded"], 16)
            sp.dma_start(w_v[:, :, 0:512], w_cols[:, :, VB0:VB0 + 512]).then_inc(S["wv_loaded"], 16)
            sp.dma_start(w_v[:, :, 512:640], w_cols[:, :, VA0:VA0 + P]).then_inc(S["wv_loaded"], 16)
            sp.dma_start(xin[:, 1, :], x_t[1]).then_inc(x_ld[1], 16)
            sp.dma_start(wka, w_cols[:, :, KA0:KA0 + P]).then_inc(S["wk_loaded"], 16)

            def load_wqa(i):
                for half in range(2):
                    sp.dma_start(wqa[:, :, HD * half:HD * half + HD],
                                 w_cols[:, :, bass.ds(QA0 + 256 * half + i * HD, HD)])\
                      .then_inc(S["wa_loaded"], 16)

            def load_wb(i):
                sp.dma_start(wqb, w_cols[:, :, bass.ds(QB0 + i * P, P)]).then_inc(S["wb_loaded"], 16)
                sp.dma_start(wkb, w_cols[:, :, bass.ds(KB0 + i * P, P)]).then_inc(S["wb_loaded"], 16)

            def load_v1(i):
                cs = bass.ds(i * P, P)
                for s0, L, vt in ((0, 512, 0), (512, 1024, 5)):
                    nb = L // P
                    mid = vb_d[s0 + 64:s0 + L - 64, cs].rearrange("(t p) c -> p t c", p=P)
                    sp.dma_start(V1[:, vt + 1:vt + nb, :], mid).then_inc(S["v1_loaded"], 16)
                    sp.dma_start(V1[0:64, vt, :], vb_d[s0:s0 + 64, cs]).then_inc(S["v1_loaded"], 16)
                    sp.dma_start(V1[0:64, vt + nb, :], vb_d[s0 + L - 64:s0 + L, cs])\
                      .then_inc(S["v1_loaded"], 16)

            def load_v2(i):
                cs = bass.ds(i * P, P)
                sp.dma_start(V2[:, 0:4, :], vb_d[0:512, cs].rearrange("(s r) c -> s r c", r=4))\
                  .then_inc(S["v2_loaded"], 16)
                for b in range(2):
                    sp.dma_start(V2[:, 4 + b:12:2, :],
                                 vb_d[512 + 512 * b:1024 + 512 * b, cs].rearrange("(s r) c -> s r c", r=4))\
                      .then_inc(S["v2_loaded"], 16)

            def load_x(t, s):
                sp.wait_ge(S["xt_made"], t - 1)
                sp.dma_start(xin[:, s, :], x_t[t]).then_inc(x_ld[s], 16)

            def store_v(t, s):
                sp.wait_ge(S["v_ready"], t + 1)
                sp.dma_start(vb_t[t], vst[:, s, :]).then_inc(vb_st[s], 16)

            load_wqa(0)
            load_wb(0)
            with sp.Fori(0, TILES // 2 - 1) as i:
                for s in range(2):
                    load_x(2 * i + 2 + s, s)
                    store_v(2 * i + s, s)
            for s in range(2):
                store_v(TILES - 2 + s, s)
            sp.dma_start(tA, tab_a[0]).then_inc(S["ta_loaded"], 16)
            sp.dma_start(t1, tab_1[0]).then_inc(S["t1_loaded"], 16)
            sp.dma_start(t2, tab_2[0]).then_inc(S["t2_loaded"], 16)
            for s in range(2):
                sp.wait_ge(vb_st[s], 16 * (TILES // 2))
            load_v1(0)
            load_v2(0)
            sp.wait_ge(S["xT_ready"], TILES)
            sp.wait_ge(S["v_made"], TILES)
            for c, rows in enumerate((w_out[0:256], w_out[256:512])):
                sp.dma_start(w_o[HD * c:HD * c + HD, 0:4, :], rows.rearrange("(i p) n -> p i n", p=HD))\
                  .then_inc(S["wo_loaded"], 16)
            sp.dma_start(w_o[:, 4:8, :], w_out[512:1024].rearrange("(k p) n -> p k n", p=P))\
              .then_inc(S["wo_loaded"], 16)
            for c in range(2):
                sp.dma_start(gains[HD * c:HD * c + HD, 0:4],
                             norm_a[256 * c:256 * c + 256].rearrange("(i p) -> p i", p=HD),
                             allow_slow_non_contiguous=True).then_inc(S["wo_loaded"], 16)
            sp.dma_start(gains[:, 4:8], norm_b.rearrange("(k p) -> p k", p=P),
                         allow_slow_non_contiguous=True).then_inc(S["wo_loaded"], 16)
            sp.dma_start(ws_gu[:, :, 0:DE], ws_gate.rearrange("(k p) f -> p k f", p=P)).then_inc(S["ws_loaded"], 16)
            sp.dma_start(ws_gu[:, :, DE:2 * DE], ws_up.rearrange("(k p) f -> p k f", p=P)).then_inc(S["ws_loaded"], 16)
            sp.dma_start(ws_d, ws_down.rearrange("(k p) n -> p k n", p=P)).then_inc(S["ws_loaded"], 16)
            sp.dma_start(w_rt, w_router.rearrange("(k p) e -> p k e", p=P)).then_inc(S["wr_loaded"], 16)
            sp.dma_start(ln1g, ln1_g.partition_broadcast(P)).then_inc(S["wr_loaded"], 16)
            sp.dma_start(ln1b, ln1_b.partition_broadcast(P)).then_inc(S["wr_loaded"], 16)
            sp.dma_start(rbias, router_bias.partition_broadcast(P)).then_inc(S["wr_loaded"], 16)
            for c in range(2):
                sp.dma_start(nsink[:, c:8:2], sink[4 * c:4 * c + 4].partition_broadcast(P),
                             allow_slow_non_contiguous=True).then_inc(S["wr_loaded"], 16)

            sp.wait_ge(S["ones_ready"], 1)
            sp.dma_start(y_d[2 * TOKENS:, :].rearrange("(p a) (h d) -> p (a h) d", p=P, d=512),
                         zeros.unsqueeze(1).to_broadcast([P, 2 * (SLOT_TILES - 2 * TILES), 512]))\
              .then_inc(S["y_zeroed"], 16)

            def store_o(kind, i):
                c0 = (2 * PAIRS * kind) * OW
                sem = S[("oA_st", "o1_st", "o2_st")[kind]]
                cs = bass.ds(i * (2 * OW) + c0, 2 * OW)
                flat = ost[kind].rearrange("p t h e -> p t (h e)")
                if kind < 2:
                    sp.dma_start(o_d[:, cs].rearrange("(t p) e -> p t e", p=P), flat).then_inc(sem, 16)
                    return
                sp.dma_start(o_d[0:512, cs].rearrange("(s r) e -> s r e", r=4), flat[:, 0:4, :]).then_inc(sem, 16)
                for b in range(2):
                    sp.dma_start(o_d[512 + 512 * b:1024 + 512 * b, cs].rearrange("(s r) e -> s r e", r=4),
                                 flat[:, 4 + b:12:2, :]).then_inc(sem, 16)

            def pair(i, last):
                if not last:
                    sp.wait_ge(S["proj_made"], 6 + i * 9)
                    load_wqa(i + 1)
                    sp.wait_ge(S["proj_made"], 12 + i * 9)
                    load_wb(i + 1)
                    sp.wait_ge(S["biased"], i * UNITS + 24)
                    sp.dma_start(tA, tab_a[i + 1]).then_inc(S["ta_loaded"], 16)
                sp.wait_ge(S["o_ready"], i * 18 + 6)
                store_o(0, i)
                if not last:
                    sp.wait_ge(S["biased"], i * UNITS + 48)
                    sp.dma_start(t1, tab_1[i + 1]).then_inc(S["t1_loaded"], 16)
                sp.wait_ge(S["o_ready"], i * 18 + 12)
                store_o(1, i)
                if not last:
                    load_v1(i + 1)
                    sp.wait_ge(S["biased"], i * UNITS + 72)
                    sp.dma_start(t2, tab_2[i + 1]).then_inc(S["t2_loaded"], 16)
                sp.wait_ge(S["o_ready"], i * 18 + 18)
                store_o(2, i)
                if not last:
                    load_v2(i + 1)

            with sp.Fori(0, PAIRS - 1) as i:
                pair(i, False)
            pair(PAIRS - 1, True)

            sp.wait_ge(S["oA_st"], 16 * PAIRS)
            sp.wait_ge(S["o1_st"], 16 * PAIRS)
            sp.wait_ge(S["o2_st"], 48 * PAIRS)
            od_ld, xr_ld, x1_st = (S["od_ld0"], S["od_ld1"]), (S["xr_ld0"], S["xr_ld1"]), (S["x1_st0"], S["x1_st1"])
            sp.dma_start(odt[:, 0, :], od_t[0]).then_inc(od_ld[0], 16)
            sp.dma_start(odt[:, 1, :], od_t[1]).then_inc(od_ld[1], 16)
            sp.dma_start(xr[:, 0, :], x_t[0]).then_inc(xr_ld[0], 16)

            def c_step(t, s, od=True, xl=True):
                if od:
                    sp.wait_ge(S["merged"], t + 1)
                    sp.dma_start(odt[:, s, :], od_t[t + 2]).then_inc(od_ld[s], 16)
                if xl:
                    sp.wait_ge(S["res_done"], t)
                    sp.dma_start(xr[:, 1 - s, :], x_t[t + 1]).then_inc(xr_ld[1 - s], 16)
                sp.wait_ge(S["x1_ready"], t + 1)
                sp.dma_start(x1_t[t], x1s[:, s, :]).then_inc(x1_st[s], 16)

            with sp.Fori(0, TILES // 2 - 1) as i:
                for s in range(2):
                    c_step(2 * i + s, s)
            c_step(TILES - 2, 0, od=False)
            c_step(TILES - 1, 1, od=False, xl=False)

            def load_expert(e, k):
                sem = S["we_odd"] if k else S["we_even"]
                gu = wx_gu[k].rearrange("p (k f) -> p k f", f=2 * DE)
                sp.dma_start(gu[:, :, 0:DE], w_gate[e].rearrange("(k p) f -> p k f", p=P)).then_inc(sem, 16)
                sp.dma_start(gu[:, :, DE:2 * DE], w_up[e].rearrange("(k p) f -> p k f", p=P)).then_inc(sem, 16)
                sp.dma_start(wx_d[k].rearrange("p (k n) -> p k n", n=D),
                             w_down[e].rearrange("(k p) n -> p k n", p=P)).then_inc(sem, 16)

            sp.wait_ge(S["op_made"], TILES)
            load_expert(0, 0)
            sp.wait_ge(S["dn_made"], TILES)
            load_expert(1, 1)
            sp.wait_ge(S["table_ready"], 1)
            with sp.Fori(0, NE // 2 - 1) as i:
                for k in range(2):
                    done = sp.value_load(tend_i[0:1, bass.ds(2 * i + k, 1)], min_val=0, max_val=SLOT_TILES)
                    sp.wait_ge(S["dx_made"], done)
                    load_expert(2 * i + k + 2, k)

            sp.wait_ge(S["base_all"], 1)
            sp.dma_start(ln2g, ln2_g.partition_broadcast(P)).then_inc(S["ln2_loaded"], 16)
            sp.dma_start(ln2b, ln2_b.partition_broadcast(P)).then_inc(S["ln2_loaded"], 16)
            out_st = (S["out_st0"], S["out_st1"])
            with sp.Fori(0, TILES // 2) as i:
                for s in range(2):
                    sp.wait_ge(S["fin_ready"], 2 * i + s + 1)
                    sp.dma_start(out_t[2 * i + s], ob[:, s, :]).then_inc(out_st[s], 16)
            for s in range(2):
                sp.wait_ge(out_st[s], 16 * (TILES // 2))

        @block.tensor
        def _(pe):
            def transposes(src, banks, sem):
                for c in range(KD):
                    last = nc.tensor.transpose(banks[c // 4][:, P * (c % 4):P * (c % 4) + P],
                                               src[:, P * c:P * c + P], ident)
                last.then_inc(sem, 1)

            x_ld = (S["x_ld0"], S["x_ld1"])
            pe.wait_ge(S["c_loaded"], 16)

            def xt(t, s, n):
                pe.wait_ge(x_ld[s], 16 * n)
                transposes(xin[:, s, :], bank[2 * s:2 * s + 2], S["xt_made"])

            def vproj(t, s):
                pe.wait_ge(S["xts_ready"], t + 1)
                for k in range(KD):
                    nc.tensor.matmul(bank[4 + s][:], xts[:, s, k, :], w_v[:, k, 0:512],
                                     start=k == 0, stop=k == KD - 1)
                for k in range(KD):
                    last = nc.tensor.matmul(bank[6 + s][:, 0:P], xts[:, s, k, :], w_v[:, k, 512:640],
                                            start=k == 0, stop=k == KD - 1)
                last.then_inc(S["v_made"], 1)

            xt(0, 0, 1)
            pe.wait_ge(S["wv_loaded"], 32)
            with pe.Fori(0, TILES // 2 - 1) as i:
                xt(2 * i + 1, 1, i + 1)
                vproj(2 * i, 0)
                xt(2 * i + 2, 0, i + 2)
                vproj(2 * i + 1, 1)
            xt(TILES - 1, 1, TILES // 2)
            vproj(TILES - 2, 0)
            vproj(TILES - 1, 1)

            def proj(w, g, k, n, sem=None):
                last = nc.tensor.matmul(pslot(n)[:], w[:, k, :], xT[:, k, 512 * g:512 * g + 512],
                                        start=k == 0, stop=k == KD - 1)
                if k == KD - 1:
                    last.then_inc(S["proj_made"], 1)

            pe.wait_ge(S["xT_ready"], TILES)
            pe.wait_ge(S["v_ready"], TILES)
            pe.wait_ge(S["wk_loaded"], 16)
            pe.wait_ge(S["wa_loaded"], 32)
            for n in range(6):
                if n >= 2:
                    pe.wait_ge(S["proj_ready"], n - 1)
                for k in range(KD):
                    proj(wka if n < 3 else wqa, n % 3, k, n)

            def qk(u, i):
                kind, half, tile, q, k, n, tab, v = kinds[u]
                if u == 0:
                    pe.wait_ge(S["proj_ready"], 6 + i * 9)
                if u == 24:
                    pe.wait_ge(S["proj_ready"], 12 + i * 9)
                nc.tensor.matmul(bank[u % 2][:, 0:n], q, k, start=True, stop=True).then_inc(S["qk_made"], 1)

            def pT(u, i):
                kind, half, tile, q, k, n, tab, v = kinds[u]
                pe.wait_ge(S["exp_done"], i * UNITS + u + 1)
                at = [sum(r for r, _ in v[:c]) for c in range(len(v))]
                for c in sorted(range(len(v)), key=lambda c: -v[c][0]):
                    r = v[c][0]
                    last = nc.tensor.transpose(bank[2 + u % 2][0:r, P * c:P * c + P],
                                               prob[:, u % 2, at[c]:at[c] + r], ident)
                last.then_inc(S["pT_made"], 1)

            def pv(u, i):
                kind, half, tile, q, k, n, tab, v = kinds[u]
                if u == 24:
                    pe.wait_ge(S["v1_loaded"], (i + 1) * 96)
                if u == 48:
                    pe.wait_ge(S["v2_loaded"], (i + 1) * 48)
                pe.wait_ge(S["pT_ready"], i * UNITS + u + 1)
                o = bank[4 + (u // 4) % 2][:, HD * (u % 4):HD * (u % 4) + HD]
                for c, (r, rows) in enumerate(v):
                    last = nc.tensor.matmul(o, probT[0:r, u % 2, P * c:P * c + P], rows,
                                            start=c == 0, stop=c == len(v) - 1)
                if u % 4 == 3:
                    last.then_inc(S["pv_made"], 1)

            def pair(i, last):
                for g in range(UNITS):
                    if g + 2 < UNITS:
                        qk(g + 2, i)
                    elif not last:
                        qk(g + 2 - UNITS, i + 1)
                    todo = [m for m in PLAN.get(g, []) if m[0] < 6 or not last]
                    for j, (n, k) in enumerate(todo):
                        if k == 0:
                            pe.wait_ge(S["proj_ready"], i * 9 + (6 if n == 0 else 5 + n))
                            if n == 0:
                                pe.wait_ge(S["wb_loaded"], (i + 1) * 32)
                            if n == 6:
                                pe.wait_ge(S["wa_loaded"], (i + 2) * 32)
                        proj((wqb, wkb, wqa)[n // 3], n % 3, k, n)
                    if g + 1 < UNITS:
                        pT(g + 1, i)
                    elif not last:
                        pT(0, i + 1)
                    pv(g, i)

            qk(0, 0)
            qk(1, 0)
            pT(0, 0)
            with pe.Fori(0, PAIRS - 1) as i:
                pair(i, False)
            pair(PAIRS - 1, True)

            pe.wait_ge(S["o_ready"], 18 * PAIRS)
            pe.wait_ge(S["wo_scaled"], 1)
            pe.wait_ge(S["ws_loaded"], 48)
            pe.wait_ge(S["wr_loaded"], 96)

            def op(t, s):
                pe.wait_ge(S["oT_ready"], t + 1)
                pe.wait_ge(S["res_done"], t)
                for k in range(KD):
                    for c in range(2):
                        last = nc.tensor.matmul(bank[c][:], oTs[:, s, k, :], w_o[:, k, 512 * c:512 * c + 512],
                                                start=k == 0, stop=k == KD - 1)
                last.then_inc(S["op_made"], 1)

            def x1t(t, s):
                pe.wait_ge(S["x1_ready"], t + 1)
                transposes(x1s[:, s, :], bank[2:4], S["x1T_made"])

            def ht(t, s):
                pe.wait_ge(S["h_ready"], t + 1)
                for c in range(2):
                    last = nc.tensor.transpose(bank[5][:, P * c:P * c + P], hid[:, s, P * c:P * c + P], ident)
                last.then_inc(S["hT_made"], 1)

            def dn(t, s):
                pe.wait_ge(S["hT_ready"], t + 1)
                pe.wait_ge(S["base_done"], t)
                for k in range(2):
                    for c in range(2):
                        last = nc.tensor.matmul(bank[6 + c][:], hTs[:, s, k, :], ws_d[:, k, 512 * c:512 * c + 512],
                                                start=k == 0, stop=k == 1)
                last.then_inc(S["dn_made"], 1)

            def rt(t, s):
                pe.wait_ge(S["x1T_ready"], t + 1)
                for k in range(KD):
                    last = nc.tensor.matmul(bank[5][:, 256:256 + NE], x1T[:, s, k, :], w_rt[:, k, :],
                                            start=k == 0, stop=k == KD - 1)
                last.then_inc(S["lg_made"], 1)

            def ot(t, s):
                pe.wait_ge(S["om_ready"], t + 1)
                transposes(om[:, s, :], bank[2:4], S["oT_made"])

            def gu(t, s):
                pe.wait_ge(S["lg_ready"], t + 1) 
                for k in range(KD):
                    last = nc.tensor.matmul(bank[4][:], x1T[:, s, k, :], ws_gu[:, k, :],
                                            start=k == 0, stop=k == KD - 1)
                last.then_inc(S["gu_made"], 1)

            def c_step(t, s, ok):
                if ok(0):
                    op(t, s)
                if ok(-1):
                    x1t(t - 1, 1 - s)
                if ok(-2):
                    ht(t - 2, s)
                    dn(t - 2, s)
                if ok(-1):
                    rt(t - 1, 1 - s)
                if ok(1):
                    ot(t + 1, 1 - s)
                if ok(-1):
                    gu(t - 1, 1 - s)

            for t in range(-1, 2):
                c_step(t, t % 2, lambda d, t=t: 0 <= t + d < TILES)
            with pe.Fori(0, TILES // 2 - 2) as i:
                for s in range(2):
                    c_step(2 * i + 2 + s, s, lambda d: True)
            for t in range(TILES - 2, TILES + 1):
                c_step(t, t % 2, lambda d, t=t: 0 <= t + d < TILES)

            pe.wait_ge(S["cum_need"], 1)
            cum = bank[0]
            nc.tensor.matmul(cum[:, 0:(TILES + 1) * NE], tri, msk.rearrange("p t e -> p (t e)"),
                             start=True, stop=False)
            for t in range(TILES):
                rest = TILES - t
                last = nc.tensor.matmul(cum[:, (t + 1) * NE:(TILES + 1) * NE], ones,
                                        msk[:, t:t + 1, :].to_broadcast([P, rest, NE]),
                                        start=False, stop=t == TILES - 1)
            last.then_inc(S["cum_made"], 1)
            ht(TILES - 1, 1)
            dn(TILES - 1, 1)
            pe.wait_ge(S["id_need"], 1)
            for c in range(2 * TILES):
                last = nc.tensor.matmul(bank[1][:, 0:SLOT_TILES], oneA[:, c, :], oneB[:, c, :],
                                        start=c == 0, stop=c == 2 * TILES - 1)
            last.then_inc(S["idm_made"], 1)

            pe.wait_ge(S["table_ready"], 1)
            more = pe.value_load(pairs_i[0:1, 0:1], min_val=0, max_val=SLOT_TILES // 2 - 1)
            g_ld = (S["g_ld0"], S["g_ld1"])

            def dxt(j, s, n):
                pe.wait_ge(g_ld[s], n)
                transposes(xg[:, s, :], bank[3:5], S["xgT_made"])

            def dgu(j, s):
                k_slot = pe.value_load(ej_i[0:1, 0, bass.ds(j, 1)], min_val=0, max_val=1)
                even = pe.value_load(ej_i[0:1, 1, bass.ds(j, 1)], min_val=0, max_val=48 * NE)
                odd = pe.value_load(ej_i[0:1, 2, bass.ds(j, 1)], min_val=0, max_val=48 * NE)
                pe.wait_ge(S["we_even"], even)
                pe.wait_ge(S["we_odd"], odd)
                pe.wait_ge(S["xgT_ready"], j + 1)
                for k in range(KD):
                    last = nc.tensor.matmul(bank[s][:], xgT[:, s, k, :],
                                            arena[:, bass.ds(k_slot * slot_words + (r1 + k * 2 * DE), 2 * DE)],
                                            start=k == 0, stop=k == KD - 1)
                last.then_inc(S["gx_made"], 1)

            def dht(j, s):
                pe.wait_ge(S["hx_ready"], j + 1)
                for c in range(2):
                    last = nc.tensor.transpose(bank[2][:, P * c:P * c + P], hx[:, s, P * c:P * c + P], ident)
                last.then_inc(S["hxT_made"], 1)

            def ddn(j, s):
                k_slot = pe.value_load(ej_i[0:1, 0, bass.ds(j, 1)], min_val=0, max_val=1)
                pe.wait_ge(S["hxT_ready"], j + 1)
                pe.wait_ge(S["ya_ready"], j)
                pe.wait_ge(S["yb_ready"], j)
                for k in range(2):
                    for c in range(2):
                        w0 = r1 + KD * 2 * DE + k * D + 512 * c
                        last = nc.tensor.matmul(bank[5 + c][:], hxT[:, s, k, :],
                                                arena[:, bass.ds(k_slot * slot_words + w0, 512)],
                                                start=k == 0, stop=k == 1)
                last.then_inc(S["dx_made"], 1)

            dxt(0, 0, 16)
            dgu(0, 0)
            dxt(1, 1, 16)
            with pe.Fori(0, more) as i:
                for s, j in ((1, 2 * i + 1), (0, 2 * i + 2)):
                    dgu(j, s)
                    dht(j - 1, 1 - s)
                    dxt(j + 1, 1 - s, i * 16 + 32)
                    ddn(j - 1, 1 - s)
            end = more * 2 + 1
            dgu(end, 1)
            dht(end - 1, 0)
            ddn(end - 1, 0)
            dht(end, 1)
            ddn(end, 1)

        @block.scalar
        def _(act):
            def copy(o, i):
                return nc.scalar.activation(o, i, ACT.Copy)

            def two_banks(dst, banks, sem):
                copy(dst[:, 0:4, :], banks[0][:].rearrange("p (k c) -> p k c", c=P))
                copy(dst[:, 4:8, :], banks[1][:].rearrange("p (k c) -> p k c", c=P)).then_inc(sem, 1)

            vb_st = (S["vb_st0"], S["vb_st1"])

            def xt(t, s, first=False):
                act.wait_ge(S["xt_made"], t + 1)
                if not first:
                    act.wait_ge(S["xT_ready"], t - 1)
                two_banks(xts[:, s], bank[2 * s:2 * s + 2], S["xts_ready"])

            def vproj(t, s, n):
                act.wait_ge(S["v_made"], t + 1)
                act.wait_ge(vb_st[s], n * 16)
                copy(vst[:, s, :], bank[4 + s][:])
                copy(Va[:, t, :], bank[6 + s][:, 0:P]).then_inc(S["v_ready"], 1)

            xt(0, 0, True)
            with act.Fori(0, TILES // 2 - 1) as i:
                xt(2 * i + 1, 1)
                vproj(2 * i, 0, i)
                xt(2 * i + 2, 0)
                vproj(2 * i + 1, 1, i)
            xt(TILES - 1, 1)
            vproj(TILES - 2, 0, TILES // 2 - 1)
            vproj(TILES - 1, 1, TILES // 2 - 1)

            def proj(dst, g, n, count):
                act.wait_ge(S["proj_made"], count)
                copy(dst[:, 512 * g:512 * g + 512], pslot(n)[:]).then_inc(S["proj_ready"], 1)

            for n in range(6):
                proj(KA if n < 3 else QA, n % 3, n, n + 1)

            def exps(u, i):
                kind, half, tile, q, k, n, tab, v = kinds[u]
                act.wait_ge(S["biased"], i * UNITS + u + 1)
                nc.scalar.activation(prob[:, u % 2, 0:n], prob[:, u % 2, 0:n], ACT.Exp, scale=-1.0,
                                     bias=ost[kind][:, tile, half, HD:HD + 1],
                                     accum_out=ost[kind][:, tile, half, HD + 1:HD + 2])\
                  .then_inc(S["exp_done"], 1)

            def results(q, i):
                kind, half, tile = kinds[4 * q][0:3]
                act.wait_ge(S["pv_made"], i * 18 + q + 1)
                copy(ost[kind][:, tile:tile + 4, half, 0:HD],
                     bank[4 + q % 2][:, 0:4 * HD].rearrange("p (t e) -> p t e", e=HD)).then_inc(S["o_ready"], 1)

            def pair(i, last):
                for g in range(UNITS):
                    for n in range(9):
                        if GROUP_END[n] == g - 1 and (n < 6 or not last):
                            proj((QB, KB, QA)[n // 3], n % 3, n, i * 9 + n + 7)
                    if g + 2 < UNITS:
                        exps(g + 2, i)
                    elif not last:
                        exps(g + 2 - UNITS, i + 1)
                    if g % 4 == 3:
                        results(g // 4, i)

            exps(0, 0)
            exps(1, 0)
            with act.Fori(0, PAIRS - 1) as i:
                pair(i, False)
            pair(PAIRS - 1, True)

            def c_step(t, s, ok):
                if ok(-1):
                    act.wait_ge(S["x1T_made"], t)
                    two_banks(x1T[:, 1 - s], bank[2:4], S["x1T_ready"])
                if ok(-2):
                    act.wait_ge(S["hT_made"], t - 1)
                    copy(hTs[:, s], bank[5][:, 0:256].rearrange("p (k c) -> p k c", c=P)).then_inc(S["hT_ready"], 1)
                if ok(2):
                    act.wait_ge(S["merge_need"], t + 3)
                    nc.scalar.activation(mD, mD, ACT.Exp).then_inc(S["merge_exp"], 1)
                if ok(-1):
                    act.wait_ge(S["lg_made"], t)
                    copy(logits[:, t - 1, :], bank[5][:, 256:256 + NE]).then_inc(S["lg_ready"], 1)
                if ok(1):
                    act.wait_ge(S["oT_made"], t + 2)
                    two_banks(oTs[:, 1 - s], bank[2:4], S["oT_ready"])
                if ok(2):
                    act.wait_ge(S["merged"], t + 3)
                    for h in range(2):
                        last = nc.scalar.activation(junk, om[:, s, 512 * h:512 * h + 512], ACT.Square,
                                                    accum_out=ssq[:, s, h:h + 1])
                        if h == 0:
                            act.drain()
                    last.then_inc(S["squares"], 1)
                if ok(-1):
                    act.wait_ge(S["gu_made"], t)
                    nc.scalar.activation(eg[:, 1 - s, :], bank[4][:, 0:DE], ACT.Exp, scale=-1.0)\
                      .then_inc(S["gexp_done"], 1)

            for t in range(-2, 2):
                c_step(t, t % 2, lambda d, t=t: 0 <= t + d < TILES)
            with act.Fori(0, TILES // 2 - 2) as i:
                for s in range(2):
                    c_step(2 * i + 2 + s, s, lambda d: True)
            for t in range(TILES - 2, TILES):
                c_step(t, t % 2, lambda d, t=t: 0 <= t + d < TILES)
            act.wait_ge(S["x1T_made"], TILES)
            two_banks(x1T[:, 1], bank[2:4], S["x1T_ready"])
            act.wait_ge(S["hT_made"], TILES - 1)
            copy(hTs[:, 0], bank[5][:, 0:256].rearrange("p (k c) -> p k c", c=P)).then_inc(S["hT_ready"], 1)
            act.wait_ge(S["lg_made"], TILES)
            copy(logits[:, TILES - 1, :], bank[5][:, 256:256 + NE]).then_inc(S["lg_ready"], 1)
            act.wait_ge(S["lg_ready"], TILES)
            nc.scalar.activation(score.rearrange("p t e -> p (t e)"), logits.rearrange("p t e -> p (t e)"),
                                 ACT.Exp, scale=-1.0).then_inc(S["lgexp_done"], 1)
            act.wait_ge(S["gu_made"], TILES)
            nc.scalar.activation(eg[:, 1, :], bank[4][:, 0:DE], ACT.Exp, scale=-1.0).then_inc(S["gexp_done"], 1)
            act.wait_ge(S["hT_made"], TILES)
            copy(hTs[:, 1], bank[5][:, 0:256].rearrange("p (k c) -> p k c", c=P)).then_inc(S["hT_ready"], 1)

            act.wait_ge(S["table_ready"], 1)
            more = act.value_load(pairs_i[0:1, 0:1], min_val=0, max_val=SLOT_TILES // 2 - 1)
            y_st = (S["y_st0"], S["y_st1"])
            y_t = y_d.rearrange("(t p) d -> t p d", p=P)
            act.wait_ge(S["base_done"], TILES)
            act.wait_ge(S["y_zeroed"], 16)

            def dxt(j, s):
                act.wait_ge(S["xgT_made"], j + 1)
                two_banks(xgT[:, s], bank[3:5], S["xgT_ready"])

            def dsilu(j, s):
                act.wait_ge(S["gx_made"], j + 1)
                nc.scalar.activation(sg[:, s, :], bank[s][:, 0:DE], ACT.Silu).then_inc(S["sg_ready"], 1)

            def dht(j, s):
                act.wait_ge(S["hxT_made"], j + 1)
                copy(hxT[:, s], bank[2][:, 0:256].rearrange("p (k c) -> p k c", c=P)).then_inc(S["hxT_ready"], 1)

            def dy(j, s, n):
                act.wait_ge(S["dx_made"], j + 1)
                act.wait_ge(y_st[s], n)
                copy(ysb[:, s, 0:512], bank[5][:]).then_inc(S["ya_ready"], 1)
                act.wait_ge(S["ya_ready"], j + 1)
                act.wait_ge(S["yb_ready"], j + 1)
                act.dma_start(y_t[j], ysb[:, s, :]).then_inc(y_st[s], 16)

            dxt(0, 0)
            dsilu(0, 0)
            dxt(1, 1)
            with act.Fori(0, more) as i:
                for s, j in ((1, 2 * i + 1), (0, 2 * i + 2)):
                    dsilu(j, s)
                    dht(j - 1, 1 - s)
                    dxt(j + 1, 1 - s)
                    dy(j - 1, 1 - s, i * 16)
            end = more * 2 + 1
            dsilu(end, 1)
            dht(end - 1, 0)
            dy(end - 1, 0, more * 16)
            dht(end, 1)
            dy(end, 1, more * 16)

            with act.Fori(0, TILES // 2) as i:
                for s in range(2):
                    t = 2 * i + s
                    act.wait_ge(S["z_nmr"], t + 1)
                    nc.scalar.activation(zb[:, s, :], zb[:, s, :], ACT.Identity, bias=nmr2[:, s, :],
                                         scale=rstd2[:, s, :]).then_inc(S["z_norm"], 1)

        @block.vector
        def _(dve):
            V = nc.vector

            V.memset(zeros, 0.0)
            V.memset(ones, 1.0)
            V.memset(minus_half, -0.5).then_inc(S["ones_ready"], 1)

            def bias(u, i):
                kind, half, tile, q, k, n, tab, v = kinds[u]
                if u % 24 == 0:
                    dve.wait_ge(S[("ta_loaded", "t1_loaded", "t2_loaded")[kind]], i * 16 + 16)
                    dve.wait_ge(S[("oA_st", "o1_st", "o2_st")[kind]], i * (16, 16, 48)[kind])
                dve.wait_ge(S["qk_made"], i * UNITS + u + 1)
                dve.sem_inc(S["units_begun"], 1)
                V.tensor_tensor_reduce(out=prob[:, u % 2, 0:n], in0=bank[u % 2][:, 0:n], in1=tab,
                                       scale=-(HD ** -0.5), scalar=BIG, op0=ALU.add, op1=ALU.min,
                                       accum_out=ost[kind][:, tile, half, HD:HD + 1]).then_inc(S["biased"], 1)

            def pT(u, i):
                kind, half, tile, q, k, n, tab, v = kinds[u]
                dve.wait_ge(S["pT_made"], i * UNITS + u + 1)
                if all(r == P for r, _ in v):
                    last = V.tensor_copy(probT[:, u % 2, 0:n], bank[2 + u % 2][:, 0:n])
                else:
                    for c, (r, _) in enumerate(v):
                        last = V.tensor_copy(probT[0:r, u % 2, P * c:P * c + P],
                                             bank[2 + u % 2][0:r, P * c:P * c + P])
                last.then_inc(S["pT_ready"], 1)

            def pair(i, last):
                for g in range(UNITS):
                    if g + 2 < UNITS:
                        bias(g + 2, i)
                    elif not last:
                        bias(g + 2 - UNITS, i + 1)
                    if g + 1 < UNITS:
                        pT(g + 1, i)
                    elif not last:
                        pT(0, i + 1)

            bias(0, 0)
            bias(1, 0)
            pT(0, 0)
            with dve.Fori(0, PAIRS - 1) as i:
                pair(i, False)
            pair(PAIRS - 1, True)

            dve.wait_ge(S["wr_loaded"], 96)
            dve.wait_ge(S["o_ready"], 18 * PAIRS)
            V.tensor_scalar(nsink, nsink, -1.0, None, ALU.mult)
            dve.drain()
            od_ld, xr_ld, x1_st = (S["od_ld0"], S["od_ld1"]), (S["xr_ld0"], S["xr_ld1"]), (S["x1_st0"], S["x1_st1"])

            def residual(t, s, n):
                dve.wait_ge(S["op_made"], t + 1)
                dve.wait_ge(xr_ld[s], n)
                for c in range(2):
                    last = V.scalar_tensor_tensor(res[:, 512 * c:512 * c + 512], xr[:, s, 512 * c:512 * c + 512],
                                                  ALPHA, bank[c][:], ALU.mult, ALU.add)
                last.then_inc(S["res_done"], 1)

            def shared(t, s):
                dve.wait_ge(S["dn_made"], t + 1)
                for c in range(2):
                    last = V.scalar_tensor_tensor(base[:, t, 512 * c:512 * c + 512],
                                                  x1s[:, s, 512 * c:512 * c + 512],
                                                  ALPHA, bank[6 + c][:], ALU.mult, ALU.add)
                last.then_inc(S["base_done"], 1)

            def ln1(t, s, n):
                dve.drain()
                for c in range(2):
                    V.bn_stats(bst[:, c, :], res[:, 512 * c:512 * c + 512])
                dve.drain()
                V.bn_aggr(mv[:, s, :], bst.rearrange("p a b -> p (a b)"))
                dve.drain()
                V.tensor_scalar(rstd[:, s, :], mv[:, s, 1:2], LN_EPS, None, ALU.add).then_inc(S["ln_var"], 1)
                dve.wait_ge(S["ln_rstd"], t + 1)
                V.tensor_scalar(res, res, mv[:, s, 0:1], rstd[:, s, :], ALU.subtract, ALU.mult)
                dve.drain()
                V.tensor_tensor(res, res, ln1g, ALU.mult)
                dve.drain()
                dve.wait_ge(x1_st[s], n)
                V.tensor_tensor(x1s[:, s, :], res, ln1b, ALU.add).then_inc(S["x1_ready"], 1)

            def merge(t, s, n):
                dve.wait_ge(od_ld[s], n)
                heads = odt[:, s, :].rearrange("p (k h e) -> p k h e", k=3, e=OW)
                nm, ls = heads[:, :, :, HD], heads[:, :, :, HD + 1]
                V.tensor_tensor(mM[:, 0, :], nm[:, 0, :], nsink, ALU.min)
                V.tensor_tensor(mM[:, 1, :], nm[:, 1, :], nm[:, 2, :], ALU.min)
                dve.drain()
                V.tensor_tensor(mD[:, 0:2, :], mM, nm[:, 0:2, :], ALU.subtract)
                V.tensor_tensor(mD[:, 2, :], mM[:, 1, :], nm[:, 2, :], ALU.subtract)
                V.tensor_tensor(mD[:, 3, :], mM[:, 0, :], nsink, ALU.subtract).then_inc(S["merge_need"], 1)
                dve.wait_ge(S["merge_exp"], t + 1)
                V.tensor_tensor(mL, mD[:, 0:3, :], ls, ALU.mult)
                dve.drain()
                V.tensor_tensor(mR[:, 0, :], mL[:, 0, :], mD[:, 3, :], ALU.add)
                V.tensor_tensor(mR[:, 1, :], mL[:, 1, :], mL[:, 2, :], ALU.add)
                dve.drain()
                V.reciprocal(mR, mR)
                dve.drain()
                V.tensor_tensor(mW[:, 0:2, :], mD[:, 0:2, :], mR, ALU.mult)
                V.tensor_tensor(mW[:, 2, :], mD[:, 2, :], mR[:, 1, :], ALU.mult)
                dve.drain()
                o2 = junk2.rearrange("p (h e) -> p h e", e=HD)
                V.tensor_tensor(om[:, s, 0:512].rearrange("p (h e) -> p h e", e=HD), heads[:, 0, :, 0:HD],
                                mW[:, 0, :].unsqueeze(2).to_broadcast([P, 8, HD]), ALU.mult)
                V.tensor_tensor(om[:, s, 512:1024].rearrange("p (h e) -> p h e", e=HD), heads[:, 1, :, 0:HD],
                                mW[:, 1, :].unsqueeze(2).to_broadcast([P, 8, HD]), ALU.mult)
                V.tensor_tensor(o2, heads[:, 2, :, 0:HD],
                                mW[:, 2, :].unsqueeze(2).to_broadcast([P, 8, HD]), ALU.mult)
                dve.drain()
                V.tensor_tensor(om[:, s, 512:1024], om[:, s, 512:1024], junk2, ALU.add).then_inc(S["merged"], 1)
                dve.wait_ge(S["squares"], t + 1)
                V.tensor_scalar(rms[:, s, :], ssq[:, s, :], 1.0 / 512, RMS_EPS, ALU.mult, ALU.add)\
                 .then_inc(S["rms_var"], 1)
                dve.wait_ge(S["rms_rstd"], t + 1)
                for h in range(2):
                    last = V.tensor_scalar(om[:, s, 512 * h:512 * h + 512], om[:, s, 512 * h:512 * h + 512],
                                           rms[:, s, h:h + 1], None, ALU.mult)
                last.then_inc(S["om_ready"], 1)

            def hidden(t, s):
                dve.wait_ge(S["gexp_done"], t + 1)
                V.tensor_scalar(eg[:, s, :], eg[:, s, :], 1.0, None, ALU.add)
                dve.drain()
                V.reciprocal(eg[:, s, :], eg[:, s, :])
                dve.drain()
                V.tensor_tensor(eg[:, s, :], eg[:, s, :], bank[4][:, 0:DE], ALU.mult)
                dve.drain()
                V.tensor_tensor(hid[:, s, :], eg[:, s, :], bank[4][:, DE:2 * DE], ALU.mult).then_inc(S["h_ready"], 1)

            def c_step(t, s, m, ok):
                if ok(0):
                    residual(t, s, m * 16 + 16)
                if ok(-2):
                    shared(t - 2, s)
                if ok(0):
                    ln1(t, s, m * 16)
                if ok(2):
                    merge(t + 2, s, m * 16 + 32)
                if ok(-1):
                    hidden(t - 1, 1 - s)

            for t in range(-2, 2):
                c_step(t, t % 2, t // 2, lambda d, t=t: 0 <= t + d < TILES)
            with dve.Fori(0, TILES // 2 - 2) as i:
                for s in range(2):
                    c_step(2 * i + 2 + s, s, i + 1, lambda d: True)
            for t in range(TILES - 2, TILES):
                c_step(t, t % 2, t // 2, lambda d, t=t: 0 <= t + d < TILES)
            shared(TILES - 2, 0)

            def ranks(val, tmp, rk, start):
                n = val.shape[1] * val.shape[2] // 4
                v4, c4, r4_ = (a.rearrange("p t e -> p (t e)").rearrange("p (n f) -> p n f", f=4)
                               for a in (val, tmp, rk))
                V.tensor_copy(r4_, start.unsqueeze(1).to_broadcast([P, n, 4]))
                for d in range(1, 4):
                    dve.drain()
                    V.tensor_tensor(c4[:, :, 0:4 - d], v4[:, :, 0:4 - d], v4[:, :, d:4], ALU.is_ge)
                    dve.drain()
                    V.tensor_tensor(r4_[:, :, d:4], r4_[:, :, d:4], c4[:, :, 0:4 - d], ALU.add)
                    dve.drain()
                    V.tensor_tensor(r4_[:, :, 0:4 - d], r4_[:, :, 0:4 - d], c4[:, :, 0:4 - d], ALU.subtract)
                dve.drain()

            def flat(a):
                return a.rearrange("p t e -> p (t e)")

            V.memset(msk[:, TILES, :], 0.0)
            dve.wait_ge(S["lgexp_done"], 1)
            V.tensor_scalar(flat(score), flat(score), 1.0, None, ALU.add)
            dve.drain()
            V.reciprocal(flat(score), flat(score))
            dve.drain()
            V.tensor_tensor(bia, score, rbias.unsqueeze(1).to_broadcast([P, TILES, NE]), ALU.add)
            dve.drain()
            ranks(bia, cmp_, rank, rank0)
            V.tensor_scalar(flat(rank), flat(rank), 1.5, None, ALU.is_lt)
            dve.drain()
            V.tensor_tensor(flat(cmp_), flat(rank), flat(bia), ALU.mult)
            dve.drain()
            V.tensor_reduce(flat(gsc), flat(cmp_).rearrange("p (n f) -> p n f", f=4), AX.X, ALU.add)
            dve.drain()
            ranks(gsc, gcmp, grank, rank0)
            V.scalar_tensor_tensor(flat(msk[:, 0:TILES, :]).rearrange("p (n f) -> p n f", f=4),
                                   flat(grank).unsqueeze(2).to_broadcast([P, TILES * NGRP, 4]), 0.5,
                                   flat(rank).rearrange("p (n f) -> p n f", f=4),
                                   ALU.is_lt, ALU.mult).then_inc(S["cum_need"], 1)
            hidden(TILES - 1, 1)
            dve.drain()
            V.tensor_tensor(flat(msc), flat(msk[:, 0:TILES, :]), flat(score), ALU.mult)
            dve.drain()
            V.tensor_reduce(den, msc, AX.X, ALU.add)
            dve.drain()
            V.reciprocal(den, den)
            dve.wait_ge(S["cum_made"], 1)
            V.tensor_scalar(ntil_i[:], bank[0][:, TILES * NE:(TILES + 1) * NE], float(P - 1), None, ALU.add)
            dve.drain()
            V.tensor_scalar(ntil_i[:], ntil_i[:], 7, None, ALU.arith_shift_right)
            dve.drain()
            V.tensor_copy(ntil, ntil_i[:])
            dve.drain()
            V.tensor_tensor_scan(tend, ones[:, 0:NE], ntil, 0.0, ALU.mult, ALU.add)
            dve.drain()
            V.tensor_tensor(ntil, tend, ntil, ALU.subtract)
            V.tensor_copy(tend_i[:], tend)
            dve.drain()
            V.tensor_scalar(ntil, ntil, float(P), None, ALU.mult)
            dve.drain()
            V.tensor_tensor(slot, bank[0][:, 0:TILES * NE].rearrange("p (t e) -> p t e", e=NE),
                            ntil.unsqueeze(1).to_broadcast([P, TILES, NE]), ALU.add)
            dve.drain()
            V.tensor_tensor(flat(slot), flat(slot), flat(msk[:, 0:TILES, :]), ALU.mult)
            dve.drain()
            V.tensor_reduce(two[:, :, 1], slot, AX.X, ALU.max)
            V.tensor_reduce(two[:, :, 0], slot, AX.X, ALU.add)
            dve.drain()
            V.tensor_tensor(two[:, :, 0], two[:, :, 0], two[:, :, 1], ALU.subtract)
            V.tensor_tensor(cmp_, slot, two[:, :, 1:2].to_broadcast([P, TILES, NE]), ALU.is_equal)
            dve.drain()
            V.tensor_copy(two_i[:], two)
            V.tensor_tensor(flat(cmp_), flat(cmp_), flat(msc), ALU.mult)
            dve.drain()
            V.tensor_reduce(gate[:, :, 1], cmp_, AX.X, ALU.add)
            V.tensor_tensor(flat(msc), flat(msc), flat(cmp_), ALU.subtract)
            V.tensor_scalar(rq_i[:, 0, :], flat(two_i[:]), P - 1, None, ALU.bitwise_and)
            V.tensor_scalar(rq_i[:, 1, :], flat(two_i[:]), 7, None, ALU.arith_shift_right)
            dve.drain()
            V.tensor_reduce(gate[:, :, 0], msc, AX.X, ALU.add)
            V.tensor_copy(flat(rq), flat(rq_i[:]))
            dve.drain()
            V.tensor_tensor(gate, gate, den.unsqueeze(2).to_broadcast([P, TILES, 2]), ALU.mult)
            V.tensor_tensor(oneB, rq[:, 1, :].unsqueeze(2).to_broadcast([P, 2 * TILES, SLOT_TILES]),
                            iota_j.unsqueeze(1).to_broadcast([P, 2 * TILES, SLOT_TILES]), ALU.is_equal)
            dve.drain()
            for h in range(2):
                last = V.tensor_tensor(oneB[:, h::2, :], oneB[:, h::2, :],
                                       token_id.unsqueeze(2).to_broadcast([P, TILES, SLOT_TILES]), ALU.mult)
            last = V.tensor_tensor(oneA, rq[:, 0, :].unsqueeze(2).to_broadcast([P, 2 * TILES, P]),
                                   iota_p.unsqueeze(1).to_broadcast([P, 2 * TILES, P]), ALU.is_equal)
            last.then_inc(S["id_need"], 1)
            V.tensor_tensor(cmpj, iota_j.unsqueeze(2).to_broadcast([P, SLOT_TILES, NE]),
                            tend.unsqueeze(1).to_broadcast([P, SLOT_TILES, NE]), ALU.is_ge)
            dve.drain()
            V.tensor_reduce(ej, cmpj, AX.X, ALU.add)
            dve.drain()
            V.tensor_scalar(ej, ej, float(NE - 1), None, ALU.min)
            dve.drain()
            V.tensor_copy(ej_i[:, 0, :], ej)
            V.tensor_scalar(ej_i[:, 1, :], ej, 2.0, None, ALU.add)
            V.tensor_scalar(ej_i[:, 2, :], ej, 1.0, None, ALU.add)
            V.tensor_scalar(pairs_i[:, 0:1], tend[:, NE - 1:NE], -1.0, None, ALU.add)
            dve.drain()
            V.tensor_scalar(ej_i[:, 0, :], ej_i[:, 0, :], 1, None, ALU.bitwise_and)
            V.tensor_scalar(ej_i[:, 1:3, :], ej_i[:, 1:3, :], 1, None, ALU.arith_shift_right)
            V.tensor_scalar(pairs_i[:, 0:1], pairs_i[:, 0:1], 1, None, ALU.arith_shift_right)
            dve.drain()
            V.tensor_scalar(ej_i[:, 1:3, :], ej_i[:, 1:3, :], 48.0, None, ALU.mult)
            V.memset(idtab[:, SLOT_TILES:SLOT_TILES + 2], 0)
            dve.wait_ge(S["idm_made"], 1)
            V.tensor_copy(idtab[:, 0:SLOT_TILES], bank[1][:, 0:SLOT_TILES]).then_inc(S["table_ready"], 1)
            shared(TILES - 1, 1)

            dve.wait_ge(S["table_ready"], 1)
            more = dve.value_load(pairs_i[0:1, 0:1], min_val=0, max_val=SLOT_TILES // 2 - 1)
            y_st = (S["y_st0"], S["y_st1"])

            def dhid(j, s):
                dve.wait_ge(S["sg_ready"], j + 1)
                V.tensor_tensor(hx[:, s, :], sg[:, s, :], bank[s][:, DE:2 * DE], ALU.mult).then_inc(S["hx_ready"], 1)

            def dy(j, s, n):
                dve.wait_ge(S["dx_made"], j + 1)
                dve.wait_ge(y_st[s], n)
                V.tensor_copy(ysb[:, s, 512:1024], bank[6][:]).then_inc(S["yb_ready"], 1)

            dhid(0, 0)
            with dve.Fori(0, more) as i:
                for s, j in ((1, 2 * i + 1), (0, 2 * i + 2)):
                    dhid(j, s)
                    dy(j - 1, 1 - s, i * 16)
            end = more * 2 + 1
            dhid(end, 1)
            dy(end - 1, 0, more * 16)
            dy(end, 1, more * 16)
            dve.wait_ge(y_st[0], more * 16 + 16)
            dve.wait_ge(y_st[1], more * 16 + 16)
            V.memset(bst2, 0.0).then_inc(S["base_all"], 1)

            ye_ld, out_st = (S["ye_ld0"], S["ye_ld1"]), (S["out_st0"], S["out_st1"])
            dve.wait_ge(S["ln2_loaded"], 32)
            dve.drain()

            def z_stats(t, s, n):
                dve.drain()
                dve.wait_ge(ye_ld[s], n * 32)
                V.scalar_tensor_tensor(zb[:, s, :], y1[:, s, :], gcol[:, s, 0:1], base[:, t, :], ALU.mult, ALU.add)
                dve.drain()
                V.scalar_tensor_tensor(zb[:, s, :], y2[:, s, :], gcol[:, s, 1:2], zb[:, s, :],
                                       ALU.mult, ALU.add).then_inc(S["z_sum"], 1)
                dve.drain()
                for c in range(2):
                    V.bn_stats(bst2[:, s, c, :], zb[:, s, 512 * c:512 * c + 512])
                dve.drain()
                V.bn_aggr(mv2[:, s, :], bst2[:, s].rearrange("p a b -> p (a b)"))
                dve.drain()
                V.tensor_scalar(rstd2[:, s, :], mv2[:, s, 1:2], LN_EPS, None, ALU.add).then_inc(S["z_var"], 1)
                dve.wait_ge(S["z_rstd"], t + 1)
                V.scalar_tensor_tensor(nmr2[:, s, :], mv2[:, s, 0:1], -1.0, rstd2[:, s, :], ALU.mult, ALU.mult)\
                 .then_inc(S["z_nmr"], 1)

            def z_out(t, s, n):
                dve.wait_ge(S["z_gain"], t + 1)
                dve.wait_ge(out_st[s], n * 16)
                V.tensor_tensor(ob[:, s, :], zb[:, s, :], ln2b, ALU.add).then_inc(S["fin_ready"], 1)

            z_stats(0, 0, 1)
            with dve.Fori(0, TILES // 2 - 1) as i:
                z_stats(2 * i + 1, 1, i + 1)
                z_out(2 * i, 0, i)
                z_stats(2 * i + 2, 0, i + 2)
                z_out(2 * i + 1, 1, i)
            z_stats(TILES - 1, 1, TILES // 2)
            z_out(TILES - 2, 0, TILES // 2 - 1)
            z_out(TILES - 1, 1, TILES // 2 - 1)

        @block.gpsimd
        def _(pool):
            G = nc.gpsimd

            with pool.Fori(0, TILES // 2) as i:
                for s in range(2):
                    t = 2 * i + s
                    pool.wait_ge(S["xts_ready"], t + 1)
                    G.tensor_copy(xT[:, :, bass.ds(t * P, P)], xts[:, s]).then_inc(S["xT_ready"], 1)
            pool.wait_ge(S["wo_loaded"], 96)
            for k in range(KD):
                last = G.tensor_scalar(w_o[:, k, :], w_o[:, k, :], gains[:, k:k + 1], None, ALU.mult)
            last.then_inc(S["wo_scaled"], 1)

            pool.wait_ge(S["ones_ready"], 1)

            def c_step(t, s, ok):
                if ok(0):
                    pool.wait_ge(S["ln_var"], t + 1)
                    G.tensor_tensor(rstd[:, s, :], rstd[:, s, :], minus_half, ALU.pow).then_inc(S["ln_rstd"], 1)
                if ok(2):
                    pool.wait_ge(S["rms_var"], t + 3)
                    G.tensor_tensor(rms[:, s, :], rms[:, s, :], minus_half.to_broadcast([P, 2]), ALU.pow)\
                     .then_inc(S["rms_rstd"], 1)

            for t in range(-2, 2):
                c_step(t, t % 2, lambda d, t=t: 0 <= t + d < TILES)
            with pool.Fori(0, TILES // 2 - 2) as i:
                for s in range(2):
                    c_step(2 * i + 2 + s, s, lambda d: True)
            for t in range(TILES - 2, TILES):
                c_step(t, t % 2, lambda d, t=t: 0 <= t + d < TILES)

            pool.wait_ge(S["table_ready"], 1)
            pool.wait_ge(S["x1_st0"], 16 * (TILES // 2))
            pool.wait_ge(S["x1_st1"], 16 * (TILES // 2))
            pool.wait_ge(S["base_done"], TILES)
            more = pool.value_load(pairs_i[0:1, 0:1], min_val=0, max_val=SLOT_TILES // 2 - 1)
            g_ld = (S["g_ld0"], S["g_ld1"])

            def gather(j, s, first=False):
                if not first:
                    pool.wait_ge(S["xgT_made"], j - 1)
                G.tensor_copy(idc[:, s:s + 1], idtab[:, bass.ds(j, 1)]).then_inc(S["ids_col"], 1)
                pool.wait_ge(S["ids_col"], j + 1)
                pool.sem_inc(S["gathers_begun"], 1)
                G.indirect_dma_start(out=xg[:, s, :], out_offset=None, in_=x1_d,
                                     in_offset=bass.IndirectOffsetOnAxis(ap=idc[:, s:s + 1].bitcast(U32), axis=0))\
                 .then_inc(g_ld[s], 16)

            gather(0, 0, True)
            gather(1, 1, True)
            with pool.Fori(0, more) as i:
                for s in range(2):
                    gather(2 * i + 2 + s, s)

            pool.wait_ge(S["base_all"], 1)
            pool.wait_ge(S["ln2_loaded"], 32)
            ye_ld = (S["ye_ld0"], S["ye_ld1"])

            def fetch(t, s, first=False):
                if not first:
                    pool.wait_ge(S["z_sum"], t - 1)
                G.tensor_copy(gcol[:, s, :], gate[:, t, :])
                G.tensor_copy(idy[:, s, :], two_i[:, t, :]).then_inc(S["cols_ready"], 1)
                pool.wait_ge(S["cols_ready"], t + 1)
                pool.sem_inc(S["gathers_begun"], 1)
                for c, y in enumerate((y1, y2)):
                    G.indirect_dma_start(out=y[:, s, :], out_offset=None, in_=y_d,
                                         in_offset=bass.IndirectOffsetOnAxis(ap=idy[:, s, c:c + 1].bitcast(U32),
                                                                             axis=0)).then_inc(ye_ld[s], 16)

            def finish(t, s):
                pool.wait_ge(S["z_var"], t + 1)
                G.tensor_tensor(rstd2[:, s, :], rstd2[:, s, :], minus_half, ALU.pow).then_inc(S["z_rstd"], 1)
                pool.wait_ge(S["z_norm"], t + 1)
                G.tensor_tensor(zb[:, s, :], zb[:, s, :], ln2g, ALU.mult).then_inc(S["z_gain"], 1)

            fetch(0, 0, True)
            fetch(1, 1, True)
            with pool.Fori(0, TILES // 2 - 1) as i:
                for s in range(2):
                    finish(2 * i + s, s)
                    fetch(2 * i + 2 + s, s)
            for s in range(2):
                finish(TILES - 2 + s, s)


_WEIGHTS = ["w_in", "sink_a", "norm_a", "norm_b", "w_out", "ln1_g", "ln1_b", "w_router", "router_bias",
            "w_gate", "w_up", "w_down", "ws_gate", "ws_up", "ws_down", "ln2_g", "ln2_b"]
_WHOLE = {"w_router", "router_bias"}


def kernel(**inputs):
    import concourse.bacc as _bacc
    from concourse.bass_utils import run_bass_kernel_spmd as _run

    nc = _bacc.Bacc("TRN2", target_bir_lowering=False, num_devices=1)
    arrays, args = {}, []

    def give(name, a):
        a = np.ascontiguousarray(a)
        arrays[f"in_{name}"] = a
        args.append(nc.dram_tensor(f"in_{name}", a.shape, mybir.dt.from_np(a.dtype), kind="ExternalInput").ap())

    give("x", np.concatenate([np.asarray(inputs["x_prompt"])[0], np.asarray(inputs["x_sample"])[0]], 0))
    for name in _WEIGHTS:
        a = np.asarray(inputs[name])
        give(name, a if name in _WHOLE else a[0])
    for name, a in constants().items():
        give(name, a)
    args.append(nc.dram_tensor("out_y", (TOKENS, D), FP32, kind="ExternalOutput").ap())
    encoder_layer(nc, *args)
    r = _run(nc, [arrays], core_ids=[0])
    y = r.results[0]["out_y"]
    return y[0:512].reshape(1, 512, D), y[512:TOKENS].reshape(1, 1024, D)
```

```python
import numpy as np
import concourse.bass as bass
from concourse import mybir
from contextlib import ExitStack

FP32 = mybir.dt.float32
FP32R = mybir.dt.float32r
I32 = mybir.dt.int32
U32 = mybir.dt.uint32
ALU = mybir.AluOpType
ACT = mybir.ActivationFunctionType
AX = mybir.AxisListType

P = 128
D = 1024
KD = D // P
SEQS = ((0, 512), (512, 1024))
TOKENS = 1536
TILES = TOKENS // P
GROUPS = TOKENS // 512
HD = 64
PAIRS = 4
OW = HD + 2
NE = 16
NGRP = 4
DE = 256
ALPHA = 2.0 ** 0.25
LN_EPS = 1e-5
RMS_EPS = 1e-6
A_RADIUS = 128
B_RADIUS = 64
ST = 256
SHARED_TILES = TOKENS // ST
SLOT_TILES = (2 * TOKENS + NE * (ST - 1)) // ST // 2 * 2 + 2
MIN_PAIRS = 2 * TOKENS // ST // 2
COLS = SLOT_TILES * 2
QA0, KA0, VA0, QB0, KB0, VB0 = 0, 512, 640, 768, 1280, 1792
UNITS = 72
BIG = 3.0e38


def constants():
    h = np.arange(1, 17, dtype=np.float32)
    slopes = np.exp2(-8.0 * h / 16).astype(np.float32)
    p = np.arange(P)[:, None]
    hd8 = np.float32(8.0)

    def table(step, ok, slope, mult=None):
        t = -slope * np.abs(step).astype(np.float32)
        if mult is not None:
            t = t + np.log(np.maximum(mult, 1)).astype(np.float32)
        return np.where(ok, hd8 * t, np.float32(-1e37)).astype(np.float32)

    rel_a = np.arange(384)[None, :] - 128 - p
    rel_1 = np.arange(256)[None, :] - 64 - p
    rel_2 = np.arange(384)[None, :] - 128 - p
    mult2 = (np.abs(rel_2) <= B_RADIUS).astype(np.float32) + (rel_2 % 4 == 0)
    tab_a = np.stack([np.stack([table(rel_a, np.abs(rel_a) <= A_RADIUS, slopes[0::2][i + 4 * half])
                                for half in range(2)], 1) for i in range(PAIRS)])
    tab_1 = np.stack([np.stack([table(rel_1, np.abs(rel_1) <= B_RADIUS, slopes[1::2][2 * i + half])
                                for half in range(2)], 1) for i in range(PAIRS)])
    tab_2 = np.stack([np.stack([table(4 * rel_2, mult2 > 0, slopes[1::2][2 * i + half], mult2)
                                for half in range(2)], 1) for i in range(PAIRS)])
    row = np.zeros((P, 512), np.float32)
    row[:, 0:128] = np.eye(P)
    row[:, 128:256] = np.arange(P)[:, None] < np.arange(P)[None, :]
    row[:, 256:384] = np.arange(P)[None, :]
    row[:, 384:384 + COLS] = np.arange(COLS)[None, :]
    row[:, 440:440 + TILES] = np.arange(TILES)[None, :] * P + np.arange(P)[:, None]
    row[:, 452:456] = 3 - np.arange(4)[None, :]
    return {"tab_a": tab_a, "tab_1": tab_1, "tab_2": tab_2, "const": row}


def encoder_layer(nc, x, w_in, sink, norm_a, norm_b, w_out, ln1_g, ln1_b, w_router, router_bias,
                  w_gate, w_up, w_down, ws_gate, ws_up, ws_down, ln2_g, ln2_b,
                  tab_a, tab_1, tab_2, const, out):
    vb_d = nc.dram_tensor("vb_scratch", (TOKENS, 512), FP32, kind="Internal").ap()
    o_d = nc.dram_tensor("o_scratch", (TOKENS, 3 * PAIRS * 2 * OW), FP32, kind="Internal").ap()
    x1_d = nc.dram_tensor("x1_scratch", (TOKENS, D), FP32, kind="Internal").ap()
    y_d = nc.dram_tensor("y_scratch", (SLOT_TILES * ST, D), FP32, kind="Internal").ap()

    ctx = ExitStack()
    with ctx:
        def isb(name, *shape):
            return ctx.enter_context(nc.sbuf_tensor(name, list(shape), I32))

        def cut(tensor):
            at = [0]

            def take(*dims):
                n = int(np.prod(dims))
                v = tensor[:, at[0]:at[0] + n]
                at[0] += n
                assert at[0] <= tensor.shape[1], (tensor.name, at[0])
                if len(dims) == 2:
                    v = v.rearrange("p (a b) -> p a b", b=dims[1])
                if len(dims) == 3:
                    v = v.rearrange("p (a b c) -> p a b c", b=dims[1], c=dims[2])
                return v

            def move(word):
                at[0] = word
            return take, move

        keep = ctx.enter_context(nc.sbuf_tensor("keep", [P, 1088], FP32))
        take, _ = cut(keep)
        cst = take(512)
        ident, tri, iota_p = cst[:, 0:128], cst[:, 128:256], cst[:, 256:384]
        token_id, rank0 = cst[:, 440:440 + TILES], cst[:, 452:456]
        iota_j = cst[:, 384:384 + COLS]
        logits = take(TILES, NE)
        w_rt = take(KD, NE)
        rbias = take(NE)
        nsink = take(8)
        gains = take(KD)
        minus_half = take(1)
        eps_ln = take(1)
        eps_rms = take(1)
        ones = take(P)
        gtab = take(COLS)
        gcol = take(2)
        two_i = isb("two_i", P, TILES, 2)
        rq_i = isb("rq_i", P, 2, TILES * 2)
        idtab = isb("idtab", P, COLS)
        ntil_i = isb("ntil_i", P, NE)
        ej_i = isb("ej_i", P, SLOT_TILES)
        more_i = isb("more_i", P, 2)
        idc = isb("idc", P, 2)

        RAW = 2 * D + KD * D
        with ExitStack() as phase:
            ab = phase.enter_context(nc.sbuf_tensor("ab", [P, 45456], FP32))
            take, move = cut(ab)
            w_v = take(KD, 640)
            xin = take(2, D)
            xts = take(2, KD, P)
            vst = take(2, 512)
            move(RAW)
            xT = take(KD, TOKENS)
            Va = take(TILES, P)
            V1 = take(14, P)
            V2 = take(TILES, P)
            ost = [take(TILES, 2, OW) for _ in range(3)]
            QA, KA, QB, KB = (take(TOKENS) for _ in range(4))
            wqa, wqb, wkb = (take(KD, P) for _ in range(3))
            tA = take(2, 384)
            t1 = take(2, 256)
            t2 = take(2, 384)
            prob = take(2, 384)
            probT = take(2, 384)
            zeros = take(512)
            wka = ost[0].rearrange("p a b c -> p (a b c)")[:, 0:1024].rearrange("p (k c) -> p k c", c=P)
        with ExitStack() as phase:
            c_raw = phase.enter_context(nc.sbuf_tensor("c_raw", [P, RAW], FP32))
            take, _ = cut(c_raw)
            ln1g = take(D)
            ln1b = take(D)
            raw_o = take(KD, D)
            c_work = phase.enter_context(nc.sbuf_tensor("c_work", [P, 12288], FP32))
            take, _ = cut(c_work)
            odt = take(2, 3 * PAIRS * 2 * OW)
            xr = take(2, D)
            om = take(2, D)
            res = take(D)
            x1s = take(2, D)
            x1T = take(KD, P)
            junk2 = take(512)
            mD = take(4, 8)
            mM = take(2, 8)
            mL = take(3, 8)
            mR = take(2, 8)
            mW = take(3, 8)
            ssq = take(2, 2)
            rms = take(2, 2)
            bst = take(2, 6)
            mv = take(2, 2)
            rstd = take(2, 1)

            def split_pair(stack, name, words):
                return [stack.enter_context(nc.sbuf_tensor(name + part, [P, words], FP32R))
                        for part in ("_hi", "_lo")]

            oT_hi, oT_lo = split_pair(phase, "oT", 2 * D)
            wo_hi, wo_lo = split_pair(phase, "w_o", KD * D)
        GU = KD * 2 * DE
        d_work = ctx.enter_context(nc.sbuf_tensor("d_work", [P, RAW + TILES * D], FP32))
        take, _ = cut(d_work)
        sg = take(2, 512)
        hx = take(2, 512)
        raw_gu = take(KD, 2 * DE)
        raw_d = take(2, D)
        slab = take(2, D)
        base = take(TILES, D)
        with ExitStack() as phase:
            r_work = phase.enter_context(nc.sbuf_tensor("r_work", [P, 2 * GU], FP32))
            take, _ = cut(r_work)
            score = take(TILES, NE)
            rank = take(TILES, NE)
            cmp_ = take(TILES, NE)
            bia = take(TILES, NE)
            gsc = take(TILES, NGRP)
            grank = take(TILES, NGRP)
            gcmp = take(TILES, NGRP)
            msk = take(TILES + 1, NE)
            msc = take(TILES, NE)
            slot = take(TILES, NE)
            den = take(TILES)
            two = take(TILES, 2)
            gate = take(TILES, 2)
            tend = take(NE)
            ntil = take(NE)
            cmpj = take(SLOT_TILES, NE)
            ej = take(SLOT_TILES)
            rq = take(2, TILES * 2)
            oneB = take(2 * TILES, 2, COLS)
            oneA = take(2 * TILES, P)
        gu0 = split_pair(ctx, "w_gu0", GU)
        xg_hi, xg_lo = split_pair(ctx, "xgT", KD * 2 * P)
        wd_hi, wd_lo = split_pair(ctx, "w_dn", 2 * D)
        h_hi, h_lo = split_pair(ctx, "hT", 2 * 512)
        xg = ctx.enter_context(nc.sbuf_tensor("xg", [P, 2, D], FP32))
        gu1 = split_pair(ctx, "w_gu1", GU)
        w_gu = (gu0, gu1)
        take, move = cut(d_work)
        ob = take(2, D)
        ln2g = take(D)
        ln2b = take(D)
        zb = take(D)
        bst2 = take(2, 2, 6)
        mv2 = take(2, 2)
        rstd2 = take(2, 1)

        def whole(t, w):
            return t[:].rearrange("p (k c) -> p k c", c=w)

        def plain(a):
            return a.bitcast(FP32)

        bank = [ctx.enter_context(nc.psum_tensor(f"bank{b}", [P, 512], FP32)) for b in range(8)]

        names = """c_loaded wv_loaded wk_loaded wa_loaded wb_loaded x_ld0 x_ld1 xt_made xts_ready
            xT_ready v_made v_ready vb_st0 vb_st1 proj_made proj_ready ta_loaded t1_loaded t2_loaded
            v1_loaded v2_loaded qk_made biased exp_done pT_made pT_ready pv_made o_ready units_begun
            oA_st o1_st o2_st wo_loaded wr_loaded ones_ready y_zeroed
            wo_hi wo_lo od_ld0 od_ld1 xr_ld0 xr_ld1 x1_st0 x1_st1 op_made res_done oT_made oT_hi oT_lo om_ready
            merge_need merge_exp merged squares rms_rstd ln_var ln_rstd x1_ready x1T_made x1T_ready
            lg_made lg_ready lgexp_done
            rows_ld base_set wg_ld wd_ld wg_hi wg_lo wd_hi wd_lo xgT_made xg_hi xg_lo gx_made sg_ready
            hx_made h_hi h_lo dx_made y_read0 y_read1 y_st0 y_st1 y_all
            cum_need cum_made cum_read ej_ready id_need idm_made table_ready ids_col gathers_begun g_ld
            gcol_ready ln2_loaded z_var z_rstd fin_ready out_st0 out_st1""".split()
        names += [f"e_add{t}" for t in range(TILES)]
        S = {n: ctx.enter_context(nc.semaphore(n)) for n in names}
        block = ctx.enter_context(nc.Block())

        kinds = []
        for half in range(2):
            hp = slice(HD * half, HD * half + HD)
            for s0, L in SEQS:
                for j in range(L // P):
                    k0, k1 = max(0, P * (j - 1)), min(L, P * (j + 2))
                    off = k0 - P * (j - 1)
                    kinds.append((0, half, s0 // P + j, QA[hp, s0 + P * j:s0 + P * j + P],
                                  KA[hp, s0 + k0:s0 + k1], k1 - k0, tA[:, half, off:off + k1 - k0],
                                  [(P, Va[:, (s0 + k0) // P + c, hp]) for c in range((k1 - k0) // P)]))
        for half in range(2):
            hp = slice(HD * half, HD * half + HD)
            for s0, L in SEQS:
                nb = L // P
                for j in range(nb):
                    k0, k1 = max(0, P * j - B_RADIUS), min(L, P * (j + 1) + B_RADIUS)
                    off = k0 - (P * j - B_RADIUS)
                    vt = 0 if s0 == 0 else 5
                    rows = [(64 if m in (0, nb) else P) for m in (j, j + 1)]
                    kinds.append((1, half, s0 // P + j, QB[hp, s0 + P * j:s0 + P * j + P],
                                  KB[hp, s0 + k0:s0 + k1], k1 - k0, t1[:, half, off:off + k1 - k0],
                                  [(r, V1[0:r, vt + m, hp]) for r, m in zip(rows, (j, j + 1))]))
        for half in range(2):
            hp = slice(HD * half, HD * half + HD)
            for s0, L in SEQS:
                qs = QB[hp, s0:s0 + L].rearrange("c (s r) -> c r s", r=4)
                ks = KB[hp, s0:s0 + L].rearrange("c (s r) -> c r s", r=4)
                nb = L // 512
                for r in range(4):
                    for b in range(nb):
                        off = P * (1 - b)
                        kinds.append((2, half, s0 // P + r * nb + b, qs[:, r, P * b:P * b + P],
                                      ks[:, r, :], L // 4, t2[:, half, off:off + L // 4],
                                      [(P, V2[:, s0 // P + r * nb + c, hp]) for c in range(nb)]))
        assert len(kinds) == UNITS

        def proj_plan():
            plan = {}
            for n in range(48):
                plan.setdefault(n * 20 // 48, []).append((n // 8, n % 8))
            for n in range(24):
                plan.setdefault(26 + n * 40 // 24, []).append((6 + n // 8, n % 8))
            return plan

        PLAN = proj_plan()
        GROUP_END = {g: max(s for s, ms in PLAN.items() if any(m[0] == g for m in ms)) for g in range(9)}

        def pslot(n):
            return bank[6 + n % 2]

        @block.sync
        def _(sp):
            x_t = x.rearrange("(t p) d -> t p d", p=P)
            out_t = out.rearrange("(t p) d -> t p d", p=P)
            vb_t = vb_d.rearrange("(t p) d -> t p d", p=P)
            od_t = o_d.rearrange("(t p) d -> t p d", p=P)
            w_cols = w_in.rearrange("(k p) c -> p k c", p=P)
            x_ld, vb_st = (S["x_ld0"], S["x_ld1"]), (S["vb_st0"], S["vb_st1"])

            sp.dma_start(xin[:, 0, :], x_t[0]).then_inc(x_ld[0], 16)
            sp.dma_start(cst, const).then_inc(S["c_loaded"], 16)
            sp.dma_start(w_v[:, :, 0:512], w_cols[:, :, VB0:VB0 + 512]).then_inc(S["wv_loaded"], 16)
            sp.dma_start(w_v[:, :, 512:640], w_cols[:, :, VA0:VA0 + P]).then_inc(S["wv_loaded"], 16)
            sp.dma_start(xin[:, 1, :], x_t[1]).then_inc(x_ld[1], 16)
            sp.dma_start(wka, w_cols[:, :, KA0:KA0 + P]).then_inc(S["wk_loaded"], 16)

            def load_wqa(i):
                for half in range(2):
                    sp.dma_start(wqa[:, :, HD * half:HD * half + HD],
                                 w_cols[:, :, bass.ds(QA0 + 256 * half + i * HD, HD)])\
                      .then_inc(S["wa_loaded"], 16)

            def load_wb(i):
                sp.dma_start(wqb, w_cols[:, :, bass.ds(QB0 + i * P, P)]).then_inc(S["wb_loaded"], 16)
                sp.dma_start(wkb, w_cols[:, :, bass.ds(KB0 + i * P, P)]).then_inc(S["wb_loaded"], 16)

            def load_v1(i):
                cs = bass.ds(i * P, P)
                for s0, L, vt in ((0, 512, 0), (512, 1024, 5)):
                    nb = L // P
                    mid = vb_d[s0 + 64:s0 + L - 64, cs].rearrange("(t p) c -> p t c", p=P)
                    sp.dma_start(V1[:, vt + 1:vt + nb, :], mid).then_inc(S["v1_loaded"], 16)
                    sp.dma_start(V1[0:64, vt, :], vb_d[s0:s0 + 64, cs]).then_inc(S["v1_loaded"], 16)
                    sp.dma_start(V1[0:64, vt + nb, :], vb_d[s0 + L - 64:s0 + L, cs])\
                      .then_inc(S["v1_loaded"], 16)

            def load_v2(i):
                cs = bass.ds(i * P, P)
                sp.dma_start(V2[:, 0:4, :], vb_d[0:512, cs].rearrange("(s r) c -> s r c", r=4))\
                  .then_inc(S["v2_loaded"], 16)
                for b in range(2):
                    sp.dma_start(V2[:, 4 + b:12:2, :],
                                 vb_d[512 + 512 * b:1024 + 512 * b, cs].rearrange("(s r) c -> s r c", r=4))\
                      .then_inc(S["v2_loaded"], 16)

            def load_x(t, s):
                sp.wait_ge(S["xt_made"], t - 1)
                sp.dma_start(xin[:, s, :], x_t[t]).then_inc(x_ld[s], 16)

            def store_v(t, s):
                sp.wait_ge(S["v_ready"], t + 1)
                sp.dma_start(vb_t[t], vst[:, s, :]).then_inc(vb_st[s], 16)

            load_wqa(0)
            load_wb(0)
            with sp.Fori(0, TILES // 2 - 1) as i:
                for s in range(2):
                    load_x(2 * i + 2 + s, s)
                    store_v(2 * i + s, s)
            for s in range(2):
                store_v(TILES - 2 + s, s)
            sp.dma_start(tA, tab_a[0]).then_inc(S["ta_loaded"], 16)
            sp.dma_start(t1, tab_1[0]).then_inc(S["t1_loaded"], 16)
            sp.dma_start(t2, tab_2[0]).then_inc(S["t2_loaded"], 16)
            for s in range(2):
                sp.wait_ge(vb_st[s], 16 * (TILES // 2) + 16)
            load_v1(0)
            load_v2(0)
            sp.wait_ge(S["xT_ready"], TILES)
            sp.wait_ge(S["v_made"], TILES)
            for c, part in enumerate((w_out[0:256], w_out[256:512])):
                sp.dma_start(raw_o[HD * c:HD * c + HD, 0:4, :], part.rearrange("(i p) n -> p i n", p=HD))\
                  .then_inc(S["wo_loaded"], 16)
            sp.dma_start(raw_o[:, 4:8, :], w_out[512:1024].rearrange("(k p) n -> p k n", p=P))\
              .then_inc(S["wo_loaded"], 16)
            for c in range(2):
                sp.dma_start(gains[HD * c:HD * c + HD, 0:4],
                             norm_a[256 * c:256 * c + 256].rearrange("(i p) -> p i", p=HD),
                             allow_slow_non_contiguous=True).then_inc(S["wo_loaded"], 16)
            sp.dma_start(gains[:, 4:8], norm_b.rearrange("(k p) -> p k", p=P),
                         allow_slow_non_contiguous=True).then_inc(S["wo_loaded"], 16)
            sp.dma_start(w_rt, w_router.rearrange("(k p) e -> p k e", p=P)).then_inc(S["wr_loaded"], 16)
            sp.dma_start(ln1g, ln1_g.partition_broadcast(P)).then_inc(S["wr_loaded"], 16)
            sp.dma_start(ln1b, ln1_b.partition_broadcast(P)).then_inc(S["wr_loaded"], 16)
            sp.dma_start(rbias, router_bias.partition_broadcast(P)).then_inc(S["wr_loaded"], 16)
            for c in range(2):
                sp.dma_start(nsink[:, c:8:2], sink[4 * c:4 * c + 4].partition_broadcast(P),
                             allow_slow_non_contiguous=True).then_inc(S["wr_loaded"], 16)

            sp.wait_ge(S["ones_ready"], 1)
            sp.dma_start(y_d[2 * TOKENS:, :].rearrange("(p a) (h d) -> p (a h) d", p=P, d=512),
                         zeros.unsqueeze(1).to_broadcast([P, 2 * (SLOT_TILES * ST - 2 * TOKENS) // P, 512]))\
              .then_inc(S["y_zeroed"], 16)

            def store_o(kind, i):
                c0 = (2 * PAIRS * kind) * OW
                sem = S[("oA_st", "o1_st", "o2_st")[kind]]
                cs = bass.ds(i * (2 * OW) + c0, 2 * OW)
                flat = ost[kind].rearrange("p t h e -> p t (h e)")
                if kind < 2:
                    sp.dma_start(o_d[:, cs].rearrange("(t p) e -> p t e", p=P), flat).then_inc(sem, 16)
                    return
                sp.dma_start(o_d[0:512, cs].rearrange("(s r) e -> s r e", r=4), flat[:, 0:4, :]).then_inc(sem, 16)
                for b in range(2):
                    sp.dma_start(o_d[512 + 512 * b:1024 + 512 * b, cs].rearrange("(s r) e -> s r e", r=4),
                                 flat[:, 4 + b:12:2, :]).then_inc(sem, 16)

            def pair(i, last):
                if not last:
                    sp.wait_ge(S["proj_made"], 6 + i * 9)
                    load_wqa(i + 1)
                    sp.wait_ge(S["proj_made"], 12 + i * 9)
                    load_wb(i + 1)
                    sp.wait_ge(S["biased"], i * UNITS + 24)
                    sp.dma_start(tA, tab_a[i + 1]).then_inc(S["ta_loaded"], 16)
                sp.wait_ge(S["o_ready"], i * 18 + 6)
                store_o(0, i)
                if not last:
                    sp.wait_ge(S["biased"], i * UNITS + 48)
                    sp.dma_start(t1, tab_1[i + 1]).then_inc(S["t1_loaded"], 16)
                sp.wait_ge(S["o_ready"], i * 18 + 12)
                store_o(1, i)
                if not last:
                    load_v1(i + 1)
                    sp.wait_ge(S["biased"], i * UNITS + 72)
                    sp.dma_start(t2, tab_2[i + 1]).then_inc(S["t2_loaded"], 16)
                sp.wait_ge(S["o_ready"], i * 18 + 18)
                store_o(2, i)
                if not last:
                    load_v2(i + 1)

            with sp.Fori(0, PAIRS - 1) as i:
                pair(i, False)
            pair(PAIRS - 1, True)

            sp.wait_ge(S["oA_st"], 16 * PAIRS + 16)
            sp.wait_ge(S["o1_st"], 16 * PAIRS + 16)
            sp.wait_ge(S["o2_st"], 48 * PAIRS + 48)
            od_ld, xr_ld = (S["od_ld0"], S["od_ld1"]), (S["xr_ld0"], S["xr_ld1"])
            sp.wait_ge(S["o_ready"], 18 * PAIRS)
            sp.wait_ge(S["pT_ready"], UNITS * PAIRS)
            sp.dma_start(odt[:, 0, :], od_t[0]).then_inc(od_ld[0], 16)
            sp.dma_start(odt[:, 1, :], od_t[1]).then_inc(od_ld[1], 16)
            sp.dma_start(xr[:, 0, :], x_t[0]).then_inc(xr_ld[0], 16)

            def load_raw_gu(gate_w, up_w):
                sp.dma_start(raw_gu[:, :, 0:DE], gate_w.rearrange("(k p) f -> p k f", p=P)).then_inc(S["wg_ld"], 16)
                sp.dma_start(raw_gu[:, :, DE:2 * DE], up_w.rearrange("(k p) f -> p k f", p=P))\
                  .then_inc(S["wg_ld"], 16)

            def load_raw_d(w):
                sp.dma_start(raw_d, w.rearrange("(k p) n -> p k n", p=P)).then_inc(S["wd_ld"], 16)

            def c_step(t, s, ok):
                if ok(2):
                    sp.wait_ge(S["merged"], t + 1)
                    sp.dma_start(odt[:, s, :], od_t[t + 2]).then_inc(od_ld[s], 16)
                if ok(1):
                    if not isinstance(t, int) or t > 0:
                        sp.wait_ge(S["res_done"], t)
                    sp.dma_start(xr[:, 1 - s, :], x_t[t + 1]).then_inc(xr_ld[1 - s], 16)

            for t in range(2):
                c_step(t, t, lambda d: True)
                if t == 0:
                    sp.wait_ge(S["wo_lo"], 16)
                    load_raw_gu(ws_gate, ws_up)
                    load_raw_d(ws_down)
            with sp.Fori(0, TILES // 2 - 2) as i:
                for s in range(2):
                    c_step(2 * i + 2 + s, s, lambda d: True)
            for t in range(TILES - 2, TILES):
                c_step(t, t % 2, lambda d, t=t: 0 <= t + d < TILES)

            x1_two = x1_d.rearrange("(q h p) d -> q p h d", h=2, p=P)
            for q in range(SHARED_TILES):
                for h in range(2):
                    sp.wait_ge(S[f"x1_st{h}"], 16 * (q + 1))
                if q > 0:
                    sp.wait_ge(S["base_set"], 2 * q)
                    sp.wait_ge(S["xgT_made"], 2 * q)
                sp.dma_start(slab, x1_two[q]).then_inc(S["rows_ld"], 16)
                if q == 4:
                    sp.wait_ge(S["ej_ready"], 1)
                    sp.wait_ge(S["wg_lo"], KD)
                    first = sp.value_load(ej_i[0:1, 0:1], min_val=0, max_val=NE - 1)
                    load_raw_gu(w_gate[first], w_up[first])
            sp.wait_ge(S["table_ready"], 1)
            more = sp.value_load(more_i[0:1, 0:1], min_val=MIN_PAIRS - 2, max_val=SLOT_TILES // 2 - 2)

            def load_d(j):
                e = sp.value_load(ej_i[0:1, bass.ds(j, 1)], min_val=0, max_val=NE - 1)
                sp.wait_ge(S["wd_lo"], j * 4 + 4)
                load_raw_d(w_down[e])

            def load_gu(j):
                e = sp.value_load(ej_i[0:1, bass.ds(j, 1)], min_val=0, max_val=NE - 1)
                sp.wait_ge(S["wg_lo"], j * KD + KD)
                load_raw_gu(w_gate[e], w_up[e])

            with sp.Fori(0, more * 2 + 3) as j:
                load_gu(j + 1)
                load_d(j)
            load_d(more * 2 + 3)

            sp.wait_ge(S["y_all"], 1)
            sp.dma_start(ln2g, ln2_g.partition_broadcast(P)).then_inc(S["ln2_loaded"], 16)
            sp.dma_start(ln2b, ln2_b.partition_broadcast(P)).then_inc(S["ln2_loaded"], 16)
            out_st = (S["out_st0"], S["out_st1"])
            for t in range(TILES):
                sp.wait_ge(S["fin_ready"], t + 1)
                sp.dma_start(out_t[t], ob[:, t % 2, :]).then_inc(out_st[t % 2], 16)
            for s in range(2):
                sp.wait_ge(out_st[s], 16 * (TILES // 2))

        @block.tensor
        def _(pe):
            def transposes(src, banks, sem):
                for c in range(KD):
                    last = nc.tensor.transpose(banks[c // 4][:, P * (c % 4):P * (c % 4) + P],
                                               src[:, P * c:P * c + P], ident)
                last.then_inc(sem, 1)

            x_ld = (S["x_ld0"], S["x_ld1"])
            pe.wait_ge(S["c_loaded"], 16)

            def xt(t, s, n):
                pe.wait_ge(x_ld[s], 16 * n)
                transposes(xin[:, s, :], bank[2 * s:2 * s + 2], S["xt_made"])

            def vproj(t, s):
                pe.wait_ge(S["xts_ready"], t + 1)
                for k in range(KD):
                    nc.tensor.matmul(bank[4 + s][:], xts[:, s, k, :], w_v[:, k, 0:512],
                                     start=k == 0, stop=k == KD - 1)
                for k in range(KD):
                    last = nc.tensor.matmul(bank[6 + s][:, 0:P], xts[:, s, k, :], w_v[:, k, 512:640],
                                            start=k == 0, stop=k == KD - 1)
                last.then_inc(S["v_made"], 1)

            xt(0, 0, 1)
            pe.wait_ge(S["wv_loaded"], 32)
            with pe.Fori(0, TILES // 2 - 1) as i:
                xt(2 * i + 1, 1, i + 1)
                vproj(2 * i, 0)
                xt(2 * i + 2, 0, i + 2)
                vproj(2 * i + 1, 1)
            xt(TILES - 1, 1, TILES // 2)
            vproj(TILES - 2, 0)
            vproj(TILES - 1, 1)

            def proj(w, g, k, n, sem=None):
                last = nc.tensor.matmul(pslot(n)[:], w[:, k, :], xT[:, k, 512 * g:512 * g + 512],
                                        start=k == 0, stop=k == KD - 1)
                if k == KD - 1:
                    last.then_inc(S["proj_made"], 1)

            pe.wait_ge(S["xT_ready"], TILES)
            pe.wait_ge(S["v_ready"], TILES)
            pe.wait_ge(S["wk_loaded"], 16)
            pe.wait_ge(S["wa_loaded"], 32)
            for n in range(6):
                if n >= 2:
                    pe.wait_ge(S["proj_ready"], n - 1)
                for k in range(KD):
                    proj(wka if n < 3 else wqa, n % 3, k, n)

            def qk(u, i):
                kind, half, tile, q, k, n, tab, v = kinds[u]
                if u == 0:
                    pe.wait_ge(S["proj_ready"], 6 + i * 9)
                if u == 24:
                    pe.wait_ge(S["proj_ready"], 12 + i * 9)
                nc.tensor.matmul(bank[u % 2][:, 0:n], q, k, start=True, stop=True).then_inc(S["qk_made"], 1)

            def pT(u, i):
                kind, half, tile, q, k, n, tab, v = kinds[u]
                pe.wait_ge(S["exp_done"], i * UNITS + u + 1)
                at = [sum(r for r, _ in v[:c]) for c in range(len(v))]
                for c in sorted(range(len(v)), key=lambda c: -v[c][0]):
                    r = v[c][0]
                    last = nc.tensor.transpose(bank[2 + u % 2][0:r, P * c:P * c + P],
                                               prob[:, u % 2, at[c]:at[c] + r], ident)
                last.then_inc(S["pT_made"], 1)

            def pv(u, i):
                kind, half, tile, q, k, n, tab, v = kinds[u]
                if u == 24:
                    pe.wait_ge(S["v1_loaded"], (i + 1) * 96)
                if u == 48:
                    pe.wait_ge(S["v2_loaded"], (i + 1) * 48)
                pe.wait_ge(S["pT_ready"], i * UNITS + u + 1)
                o = bank[4 + (u // 4) % 2][:, HD * (u % 4):HD * (u % 4) + HD]
                for c, (r, rows) in enumerate(v):
                    last = nc.tensor.matmul(o, probT[0:r, u % 2, P * c:P * c + P], rows,
                                            start=c == 0, stop=c == len(v) - 1)
                if u % 4 == 3:
                    last.then_inc(S["pv_made"], 1)

            def pair(i, last):
                for g in range(UNITS):
                    if g + 2 < UNITS:
                        qk(g + 2, i)
                    elif not last:
                        qk(g + 2 - UNITS, i + 1)
                    todo = [m for m in PLAN.get(g, []) if m[0] < 6 or not last]
                    for j, (n, k) in enumerate(todo):
                        if k == 0:
                            pe.wait_ge(S["proj_ready"], i * 9 + (6 if n == 0 else 5 + n))
                            if n == 0:
                                pe.wait_ge(S["wb_loaded"], (i + 1) * 32)
                            if n == 6:
                                pe.wait_ge(S["wa_loaded"], (i + 2) * 32)
                        proj((wqb, wkb, wqa)[n // 3], n % 3, k, n)
                    if g + 1 < UNITS:
                        pT(g + 1, i)
                    elif not last:
                        pT(0, i + 1)
                    pv(g, i)

            qk(0, 0)
            qk(1, 0)
            pT(0, 0)
            with pe.Fori(0, PAIRS - 1) as i:
                pair(i, False)
            pair(PAIRS - 1, True)

            pe.wait_ge(S["o_ready"], 18 * PAIRS)
            pe.wait_ge(S["pT_ready"], UNITS * PAIRS)
            pe.wait_ge(S["wr_loaded"], 96)

            def three(o, w_hi, w_lo, x_hi, x_lo, first, last):
                nc.tensor.matmul(o, w_hi, x_hi, start=first, stop=False)
                nc.tensor.matmul(o, w_hi, x_lo, start=False, stop=False)
                return nc.tensor.matmul(o, w_lo, x_hi, start=False, stop=last)

            def op(t, s, first=False):
                pe.wait_ge(S["oT_lo"], t + 1)
                if not first:
                    pe.wait_ge(S["res_done"], t)
                for k in range(KD):
                    for c in range(2):
                        if first:
                            pe.wait_ge(S["wo_lo"], 2 * k + c + 1)
                        a, b = s * D + k * P, k * D + 512 * c
                        last = three(bank[c][:], oT_hi[:, a:a + P], oT_lo[:, a:a + P],
                                     wo_hi[:, b:b + 512], wo_lo[:, b:b + 512], k == 0, k == KD - 1)
                last.then_inc(S["op_made"], 1)

            def x1t(t, s, first=False, banks=bank[2:4]):
                pe.wait_ge(S["x1_ready"], t + 1)
                if not first:
                    pe.wait_ge(S["x1T_ready"], t)
                transposes(x1s[:, s, :], banks, S["x1T_made"])

            def ot(t, s, first=False):
                pe.wait_ge(S["om_ready"], t + 1)
                if not first:
                    pe.wait_ge(S["oT_lo"], t)
                transposes(om[:, s, :], bank[5:7], S["oT_made"])

            def rt(t, first=False):
                pe.wait_ge(S["x1T_ready"], t + 1)
                if not first:
                    pe.wait_ge(S["lg_ready"], t)
                for k in range(KD):
                    last = nc.tensor.matmul(bank[4][:, 0:NE], x1T[:, k, :], w_rt[:, k, :],
                                            start=k == 0, stop=k == KD - 1)
                last.then_inc(S["lg_made"], 1)

            def c_step(t, s, ok, n):
                op(t, s, n == 0)
                if ok(-1):
                    x1t(t - 1, 1 - s, n == 1)
                if ok(2):
                    ot(t + 2, s)
                if ok(-2):
                    rt(t - 2, n == 2)

            ot(0, 0, True)
            ot(1, 1)
            for t in range(4):
                c_step(t, t % 2, lambda d, t=t: 0 <= t + d < TILES, t)
            with pe.Fori(0, TILES // 2 - 3) as i:
                for s in range(2):
                    c_step(2 * i + 4 + s, s, lambda d: True, 4)
            for t in range(TILES - 2, TILES):
                c_step(t, t % 2, lambda d, t=t: 0 <= t + d < TILES, t)

            def dxt(src, half, q, n):
                if n >= SHARED_TILES:
                    pe.wait_ge(S["g_ld"], (q - (SHARED_TILES - 1)) * 32)
                else:
                    pe.wait_ge(S["rows_ld"], 16 * (q + 1))
                if n > 0 or half:
                    pe.wait_ge(S["xg_lo"], 2 * q + half)
                else:
                    pe.wait_ge(S["x1T_ready"], TILES - 1)
                if n == 4 and half == 0:
                    pe.wait_ge(S["cum_read"], 1)
                if n == 6 and half == 0:
                    pe.wait_ge(S["table_ready"], 1)
                transposes(src[:, half, :], bank[2:4], S["xgT_made"])

            def dgu(q, s, n):
                pe.wait_ge(S["xg_lo"], 2 * q + 2)
                if n == 0 or n >= SHARED_TILES:
                    pe.wait_ge(S["wg_lo"], KD if n == 0 else (q - (SHARED_TILES - 2)) * KD)
                if n > 0:
                    pe.wait_ge(S["hx_made"], q)
                else:
                    pe.wait_ge(S["res_done"], TILES)
                w_hi, w_lo = (whole(w, 2 * DE) for w in w_gu[1 if n < SHARED_TILES else s])
                x_hi, x_lo = whole(xg_hi, 2 * P), whole(xg_lo, 2 * P)
                for f in range(4):
                    o = bank[f // 2][:, 256 * (f % 2):256 * (f % 2) + 256]
                    for k in range(KD):
                        last = three(o, w_hi[:, k, P * f:P * f + P], w_lo[:, k, P * f:P * f + P],
                                     x_hi[:, k, :], x_lo[:, k, :], k == 0, k == KD - 1)
                last.then_inc(S["gx_made"], 1)

            def ddn(q, s, half, n):
                if half == 0:
                    pe.wait_ge(S["h_lo"], q + 1)
                    if n == 0 or n >= SHARED_TILES:
                        pe.wait_ge(S["wd_lo"], 4 if n == 0 else (q - (SHARED_TILES - 2)) * 4)
                if n > 0:
                    pe.wait_ge(S["y_read0" if half == 0 else "y_read1"], q)
                else:
                    pe.wait_ge(S["lg_ready"], TILES)
                for k in range(2):
                    for c in range(2):
                        a, b = s * 512 + k * 256 + half * P, k * D + 512 * c
                        last = three(bank[4 + 2 * half + c][:], h_hi[:, a:a + P], h_lo[:, a:a + P],
                                     wd_hi[:, b:b + 512], wd_lo[:, b:b + 512], k == 0, k == 1)
                last.then_inc(S["dx_made"], 1)

            def d_step(q, s, n, last=False):
                dgu(q, s, n)
                if n == 0:
                    x1t(TILES - 1, 1, banks=bank[5:7])
                    rt(TILES - 1)
                src = slab if n + 1 < SHARED_TILES else xg
                if not last:
                    dxt(src, 0, q + 1, n + 1)
                if n > 0:
                    ddn(q - 1, 1 - s, 0, n - 1)
                if not last:
                    dxt(src, 1, q + 1, n + 1)
                if n > 0:
                    ddn(q - 1, 1 - s, 1, n - 1)

            dxt(slab, 0, 0, 0)
            dxt(slab, 1, 0, 0)
            rt(TILES - 2)
            for q in range(SHARED_TILES + 3):
                d_step(q, q % 2, q)
                if q == 2:
                    pe.wait_ge(S["cum_need"], 1)
                    pe.wait_ge(S["xg_lo"], 2 * q + 4)
                    cum = bank[2]
                    nc.tensor.matmul(cum[:, 0:(TILES + 1) * NE], tri, msk.rearrange("p t e -> p (t e)"),
                                     start=True, stop=False)
                    for t in range(TILES):
                        rest = TILES - t
                        last = nc.tensor.matmul(cum[:, (t + 1) * NE:(TILES + 1) * NE], ones,
                                                msk[:, t:t + 1, :].to_broadcast([P, rest, NE]),
                                                start=False, stop=t == TILES - 1)
                    last.then_inc(S["cum_made"], 1)
                if q == 4:
                    pe.wait_ge(S["id_need"], 1)
                    pe.wait_ge(S["xg_lo"], 2 * q + 4)
                    for c in range(2 * TILES):
                        last = nc.tensor.matmul(bank[2][:, 0:2 * COLS], oneA[:, c, :],
                                                oneB[:, c].rearrange("p a b -> p (a b)"),
                                                start=c == 0, stop=c == 2 * TILES - 1)
                    last.then_inc(S["idm_made"], 1)
            more = pe.value_load(more_i[0:1, 0:1], min_val=MIN_PAIRS - 2, max_val=SLOT_TILES // 2 - 2)
            with pe.Fori(0, more) as i:
                d_step(2 * i + (SHARED_TILES + 3), 1, SHARED_TILES + 3)
                d_step(2 * i + (SHARED_TILES + 4), 0, SHARED_TILES + 4)
            end = more * 2 + (SHARED_TILES + 3)
            d_step(end, 1, SHARED_TILES + 5, last=True)
            ddn(end, 1, 0, SHARED_TILES + 5)
            ddn(end, 1, 1, SHARED_TILES + 5)

        @block.scalar
        def _(act):
            def copy(o, i):
                return nc.scalar.activation(o, i, ACT.Copy)

            def two_banks(dst, banks, sem):
                copy(dst[:, 0:4, :], banks[0][:].rearrange("p (k c) -> p k c", c=P))
                copy(dst[:, 4:8, :], banks[1][:].rearrange("p (k c) -> p k c", c=P)).then_inc(sem, 1)

            vb_st = (S["vb_st0"], S["vb_st1"])
            for n, c in (("vb_st0", 16), ("vb_st1", 16), ("oA_st", 16), ("o1_st", 16), ("o2_st", 48),
                         ("y_st0", 16), ("y_st1", 16)):
                act.sem_inc(S[n], c)

            def xt(t, s, first=False):
                act.wait_ge(S["xt_made"], t + 1)
                if not first:
                    act.wait_ge(S["xT_ready"], t)
                two_banks(xts[:, s], bank[2 * s:2 * s + 2], S["xts_ready"])

            def vproj(t, s, n):
                act.wait_ge(S["v_made"], t + 1)
                act.wait_ge(vb_st[s], n * 16 + 16)
                copy(vst[:, s, :], bank[4 + s][:])
                copy(Va[:, t, :], bank[6 + s][:, 0:P]).then_inc(S["v_ready"], 1)

            xt(0, 0, True)
            with act.Fori(0, TILES // 2 - 1) as i:
                xt(2 * i + 1, 1)
                vproj(2 * i, 0, i)
                xt(2 * i + 2, 0)
                vproj(2 * i + 1, 1, i)
            xt(TILES - 1, 1)
            vproj(TILES - 2, 0, TILES // 2 - 1)
            vproj(TILES - 1, 1, TILES // 2 - 1)

            def proj(dst, g, n, count):
                act.wait_ge(S["proj_made"], count)
                copy(dst[:, 512 * g:512 * g + 512], pslot(n)[:]).then_inc(S["proj_ready"], 1)

            for n in range(6):
                proj(KA if n < 3 else QA, n % 3, n, n + 1)

            def exps(u, i):
                kind, half, tile, q, k, n, tab, v = kinds[u]
                act.wait_ge(S["biased"], i * UNITS + u + 1)
                nc.scalar.activation(prob[:, u % 2, 0:n], prob[:, u % 2, 0:n], ACT.Exp, scale=-1.0,
                                     bias=ost[kind][:, tile, half, HD:HD + 1],
                                     accum_out=ost[kind][:, tile, half, HD + 1:HD + 2])\
                  .then_inc(S["exp_done"], 1)

            def results(q, i):
                kind, half, tile = kinds[4 * q][0:3]
                act.wait_ge(S["pv_made"], i * 18 + q + 1)
                copy(ost[kind][:, tile:tile + 4, half, 0:HD],
                     bank[4 + q % 2][:, 0:4 * HD].rearrange("p (t e) -> p t e", e=HD)).then_inc(S["o_ready"], 1)

            def pair(i, last):
                for g in range(UNITS):
                    for n in range(9):
                        if GROUP_END[n] == g - 1 and (n < 6 or not last):
                            proj((QB, KB, QA)[n // 3], n % 3, n, i * 9 + n + 7)
                    if g + 2 < UNITS:
                        exps(g + 2, i)
                    elif not last:
                        exps(g + 2 - UNITS, i + 1)
                    if g % 4 == 3:
                        results(g // 4, i)

            exps(0, 0)
            exps(1, 0)
            with act.Fori(0, PAIRS - 1) as i:
                pair(i, False)
            pair(PAIRS - 1, True)

            act.wait_ge(S["o_ready"], 18 * PAIRS)
            act.wait_ge(S["oA_st"], 16 * PAIRS + 16)
            act.wait_ge(S["o1_st"], 16 * PAIRS + 16)
            act.wait_ge(S["o2_st"], 48 * PAIRS + 48)
            act.wait_ge(S["wo_loaded"], 96)
            def wo_high(ks):
                for k in ks:
                    for c in range(2):
                        nc.scalar.activation(wo_hi[:, k * D + 512 * c:k * D + 512 * c + 512],
                                             raw_o[:, k, 512 * c:512 * c + 512], ACT.Copy,
                                             scale=gains[:, k:k + 1]).then_inc(S["wo_hi"], 1)

            def merge_exp(t):
                act.wait_ge(S["merge_need"], t + 1)
                nc.scalar.activation(mD, mD, ACT.Exp).then_inc(S["merge_exp"], 1)

            def norm(t, s):
                act.wait_ge(S["merged"], t + 1)
                for h in range(2):
                    last = nc.scalar.activation(bank[7][:], om[:, s, 512 * h:512 * h + 512], ACT.Square,
                                                scale=512 ** -0.5, accum_out=ssq[:, s, h:h + 1])
                    if h == 0:
                        act.drain()
                last.then_inc(S["squares"], 1)
                act.wait_ge(S["rms_rstd"], t + 1)
                for h in range(2):
                    last = nc.scalar.activation(om[:, s, 512 * h:512 * h + 512], om[:, s, 512 * h:512 * h + 512],
                                                ACT.Copy, scale=rms[:, s, h:h + 1])
                last.then_inc(S["om_ready"], 1)

            def high(dst, at, step, banks, sem):
                view = dst[:].rearrange("p (k c) -> p k c", c=step)[:, at // step:at // step + KD,
                                                                  at % step:at % step + P]
                copy(view[:, 0:4, :], banks[0][:].rearrange("p (k c) -> p k c", c=P))
                copy(view[:, 4:8, :], banks[1][:].rearrange("p (k c) -> p k c", c=P)).then_inc(sem, 1)

            def oT_high(t, s):
                act.wait_ge(S["oT_made"], t + 1)
                high(oT_hi, s * D, P, bank[5:7], S["oT_hi"])

            def lg(t):
                act.wait_ge(S["lg_made"], t + 1)
                copy(logits[:, t, :], bank[4][:, 0:NE]).then_inc(S["lg_ready"], 1)

            def x1t(t, banks=bank[2:4]):
                act.wait_ge(S["x1T_made"], t + 1)
                two_banks(x1T, banks, S["x1T_ready"])

            def store_x1(t, s):
                act.wait_ge(S["x1_ready"], t + 1)
                act.dma_start(x1_t[t], x1s[:, s, :]).then_inc(S["x1_st1" if s else "x1_st0"], 16)

            def c_step(t, s, ok):
                if ok(1):
                    oT_high(t + 1, 1 - s)
                if ok(-3):
                    lg(t - 3)
                if ok(-2):
                    x1t(t - 2)
                if ok(2):
                    merge_exp(t + 2)
                if ok(-1) and ok(0):
                    store_x1(t - 1, 1 - s)
                if ok(2):
                    norm(t + 2, s)

            def gu_high(n_k, k, w):
                nc.scalar.activation(w[0][:, bass.ds(k * 512, 512)], raw_gu.rearrange("p k f -> p (k f)")
                                     [:, bass.ds(k * 512, 512)], ACT.Copy).then_inc(S["wg_hi"], 1)

            x1_t = x1_d.rearrange("(t p) d -> t p d", p=P)
            wo_high(range(0, 4))
            merge_exp(0)
            wo_high(range(4, KD))
            norm(0, 0)
            merge_exp(1)
            norm(1, 1)
            oT_high(0, 0)
            for t in range(2):
                c_step(t, t % 2, lambda d, t=t: 0 <= t + d < TILES)
            act.wait_ge(S["wg_ld"], 32)
            act.wait_ge(S["y_zeroed"], 16)
            for t in range(2, 4):
                c_step(t, t % 2, lambda d, t=t: 0 <= t + d < TILES)
                gu_high(0, t - 2, gu1)
            with act.Fori(0, TILES // 2 - 3) as i:
                for s in range(2):
                    c_step(2 * i + 4 + s, s, lambda d: True)
                    gu_high(0, 2 * i + 2 + s, gu1)
            for t in range(TILES - 2, TILES + 1):
                c_step(t, t % 2, lambda d, t=t: 0 <= t + d < TILES)

            y_t = y_d.rearrange("(t p) d -> t p d", p=P)

            def xg_high(q, half):
                act.wait_ge(S["xgT_made"], 2 * q + half + 1)
                high(xg_hi, half * P, 2 * P, bank[2:4], S["xg_hi"])

            def gu_split(q, s, n):
                act.wait_ge(S["wg_ld"], (q - 4) * 32)
                if n == SHARED_TILES:
                    act.wait_ge(S["idm_made"], 1)
                    act.wait_ge(S["table_ready"], 1)
                act.wait_ge(S["gx_made"], q - 1)
                for k in range(KD):
                    gu_high(0, k, w_gu[s])

            def dn_split(q, n):
                if n == 0:
                    act.wait_ge(S["wd_ld"], 16)
                    act.wait_ge(S["op_made"], TILES)
                else:
                    act.wait_ge(S["wd_ld"], (q - 4) * 16)
                    act.wait_ge(S["dx_made"], 2 * q)
                flat = raw_d.rearrange("p k n -> p (k n)")
                for c in range(4):
                    copy(wd_hi[:, 512 * c:512 * c + 512], flat[:, 512 * c:512 * c + 512]).then_inc(S["wd_hi"], 1)

            def y_rows(q, half, n):
                act.wait_ge(S["dx_made"], 2 * q + half + 1)
                if half == 0:
                    act.wait_ge(S["gcol_ready"], q - (SHARED_TILES - 1))
                act.wait_ge(S["y_st0" if half == 0 else "y_st1"], (q - (SHARED_TILES - 1)) * 16)
                for c in range(2):
                    last = nc.scalar.activation(slab[:, half, 512 * c:512 * c + 512], bank[4 + 2 * half + c][:],
                                                ACT.Copy, scale=gcol[:, half:half + 1])
                last.then_inc(S["y_read0" if half == 0 else "y_read1"], 1)
                act.wait_ge(S["y_read0" if half == 0 else "y_read1"], q + 1)
                act.dma_start(y_t[2 * q + (half - 2 * SHARED_TILES)], slab[:, half, :])\
                   .then_inc(S["y_st0" if half == 0 else "y_st1"], 16)

            def base_set(q):
                for h in range(2):
                    nc.scalar.activation(base[:, 2 * q + h, :], slab[:, h, :], ACT.Copy, scale=ALPHA)\
                      .then_inc(S["base_set"], 1)

            def d_step(q, s, n, last=False):
                if n - 2 >= SHARED_TILES:
                    y_rows(q - 2, 1, n - 2)
                if n - 1 >= SHARED_TILES:
                    dn_split(q - 1, n - 1)
                if n + 1 >= SHARED_TILES and not last:
                    gu_split(q + 1, 1 - s, n + 1)
                if n == 0:
                    dn_split(0, 0)
                if n == 1:
                    for h in range(2):
                        act.wait_ge(S[f"x1_st{h}"], 16 * (TILES // 2))
                if n < SHARED_TILES:
                    act.wait_ge(S["rows_ld"], 16 * (q + 1))
                    base_set(q)
                act.wait_ge(S["gx_made"], q + 1)
                nc.scalar.activation(sg[:, s, :], bank[0][:], ACT.Silu).then_inc(S["sg_ready"], 1)
                if n == 0:
                    x1t(TILES - 1, banks=bank[5:7])
                    lg(TILES - 1)
                if not last:
                    xg_high(q + 1, 0)
                act.wait_ge(S["hx_made"], q + 1)
                copy(h_hi[:, s * 512:s * 512 + 512], hx[:, s, :]).then_inc(S["h_hi"], 1)
                if n - 1 >= SHARED_TILES:
                    y_rows(q - 1, 0, n - 1)
                if not last:
                    xg_high(q + 1, 1)
                if n == 0:
                    act.wait_ge(S["lg_ready"], TILES)
                    nc.scalar.activation(score.rearrange("p t e -> p (t e)"), logits.rearrange("p t e -> p (t e)"),
                                         ACT.Exp, scale=-1.0).then_inc(S["lgexp_done"], 1)

            xg_high(0, 0)
            xg_high(0, 1)
            lg(TILES - 2)
            store_x1(TILES - 1, 1)
            for q in range(SHARED_TILES + 3):
                d_step(q, q % 2, q)
            act.wait_ge(S["table_ready"], 1)
            more = act.value_load(more_i[0:1, 0:1], min_val=MIN_PAIRS - 2, max_val=SLOT_TILES // 2 - 2)
            with act.Fori(0, more) as i:
                d_step(2 * i + (SHARED_TILES + 3), 1, SHARED_TILES + 3)
                d_step(2 * i + (SHARED_TILES + 4), 0, SHARED_TILES + 4)
            end = more * 2 + (SHARED_TILES + 3)
            d_step(end, 1, SHARED_TILES + 5, last=True)
            y_rows(end - 1, 1, SHARED_TILES + 4)
            dn_split(end, SHARED_TILES + 5)
            y_rows(end, 0, SHARED_TILES + 5)
            y_rows(end, 1, SHARED_TILES + 5)
            for half in range(2):
                act.wait_ge(S["y_st0" if half == 0 else "y_st1"], more * 32 + 80)
            act.sem_inc(S["y_all"], 1)

        @block.vector
        def _(dve):
            V = nc.vector

            V.memset(zeros, 0.0)
            V.memset(ones, 1.0)
            V.memset(eps_ln, LN_EPS)
            V.memset(eps_rms, RMS_EPS)
            V.memset(minus_half, -0.5).then_inc(S["ones_ready"], 1)

            def bias(u, i):
                kind, half, tile, q, k, n, tab, v = kinds[u]
                if u % 24 == 0:
                    dve.wait_ge(S[("ta_loaded", "t1_loaded", "t2_loaded")[kind]], i * 16 + 16)
                    first = (16, 16, 48)[kind]
                    dve.wait_ge(S[("oA_st", "o1_st", "o2_st")[kind]], i * first + first)
                dve.wait_ge(S["qk_made"], i * UNITS + u + 1)
                dve.sem_inc(S["units_begun"], 1)
                V.tensor_tensor_reduce(out=prob[:, u % 2, 0:n], in0=bank[u % 2][:, 0:n], in1=tab,
                                       scale=-(HD ** -0.5), scalar=BIG, op0=ALU.add, op1=ALU.min,
                                       accum_out=ost[kind][:, tile, half, HD:HD + 1]).then_inc(S["biased"], 1)

            def pT(u, i):
                kind, half, tile, q, k, n, tab, v = kinds[u]
                dve.wait_ge(S["pT_made"], i * UNITS + u + 1)
                if all(r == P for r, _ in v):
                    last = V.tensor_copy(probT[:, u % 2, 0:n], bank[2 + u % 2][:, 0:n])
                else:
                    for c, (r, _) in enumerate(v):
                        last = V.tensor_copy(probT[0:r, u % 2, P * c:P * c + P],
                                             bank[2 + u % 2][0:r, P * c:P * c + P])
                last.then_inc(S["pT_ready"], 1)

            def pair(i, last):
                for g in range(UNITS):
                    if g + 2 < UNITS:
                        bias(g + 2, i)
                    elif not last:
                        bias(g + 2 - UNITS, i + 1)
                    if g + 1 < UNITS:
                        pT(g + 1, i)
                    elif not last:
                        pT(0, i + 1)

            bias(0, 0)
            bias(1, 0)
            pT(0, 0)
            with dve.Fori(0, PAIRS - 1) as i:
                pair(i, False)
            pair(PAIRS - 1, True)

            dve.wait_ge(S["wr_loaded"], 96)
            dve.wait_ge(S["o_ready"], 18 * PAIRS)
            dve.wait_ge(S["oA_st"], 16 * PAIRS + 16)
            dve.wait_ge(S["o1_st"], 16 * PAIRS + 16)
            dve.wait_ge(S["o2_st"], 48 * PAIRS + 48)
            V.tensor_scalar(nsink, nsink, -1.0, None, ALU.mult)
            dve.drain()
            od_ld, xr_ld, x1_st = (S["od_ld0"], S["od_ld1"]), (S["xr_ld0"], S["xr_ld1"]), (S["x1_st0"], S["x1_st1"])

            def wo_low(ks):
                for k in ks:
                    for c in range(2):
                        dve.wait_ge(S["wo_hi"], 2 * k + c + 1)
                        w = slice(k * D + 512 * c, k * D + 512 * c + 512)
                        V.scalar_tensor_tensor(wo_lo[:, w], raw_o[:, k, 512 * c:512 * c + 512],
                                               gains[:, k:k + 1], plain(wo_hi[:, w]), ALU.mult, ALU.subtract)\
                         .then_inc(S["wo_lo"], 1)

            def low(dst, hi, at, step, banks, sem):
                dv, hv = (a[:].rearrange("p (k c) -> p k c", c=step)[:, at // step:at // step + KD,
                                                                   at % step:at % step + P]
                          for a in (dst, hi))
                for c in range(2):
                    last = V.tensor_tensor(dv[:, 4 * c:4 * c + 4, :],
                                           banks[c][:].rearrange("p (k c) -> p k c", c=P),
                                           plain(hv[:, 4 * c:4 * c + 4, :]), ALU.subtract)
                last.then_inc(sem, 1)

            def oT_low(t, s):
                dve.wait_ge(S["oT_hi"], t + 1)
                low(oT_lo, oT_hi, s * D, P, bank[5:7], S["oT_lo"])

            def residual(t, s, n):
                dve.drain()
                dve.wait_ge(S["op_made"], t + 1)
                dve.wait_ge(xr_ld[s], n)
                for c in range(2):
                    last = V.scalar_tensor_tensor(res[:, 512 * c:512 * c + 512], xr[:, s, 512 * c:512 * c + 512],
                                                  ALPHA, bank[c][:], ALU.mult, ALU.add)
                last.then_inc(S["res_done"], 1)

            def ln1_stats(t, s):
                dve.drain()
                for c in range(2):
                    V.bn_stats(bst[:, c, :], res[:, 512 * c:512 * c + 512])
                dve.drain()
                V.bn_aggr(mv[:, s, :], bst.rearrange("p a b -> p (a b)")).then_inc(S["ln_var"], 1)

            def ln1_apply(t, s, n):
                dve.wait_ge(S["ln_rstd"], t + 1)
                if n is not None:
                    dve.wait_ge(x1_st[s], n)
                V.scalar_tensor_tensor(res, res, mv[:, s, 0:1], ln1g, ALU.subtract, ALU.mult)
                dve.drain()
                V.scalar_tensor_tensor(x1s[:, s, :], res, rstd[:, s, :], ln1b, ALU.mult, ALU.add)\
                 .then_inc(S["x1_ready"], 1)

            def heads(s):
                return odt[:, s, :].rearrange("p (k h e) -> p k h e", k=3, e=OW)

            def merge_max(t, s, n):
                dve.wait_ge(od_ld[s], n)
                nm = heads(s)[:, :, :, HD]
                V.tensor_tensor(mM[:, 0, :], nm[:, 0, :], nsink, ALU.min)
                V.tensor_tensor(mM[:, 1, :], nm[:, 1, :], nm[:, 2, :], ALU.min)
                dve.drain()
                V.tensor_tensor(mD[:, 0:2, :], mM, nm[:, 0:2, :], ALU.subtract)
                V.tensor_tensor(mD[:, 2, :], mM[:, 1, :], nm[:, 2, :], ALU.subtract)
                V.tensor_tensor(mD[:, 3, :], mM[:, 0, :], nsink, ALU.subtract).then_inc(S["merge_need"], 1)

            def merge_factors(t, s):
                dve.wait_ge(S["merge_exp"], t + 1)
                V.tensor_tensor(mL, mD[:, 0:3, :], heads(s)[:, :, :, HD + 1], ALU.mult)
                dve.drain()
                V.tensor_tensor(mR[:, 0, :], mL[:, 0, :], mD[:, 3, :], ALU.add)
                V.tensor_tensor(mR[:, 1, :], mL[:, 1, :], mL[:, 2, :], ALU.add)
                dve.drain()
                V.reciprocal(mR, mR)
                dve.drain()
                V.tensor_tensor(mW[:, 0:2, :], mD[:, 0:2, :], mR, ALU.mult)
                V.tensor_tensor(mW[:, 2, :], mD[:, 2, :], mR[:, 1, :], ALU.mult)
                dve.drain()

            def merge_rows(t, s):
                o2 = junk2.rearrange("p (h e) -> p h e", e=HD)
                V.tensor_tensor(om[:, s, 512:1024].rearrange("p (h e) -> p h e", e=HD), heads(s)[:, 1, :, 0:HD],
                                mW[:, 1, :].unsqueeze(2).to_broadcast([P, 8, HD]), ALU.mult)
                V.tensor_tensor(o2, heads(s)[:, 2, :, 0:HD],
                                mW[:, 2, :].unsqueeze(2).to_broadcast([P, 8, HD]), ALU.mult)
                V.tensor_tensor(om[:, s, 0:512].rearrange("p (h e) -> p h e", e=HD), heads(s)[:, 0, :, 0:HD],
                                mW[:, 0, :].unsqueeze(2).to_broadcast([P, 8, HD]), ALU.mult)
                dve.drain()
                V.tensor_tensor(om[:, s, 512:1024], om[:, s, 512:1024], junk2, ALU.add).then_inc(S["merged"], 1)

            def c_step(t, s, m, ok):
                if ok(-1):
                    residual(t - 1, 1 - s, (m + s) * 16)
                if ok(1):
                    oT_low(t + 1, 1 - s)
                if ok(2):
                    merge_max(t + 2, s, m * 16 + 32)
                if ok(-1):
                    ln1_stats(t - 1, 1 - s)
                if ok(2):
                    merge_factors(t + 2, s)
                if ok(-1):
                    ln1_apply(t - 1, 1 - s, None if isinstance(t, int) and t < 3 else (m + s - 1) * 16)
                if ok(2):
                    merge_rows(t + 2, s)

            wo_low(range(0, 4))
            for t in range(2):
                merge_max(t, t, 16)
                merge_factors(t, t)
                merge_rows(t, t)
                if t == 0:
                    wo_low(range(4, KD))
            oT_low(0, 0)
            for t in range(4):
                c_step(t, t % 2, t // 2, lambda d, t=t: 0 <= t + d < TILES)
            with dve.Fori(0, TILES // 2 - 3) as i:
                for s in range(2):
                    c_step(2 * i + 4 + s, s, i + 2, lambda d: True)
            for t in range(TILES - 2, TILES):
                c_step(t, t % 2, t // 2, lambda d, t=t: 0 <= t + d < TILES)

            def xg_low(q, half):
                dve.wait_ge(S["xg_hi"], 2 * q + half + 1)
                low(xg_lo, xg_hi, half * P, 2 * P, bank[2:4], S["xg_lo"])

            def gu_split(q, s, n):
                flat = raw_gu.rearrange("p k f -> p (k f)")
                w_hi, w_lo = w_gu[s]
                for k in range(KD):
                    w = slice(512 * k, 512 * k + 512)
                    dve.wait_ge(S["wg_hi"], (q - 5) * KD + (k + 1))
                    V.tensor_tensor(w_lo[:, w], flat[:, w], plain(w_hi[:, w]), ALU.subtract)\
                     .then_inc(S["wg_lo"], 1)

            def dn_split(q, n):
                flat = raw_d.rearrange("p k n -> p (k n)")
                for c in range(4):
                    w = slice(512 * c, 512 * c + 512)
                    dve.wait_ge(S["wd_hi"], c + 1 if n == 0 else (q - 5) * 4 + (c + 1))
                    V.tensor_tensor(wd_lo[:, w], flat[:, w], plain(wd_hi[:, w]), ALU.subtract)\
                     .then_inc(S["wd_lo"], 1)

            def add_shared(q, half):
                dve.wait_ge(S["dx_made"], 2 * q + half + 1)
                dve.wait_ge(S["base_set"], 2 * q + half + 1)
                for c in range(2):
                    b = base[:, 2 * q + half, 512 * c:512 * c + 512]
                    last = V.tensor_tensor(b, b, bank[4 + 2 * half + c][:], ALU.add)
                last.then_inc(S["y_read0" if half == 0 else "y_read1"], 1)

            def d_step(q, s, n, last=False):
                if 0 <= n - 2 < SHARED_TILES:
                    add_shared(q - 2, 1)
                if n - 1 >= SHARED_TILES:
                    dn_split(q - 1, n - 1)
                if n + 1 >= SHARED_TILES and not last:
                    gu_split(q + 1, 1 - s, n + 1)
                if n == 0:
                    dn_split(0, 0)
                if n < len(routing):
                    routing[n]()
                dve.wait_ge(S["sg_ready"], q + 1)
                V.tensor_tensor(hx[:, s, :], sg[:, s, :], bank[1][:], ALU.mult).then_inc(S["hx_made"], 1)
                if not last:
                    xg_low(q + 1, 0)
                dve.wait_ge(S["h_hi"], q + 1)
                V.tensor_tensor(h_lo[:, s * 512:s * 512 + 512], hx[:, s, :],
                                plain(h_hi[:, s * 512:s * 512 + 512]), ALU.subtract).then_inc(S["h_lo"], 1)
                if 0 <= n - 1 < SHARED_TILES:
                    add_shared(q - 1, 0)
                if not last:
                    xg_low(q + 1, 1)

            def ranks(val, tmp, rk, start):
                n = val.shape[1] * val.shape[2] // 4
                v4, c4, r4_ = (a.rearrange("p t e -> p (t e)").rearrange("p (n f) -> p n f", f=4)
                               for a in (val, tmp, rk))
                V.tensor_copy(r4_, start.unsqueeze(1).to_broadcast([P, n, 4]))
                for d in range(1, 4):
                    dve.drain()
                    V.tensor_tensor(c4[:, :, 0:4 - d], v4[:, :, 0:4 - d], v4[:, :, d:4], ALU.is_ge)
                    dve.drain()
                    V.tensor_tensor(r4_[:, :, d:4], r4_[:, :, d:4], c4[:, :, 0:4 - d], ALU.add)
                    dve.drain()
                    V.tensor_tensor(r4_[:, :, 0:4 - d], r4_[:, :, 0:4 - d], c4[:, :, 0:4 - d], ALU.subtract)
                dve.drain()

            def flat(a):
                return a.rearrange("p t e -> p (t e)")

            def route_scores():
                V.memset(msk[:, TILES, :], 0.0)
                dve.wait_ge(S["lgexp_done"], 1)
                V.tensor_scalar(flat(score), flat(score), 1.0, None, ALU.add)
                dve.drain()
                V.reciprocal(flat(score), flat(score))
                dve.drain()
                V.tensor_tensor(bia, score, rbias.unsqueeze(1).to_broadcast([P, TILES, NE]), ALU.add)
                dve.drain()
                ranks(bia, cmp_, rank, rank0)

            def route_groups():
                V.tensor_scalar(flat(rank), flat(rank), 1.5, None, ALU.is_lt)
                dve.drain()
                V.tensor_tensor(flat(cmp_), flat(rank), flat(bia), ALU.mult)
                dve.drain()
                V.tensor_reduce(flat(gsc), flat(cmp_).rearrange("p (n f) -> p n f", f=4), AX.X, ALU.add)
                dve.drain()
                ranks(gsc, gcmp, grank, rank0)
                V.scalar_tensor_tensor(flat(msk[:, 0:TILES, :]).rearrange("p (n f) -> p n f", f=4),
                                       flat(grank).unsqueeze(2).to_broadcast([P, TILES * NGRP, 4]), 0.5,
                                       flat(rank).rearrange("p (n f) -> p n f", f=4),
                                       ALU.is_lt, ALU.mult).then_inc(S["cum_need"], 1)
                dve.drain()
                V.tensor_tensor(flat(msc), flat(msk[:, 0:TILES, :]), flat(score), ALU.mult)
                dve.drain()
                V.tensor_reduce(den, msc, AX.X, ALU.add)
                dve.drain()
                V.reciprocal(den, den)

            def route_slots():
                dve.wait_ge(S["cum_made"], 1)
                V.tensor_scalar(ntil_i[:], bank[2][:, TILES * NE:(TILES + 1) * NE], float(ST - 1), None, ALU.add)
                V.tensor_copy(slot, bank[2][:, 0:TILES * NE].rearrange("p (t e) -> p t e", e=NE))\
                 .then_inc(S["cum_read"], 1)
                dve.drain()
                V.tensor_scalar(ntil_i[:], ntil_i[:], ST.bit_length() - 1, None, ALU.arith_shift_right)
                dve.drain()
                V.tensor_copy(ntil, ntil_i[:])
                dve.drain()
                V.tensor_tensor_scan(tend, ones[:, 0:NE], ntil, 0.0, ALU.mult, ALU.add)
                dve.drain()
                V.tensor_tensor(ntil, tend, ntil, ALU.subtract)
                V.tensor_tensor(cmpj, iota_j[:, 0:SLOT_TILES].unsqueeze(2).to_broadcast([P, SLOT_TILES, NE]),
                                tend.unsqueeze(1).to_broadcast([P, SLOT_TILES, NE]), ALU.is_ge)
                V.tensor_scalar(more_i[:, 0:1], tend[:, NE - 1:NE], -3.0, None, ALU.add)
                dve.drain()
                V.tensor_reduce(ej, cmpj, AX.X, ALU.add)
                V.tensor_scalar(ntil, ntil, float(ST), None, ALU.mult)
                V.tensor_scalar(more_i[:, 0:1], more_i[:, 0:1], 1, None, ALU.arith_shift_right)
                dve.drain()
                V.tensor_scalar(ej_i[:], ej, float(NE - 1), None, ALU.min).then_inc(S["ej_ready"], 1)
                V.tensor_tensor(slot, slot, ntil.unsqueeze(1).to_broadcast([P, TILES, NE]), ALU.add)
                dve.drain()
                V.tensor_tensor(flat(slot), flat(slot), flat(msk[:, 0:TILES, :]), ALU.mult)
                dve.drain()
                V.tensor_reduce(two[:, :, 1], slot, AX.X, ALU.max)
                V.tensor_reduce(two[:, :, 0], slot, AX.X, ALU.add)
                dve.drain()
                V.tensor_tensor(two[:, :, 0], two[:, :, 0], two[:, :, 1], ALU.subtract)
                V.tensor_tensor(cmp_, slot, two[:, :, 1:2].to_broadcast([P, TILES, NE]), ALU.is_equal)
                dve.drain()
                V.tensor_copy(two_i[:], two)
                V.tensor_tensor(flat(cmp_), flat(cmp_), flat(msc), ALU.mult)
                dve.drain()
                V.tensor_reduce(gate[:, :, 1], cmp_, AX.X, ALU.add)
                V.tensor_tensor(flat(msc), flat(msc), flat(cmp_), ALU.subtract)
                V.tensor_scalar(rq_i[:, 0, :], flat(two_i[:]), P - 1, None, ALU.bitwise_and)
                V.tensor_scalar(rq_i[:, 1, :], flat(two_i[:]), 7, None, ALU.arith_shift_right)
                dve.drain()
                V.tensor_reduce(gate[:, :, 0], msc, AX.X, ALU.add)
                V.tensor_copy(flat(rq), flat(rq_i[:]))
                dve.drain()
                V.tensor_tensor(gate, gate, den.unsqueeze(2).to_broadcast([P, TILES, 2]), ALU.mult)

            def route_tables():
                V.tensor_tensor(oneA, rq[:, 0, :].unsqueeze(2).to_broadcast([P, 2 * TILES, P]),
                                iota_p.unsqueeze(1).to_broadcast([P, 2 * TILES, P]), ALU.is_equal)
                V.tensor_tensor(oneB[:, :, 0, :], rq[:, 1, :].unsqueeze(2).to_broadcast([P, 2 * TILES, COLS]),
                                iota_j.unsqueeze(1).to_broadcast([P, 2 * TILES, COLS]), ALU.is_equal)
                dve.drain()
                V.tensor_tensor(oneB[:, :, 1, :], oneB[:, :, 0, :],
                                flat(gate).unsqueeze(2).to_broadcast([P, 2 * TILES, COLS]), ALU.mult)
                dve.drain()
                for h in range(2):
                    last = V.tensor_tensor(oneB[:, h::2, 0, :], oneB[:, h::2, 0, :],
                                           token_id.unsqueeze(2).to_broadcast([P, TILES, COLS]), ALU.mult)
                last.then_inc(S["id_need"], 1)

            def route_done():
                dve.wait_ge(S["idm_made"], 1)
                V.tensor_copy(gtab, bank[2][:, COLS:2 * COLS])
                V.tensor_copy(idtab[:], bank[2][:, 0:COLS]).then_inc(S["table_ready"], 1)

            routing = [lambda: None, route_scores, route_groups, route_slots, route_tables]
            residual(TILES - 1, 1, 16 * (TILES // 2))
            ln1_stats(TILES - 1, 1)
            xg_low(0, 0)
            xg_low(0, 1)
            ln1_apply(TILES - 1, 1, 16 * (TILES // 2 - 1))
            for q in range(SHARED_TILES + 3):
                if q == SHARED_TILES - 1:
                    route_done()
                d_step(q, q % 2, q)
            more = dve.value_load(more_i[0:1, 0:1], min_val=MIN_PAIRS - 2, max_val=SLOT_TILES // 2 - 2)
            with dve.Fori(0, more) as i:
                d_step(2 * i + (SHARED_TILES + 3), 1, SHARED_TILES + 3)
                d_step(2 * i + (SHARED_TILES + 4), 0, SHARED_TILES + 4)
            end = more * 2 + (SHARED_TILES + 3)
            d_step(end, 1, SHARED_TILES + 5, last=True)
            dn_split(end, SHARED_TILES + 5)

            dve.wait_ge(S["ln2_loaded"], 32)
            out_st = (S["out_st0"], S["out_st1"])

            def z_stats(t, s):
                dve.wait_ge(S[f"e_add{t}"], 32)
                for c in range(2):
                    V.bn_stats(bst2[:, s, c, :], base[:, t, 512 * c:512 * c + 512])
                dve.drain()
                V.bn_aggr(mv2[:, s, :], bst2[:, s].rearrange("p a b -> p (a b)")).then_inc(S["z_var"], 1)

            def z_out(t, s):
                dve.wait_ge(S["z_rstd"], t + 1)
                if t > 1:
                    dve.wait_ge(out_st[s], t // 2 * 16)
                dve.drain()
                V.scalar_tensor_tensor(zb, base[:, t, :], mv2[:, s, 0:1], ln2g, ALU.subtract, ALU.mult)
                dve.drain()
                V.scalar_tensor_tensor(ob[:, s, :], zb, rstd2[:, s, :], ln2b, ALU.mult, ALU.add)\
                 .then_inc(S["fin_ready"], 1)

            z_stats(0, 0)
            for t in range(TILES):
                if t + 1 < TILES:
                    z_stats(t + 1, (t + 1) % 2)
                z_out(t, t % 2)

        @block.gpsimd
        def _(pool):
            G = nc.gpsimd

            with pool.Fori(0, TILES // 2) as i:
                for s in range(2):
                    t = 2 * i + s
                    pool.wait_ge(S["xts_ready"], t + 1)
                    G.tensor_copy(xT[:, :, bass.ds(t * P, P)], xts[:, s]).then_inc(S["xT_ready"], 1)
            def rsqrt(dst, src, eps):
                G.tensor_tensor(dst, src, eps.to_broadcast([P, dst.shape[1]]), ALU.add)
                pool.drain()
                return G.tensor_tensor(dst, dst, minus_half.to_broadcast([P, dst.shape[1]]), ALU.pow)

            def c_step(t, s, ok, k=None):
                if ok(-1):
                    pool.wait_ge(S["ln_var"], t)
                    rsqrt(rstd[:, 1 - s, :], mv[:, 1 - s, 1:2], eps_ln).then_inc(S["ln_rstd"], 1)
                if ok(2):
                    pool.wait_ge(S["squares"], t + 3)
                    rsqrt(rms[:, s, :], ssq[:, s, :], eps_rms).then_inc(S["rms_rstd"], 1)
                if k is not None:
                    pool.wait_ge(S["wg_hi"], k + 1)
                    w = bass.ds(k * 512, 512)
                    G.tensor_tensor(gu1[1][:, w], raw_gu.rearrange("p k f -> p (k f)")[:, w],
                                    plain(gu1[0][:, w]), ALU.subtract).then_inc(S["wg_lo"], 1)

            for t in range(-2, 4):
                c_step(t, t % 2, lambda d, t=t: 0 <= t + d < TILES, t - 2 if t >= 2 else None)
            with pool.Fori(0, TILES // 2 - 3) as i:
                for s in range(2):
                    c_step(2 * i + 4 + s, s, lambda d: True, 2 * i + 2 + s)
            for t in range(TILES - 2, TILES + 1):
                c_step(t, t % 2, lambda d, t=t: 0 <= t + d < TILES)

            pool.wait_ge(S["table_ready"], 1)
            for h in range(2):
                pool.wait_ge(S[f"x1_st{h}"], 16 * (TILES // 2))

            def gather(q, s):
                pool.wait_ge(S["xgT_made"], q * 2)
                G.tensor_copy(idc[:], idtab[:, bass.ds((q - SHARED_TILES) * 2, 2)]).then_inc(S["ids_col"], 1)
                pool.wait_ge(S["ids_col"], q - (SHARED_TILES - 1))
                pool.sem_inc(S["gathers_begun"], 1)
                for h in range(2):
                    G.indirect_dma_start(out=xg[:, h, :], out_offset=None, in_=x1_d,
                                         in_offset=bass.IndirectOffsetOnAxis(ap=idc[:, h:h + 1].bitcast(U32),
                                                                             axis=0)).then_inc(S["g_ld"], 16)

            def weights(q):
                pool.wait_ge(S["y_read1"], q)
                G.tensor_copy(gcol, gtab[:, bass.ds((q - SHARED_TILES) * 2, 2)]).then_inc(S["gcol_ready"], 1)

            gather(SHARED_TILES, 0)
            gather(SHARED_TILES + 1, 1)
            more = pool.value_load(more_i[0:1, 0:1], min_val=MIN_PAIRS - 2, max_val=SLOT_TILES // 2 - 2)
            with pool.Fori(0, more * 2 + 2) as i:
                weights(i + SHARED_TILES)
                gather(i + (SHARED_TILES + 2), None)
            end = more * 2 + (SHARED_TILES + 3)
            weights(end - 1)
            weights(end)

            pool.wait_ge(S["y_all"], 1)

            def add_rows(t, c):
                if c:
                    pool.wait_ge(S[f"e_add{t}"], 16)
                G.indirect_dma_start(out=base[:, t, :], out_offset=None, in_=y_d,
                                     in_offset=bass.IndirectOffsetOnAxis(ap=two_i[:, t, c:c + 1].bitcast(U32),
                                                                         axis=0),
                                     compute_op=ALU.add).then_inc(S[f"e_add{t}"], 16)

            def z_rsqrt(t, s):
                pool.wait_ge(S["z_var"], t + 1)
                rsqrt(rstd2[:, s, :], mv2[:, s, 1:2], eps_ln).then_inc(S["z_rstd"], 1)

            LAG = 3
            for t in range(TILES + 2 * LAG):
                if t < TILES:
                    add_rows(t, 0)
                if LAG <= t < TILES + LAG:
                    add_rows(t - LAG, 1)
                if t >= 2 * LAG:
                    z_rsqrt(t - 2 * LAG, t % 2)


_WEIGHTS = ["w_in", "sink_a", "norm_a", "norm_b", "w_out", "ln1_g", "ln1_b", "w_router", "router_bias",
            "w_gate", "w_up", "w_down", "ws_gate", "ws_up", "ws_down", "ln2_g", "ln2_b"]
_WHOLE = {"w_router", "router_bias"}


def kernel(**inputs):
    import concourse.bacc as _bacc
    from concourse.bass_utils import run_bass_kernel_spmd as _run

    nc = _bacc.Bacc("TRN2", target_bir_lowering=False, num_devices=1)
    arrays, args = {}, []

    def give(name, a):
        a = np.ascontiguousarray(a)
        arrays[f"in_{name}"] = a
        args.append(nc.dram_tensor(f"in_{name}", a.shape, mybir.dt.from_np(a.dtype), kind="ExternalInput").ap())

    give("x", np.concatenate([np.asarray(inputs["x_prompt"])[0], np.asarray(inputs["x_sample"])[0]], 0))
    for name in _WEIGHTS:
        a = np.asarray(inputs[name])
        give(name, a if name in _WHOLE else a[0])
    for name, a in constants().items():
        give(name, a)
    args.append(nc.dram_tensor("out_y", (TOKENS, D), FP32, kind="ExternalOutput").ap())
    encoder_layer(nc, *args)
    r = _run(nc, [arrays], core_ids=[0])
    y = r.results[0]["out_y"]
    return y[0:512].reshape(1, 512, D), y[512:TOKENS].reshape(1, 1024, D)
```

```python
import numpy as np
import concourse.bass as bass
from concourse import mybir
from contextlib import ExitStack

FP32 = mybir.dt.float32
FP32R = mybir.dt.float32r
I32 = mybir.dt.int32
U32 = mybir.dt.uint32
ALU = mybir.AluOpType
ACT = mybir.ActivationFunctionType
AX = mybir.AxisListType

P = 128
D = 1024
KD = D // P
SEQS = ((0, 512), (512, 1024))
TOKENS = 1536
TILES = TOKENS // P
HD = 64
PAIRS = 4
OW = HD + 2
NE = 16
NGRP = 4
DE = 256
ALPHA = 2.0 ** 0.25
LN_EPS = 1e-5
RMS_EPS = 1e-6
A_RADIUS = 128
B_RADIUS = 64
ST = 256
SHARED_TILES = TOKENS // ST
SLOT_TILES = (2 * TOKENS + NE * (ST - 1)) // ST // 2 * 2 + 2
MIN_PAIRS = 2 * TOKENS // ST // 2
COLS = SLOT_TILES * 2
QA0, KA0, VA0, QB0, KB0, VB0 = 0, 512, 640, 768, 1280, 1792
UNITS = 72
SHORT_UNIT = 48
SPLITS = (8, 24, 46)
ZERO_PARTS = 16
WO_UNIT = 40
BIG = 3.0e38


def constants():
    h = np.arange(1, 17, dtype=np.float32)
    slopes = np.exp2(-8.0 * h / 16).astype(np.float32)
    p = np.arange(P)[:, None]
    hd8 = np.float32(8.0)

    def table(step, ok, slope, mult=None):
        t = -slope * np.abs(step).astype(np.float32)
        if mult is not None:
            t = t + np.log(np.maximum(mult, 1)).astype(np.float32)
        return np.where(ok, hd8 * t, np.float32(-1e37)).astype(np.float32)

    rel_a = np.arange(384)[None, :] - 128 - p
    rel_1 = np.arange(256)[None, :] - 64 - p
    rel_2 = np.arange(384)[None, :] - 128 - p
    mult2 = (np.abs(rel_2) <= B_RADIUS).astype(np.float32) + (rel_2 % 4 == 0)
    tab_a = np.stack([np.stack([table(rel_a, np.abs(rel_a) <= A_RADIUS, slopes[0::2][i + 4 * half])
                                for half in range(2)], 1) for i in range(PAIRS)])
    tab_1 = np.stack([np.stack([table(rel_1, np.abs(rel_1) <= B_RADIUS, slopes[1::2][2 * i + half])
                                for half in range(2)], 1) for i in range(PAIRS)])
    tab_2 = np.stack([np.stack([table(4 * rel_2, mult2 > 0, slopes[1::2][2 * i + half], mult2)
                                for half in range(2)], 1) for i in range(PAIRS)])
    row = np.zeros((P, 512), np.float32)
    row[:, 0:128] = np.eye(P)
    row[:, 128:256] = np.arange(P)[:, None] < np.arange(P)[None, :]
    row[:, 256:384] = np.arange(P)[None, :]
    row[:, 384:384 + COLS] = np.arange(COLS)[None, :]
    row[:, 440:440 + TILES] = np.arange(TILES)[None, :] * P + np.arange(P)[:, None]
    row[:, 452:456] = 3 - np.arange(4)[None, :]
    return {"tab_a": tab_a, "tab_1": tab_1, "tab_2": tab_2, "const": row}


def encoder_layer(nc, x, w_in, sink, norm_a, norm_b, w_out, ln1_g, ln1_b, w_router, router_bias,
                  w_gate, w_up, w_down, ws_gate, ws_up, ws_down, ln2_g, ln2_b,
                  tab_a, tab_1, tab_2, const, out):
    vb_d = nc.dram_tensor("vb_scratch", (TOKENS, 512), FP32, kind="Internal").ap()
    o_d = nc.dram_tensor("o_scratch", (TOKENS, 3 * PAIRS * 2 * OW), FP32, kind="Internal").ap()
    x1_d = nc.dram_tensor("x1_scratch", (TOKENS, D), FP32, kind="Internal").ap()
    y_d = nc.dram_tensor("y_scratch", (SLOT_TILES * ST, D), FP32, kind="Internal").ap()

    ctx = ExitStack()
    with ctx:
        def isb(name, *shape):
            return ctx.enter_context(nc.sbuf_tensor(name, list(shape), I32))

        def cut(tensor):
            at = [0]

            def take(*dims):
                n = int(np.prod(dims))
                v = tensor[:, at[0]:at[0] + n]
                at[0] += n
                assert at[0] <= tensor.shape[1], (tensor.name, at[0])
                if len(dims) == 2:
                    v = v.rearrange("p (a b) -> p a b", b=dims[1])
                if len(dims) == 3:
                    v = v.rearrange("p (a b c) -> p a b c", b=dims[1], c=dims[2])
                return v

            def move(word):
                at[0] = word
            return take, move

        keep = ctx.enter_context(nc.sbuf_tensor("keep", [P, 1088], FP32))
        take, _ = cut(keep)
        cst = take(512)
        ident, tri, iota_p = cst[:, 0:128], cst[:, 128:256], cst[:, 256:384]
        token_id, rank0 = cst[:, 440:440 + TILES], cst[:, 452:456]
        iota_j = cst[:, 384:384 + COLS]
        logits = take(TILES, NE)
        w_rt = take(KD, NE)
        rbias = take(NE)
        nsink = take(8)
        gains = take(KD)
        minus_half = take(1)
        eps_ln = take(1)
        eps_rms = take(1)
        ones = take(P)
        gtab = take(COLS)
        gcol = take(2)
        two_i = isb("two_i", P, TILES, 2)
        rq_i = isb("rq_i", P, 2, TILES * 2)
        idtab = isb("idtab", P, COLS)
        ntil_i = isb("ntil_i", P, NE)
        ej_i = isb("ej_i", P, SLOT_TILES)
        more_i = isb("more_i", P, 2)
        idc = isb("idc", P, 2)

        def split_pair(stack, name, words):
            return [stack.enter_context(nc.sbuf_tensor(name + part, [P, words], FP32R))
                    for part in ("_hi", "_lo")]

        def whole(t, w):
            return t[:].rearrange("p (k c) -> p k c", c=w)

        def plain(a):
            return a.bitcast(FP32)

        RAW = 2 * D + KD * D
        with ExitStack() as phase:
            xT_hi, xT_lo = split_pair(phase, "xT", KD * TOKENS)
            Va_t = phase.enter_context(nc.sbuf_tensor("Va", [P, TILES * P], FP32))
            Va = Va_t[:].rearrange("p (t c) -> p t c", c=P)
            with ExitStack() as part:
                wv_hi, wv_lo = split_pair(part, "w_v", KD * 640)
                xs_hi, xs_lo = split_pair(part, "xs", 2 * D)
                a_work = part.enter_context(nc.sbuf_tensor("a_work", [P, 3 * D + KD * 640], FP32))
                take, _ = cut(a_work)
                xin = take(2, D)
                vst = take(2, 512)
                raw_v = take(KD, 640)
            b_work = phase.enter_context(nc.sbuf_tensor("b_work", [P, 18448], FP32))
            take, _ = cut(b_work)
            V1 = take(14, P)
            ost = [take(TILES, 2, OW)]
            V2 = take(TILES, P)
            ost += [take(TILES, 2, OW) for _ in range(2)]
            QA, KA, QB, KB = (take(TOKENS) for _ in range(4))
            tA = take(2, 384)
            t1 = take(2, 256)
            t2 = take(2, 384)
            prob = take(3, 384)
            probT = take(2, 384)
            zeros = take(256)
            w_qa, w_qb, w_kb = (split_pair(phase, n, D) for n in ("w_qa", "w_qb", "w_kb"))
            raw_w_t = phase.enter_context(nc.sbuf_tensor("raw_w", [P, D], FP32))
            raw_w = raw_w_t[:].rearrange("p (k c) -> p k c", c=P)
        with ExitStack() as phase:
            c_raw = phase.enter_context(nc.sbuf_tensor("c_raw", [P, RAW], FP32))
            take, _ = cut(c_raw)
            ln1g = take(D)
            ln1b = take(D)
            raw_o = take(KD, D)
            wo_hi, wo_lo = split_pair(phase, "w_o", KD * D)
            c_work = phase.enter_context(nc.sbuf_tensor("c_work", [P, 12288], FP32))
            take, _ = cut(c_work)
            x1s = take(2, D)
            res = take(D)
            x1T = take(KD, P)
            odt = take(2, 3 * PAIRS * 2 * OW)
            om = take(2, D)
            xr = take(2, D)
            junk2 = take(512)
            mD = take(4, 8)
            mM = take(2, 8)
            mL = take(3, 8)
            mR = take(2, 8)
            mW = take(3, 8)
            ssq = take(2, 2)
            rms = take(2, 2)
            bst = take(2, 6)
            mv = take(2, 2)
            rstd = take(2, 1)

            oT_hi, oT_lo = split_pair(phase, "oT", 2 * D)
        GU = KD * 2 * DE
        d_work = ctx.enter_context(nc.sbuf_tensor("d_work", [P, RAW + TILES * D], FP32))
        take, _ = cut(d_work)
        sg = take(2, 512)
        hx = take(2, 512)
        raw_gu = take(KD, 2 * DE)
        raw_d = take(2, D)
        slab = take(2, D)
        base = take(TILES, D)
        with ExitStack() as phase:
            r_work = phase.enter_context(nc.sbuf_tensor("r_work", [P, 2 * GU], FP32))
            take, _ = cut(r_work)
            score = take(TILES, NE)
            rank = take(TILES, NE)
            cmp_ = take(TILES, NE)
            bia = take(TILES, NE)
            gsc = take(TILES, NGRP)
            grank = take(TILES, NGRP)
            gcmp = take(TILES, NGRP)
            msk = take(TILES + 1, NE)
            msc = take(TILES, NE)
            slot = take(TILES, NE)
            den = take(TILES)
            two = take(TILES, 2)
            gate = take(TILES, 2)
            tend = take(NE)
            ntil = take(NE)
            cmpj = take(SLOT_TILES, NE)
            ej = take(SLOT_TILES)
            rq = take(2, TILES * 2)
            oneB = take(2 * TILES, 2, COLS)
            oneA = take(2 * TILES, P)
        gu0 = split_pair(ctx, "w_gu0", GU)
        xg_hi, xg_lo = split_pair(ctx, "xgT", KD * 2 * P)
        wd_hi, wd_lo = split_pair(ctx, "w_dn", 2 * D)
        h_hi, h_lo = split_pair(ctx, "hT", 2 * 512)
        xg = ctx.enter_context(nc.sbuf_tensor("xg", [P, 2, D], FP32))
        gu1 = split_pair(ctx, "w_gu1", GU)
        w_gu = (gu0, gu1)
        take, move = cut(d_work)
        ob = take(2, D)
        ln2g = take(D)
        ln2b = take(D)
        zb = take(D)
        zsum = take(TILES)
        minus_mean = take(TILES)
        mean_32 = take(TILES)
        zvar = take(TILES)
        rstd2 = take(TILES)

        bank = [ctx.enter_context(nc.psum_tensor(f"bank{b}", [P, 512], FP32)) for b in range(8)]

        names = """c_loaded x_ld0 x_ld1 xt_made xts_ready
            v_made v_ready vb_st0 vb_st1 proj_made proj_ready ta_loaded t1_loaded t2_loaded
            v1_loaded v2_loaded qk_made biased exp_done pT_made pT_ready pv_made o_ready units_begun
            oA_st o1_st o2_st0 o2_st1 wo_loaded wr_loaded ones_ready y_zeroed
            wv_ld0 wv_ld1 wv_hi wv_made xs_hi wraw_ld wq_hi wq_lo wo_scaled wo_hi wo_lo
            od_ld0 od_ld1 xr_ld0 xr_ld1 x1_st0 x1_st1 op_made res_done oT_made oT_hi oT_lo om_ready
            merge_need merge_exp merged squares rms_rstd ln_var ln_rstd x1_ready x1T_made x1T_ready
            lg_made lg_ready lgexp_done
            rows_ld base_set wg_ld wd_ld wg_hi wg_lo wd_hi wd_lo xgT_made xg_hi xg_lo gx_made sg_ready
            hx_made h_hi h_lo dx_made y_read0 y_read1 y_st0 y_st1 y_all
            cum_need cum_made cum_read ej_ready id_need idm_made table_ready ids_col gathers_begun g_ld
            gcol_ready ln2_loaded z_var z_eps z_rstd fin_ready out_st0 out_st1""".split()
        names += [f"e_add{t}" for t in range(TILES)]
        S = {n: ctx.enter_context(nc.semaphore(n)) for n in names}
        block = ctx.enter_context(nc.Block())

        kinds = []
        for half in range(2):
            hp = slice(HD * half, HD * half + HD)
            for s0, L in SEQS:
                for j in range(L // P):
                    k0, k1 = max(0, P * (j - 1)), min(L, P * (j + 2))
                    off = k0 - P * (j - 1)
                    kinds.append((0, half, s0 // P + j, QA[hp, s0 + P * j:s0 + P * j + P],
                                  KA[hp, s0 + k0:s0 + k1], k1 - k0, tA[:, half, off:off + k1 - k0],
                                  [(P, Va[:, (s0 + k0) // P + c, hp]) for c in range((k1 - k0) // P)]))
        for half in range(2):
            hp = slice(HD * half, HD * half + HD)
            for s0, L in SEQS:
                nb = L // P
                for j in range(nb):
                    k0, k1 = max(0, P * j - B_RADIUS), min(L, P * (j + 1) + B_RADIUS)
                    off = k0 - (P * j - B_RADIUS)
                    vt = 0 if s0 == 0 else 5
                    rows = [(64 if m in (0, nb) else P) for m in (j, j + 1)]
                    kinds.append((1, half, s0 // P + j, QB[hp, s0 + P * j:s0 + P * j + P],
                                  KB[hp, s0 + k0:s0 + k1], k1 - k0, t1[:, half, off:off + k1 - k0],
                                  [(r, V1[0:r, vt + m, hp]) for r, m in zip(rows, (j, j + 1))]))
        for s0, L in SEQS:
            for half in range(2):
                hp = slice(HD * half, HD * half + HD)
                qs = QB[hp, s0:s0 + L].rearrange("c (s r) -> c r s", r=4)
                ks = KB[hp, s0:s0 + L].rearrange("c (s r) -> c r s", r=4)
                nb = L // 512
                for r in range(4):
                    for b in range(nb):
                        off = P * (1 - b)
                        kinds.append((2, half, s0 // P + r * nb + b, qs[:, r, P * b:P * b + P],
                                      ks[:, r, :], L // 4, t2[:, half, off:off + L // 4],
                                      [(P, V2[:, s0 // P + r * nb + c, hp]) for c in range(nb)]))
        assert len(kinds) == UNITS

        def proj_plan():
            plan = {}
            for n in range(48):
                plan.setdefault(n * 20 // 48, []).append((n // 8, n % 8))
            for n in range(24):
                plan.setdefault(24 + n * 42 // 24, []).append((6 + n // 8, n % 8))
            return plan

        PLAN = proj_plan()
        GROUP_END = {g: max(s for s, ms in PLAN.items() if any(m[0] == g for m in ms)) for g in range(9)}

        sbank = (bank[0], bank[1], bank[6])

        def ring(u):
            return u % 2 if u < SHORT_UNIT else (2, 0, 1)[(u - SHORT_UNIT) % 3]

        def ahead(g):
            if g < SHORT_UNIT:
                return [g + 2]
            if g == SHORT_UNIT:
                return [g + 2, g + 3]
            return [g + 3] if g + 3 < UNITS else [g + 2] if g + 2 >= UNITS else []

        def pslot(n):
            return bank[6 + n % 2] if n < 6 else bank[7]

        @block.sync
        def _(sp):
            x_t = x.rearrange("(t p) d -> t p d", p=P)
            out_t = out.rearrange("(t p) d -> t p d", p=P)
            vb_t = vb_d.rearrange("(t p) d -> t p d", p=P)
            od_t = o_d.rearrange("(t p) d -> t p d", p=P)
            w_cols = w_in.rearrange("(k p) c -> p k c", p=P)
            x_ld, vb_st = (S["x_ld0"], S["x_ld1"]), (S["vb_st0"], S["vb_st1"])

            sp.dma_start(xin[:, 0, :], x_t[0]).then_inc(x_ld[0], 16)
            sp.dma_start(cst, const).then_inc(S["c_loaded"], 16)
            for h in range(2):
                sp.dma_start(raw_v[:, 4 * h:4 * h + 4, 0:512], w_cols[:, 4 * h:4 * h + 4, VB0:VB0 + 512])\
                  .then_inc(S[f"wv_ld{h}"], 16)
                sp.dma_start(raw_v[:, 4 * h:4 * h + 4, 512:640], w_cols[:, 4 * h:4 * h + 4, VA0:VA0 + P])\
                  .then_inc(S[f"wv_ld{h}"], 16)
            sp.dma_start(xin[:, 1, :], x_t[1]).then_inc(x_ld[1], 16)

            def load_w(n, first, second, wait=True):
                if wait:
                    sp.wait_ge(S["wq_lo"], n * 2)
                for half, c in enumerate((first, second)):
                    sp.dma_start(raw_w[:, :, HD * half:HD * half + HD], w_cols[:, :, bass.ds(c, HD)])\
                      .then_inc(S["wraw_ld"], 16)

            def load_qa(i):
                load_w(3 * i + 1, QA0 + i * HD, QA0 + 256 + i * HD)

            def load_qb(i):
                load_w(3 * i + 2, QB0 + i * P, QB0 + HD + i * P)

            def load_kb(i):
                load_w(3 * i + 3, KB0 + i * P, KB0 + HD + i * P)

            def load_v1(i):
                cs = bass.ds(i * P, P)
                for s0, L, vt in ((0, 512, 0), (512, 1024, 5)):
                    nb = L // P
                    mid = vb_d[s0 + 64:s0 + L - 64, cs].rearrange("(t p) c -> p t c", p=P)
                    sp.dma_start(V1[:, vt + 1:vt + nb, :], mid).then_inc(S["v1_loaded"], 16)
                    sp.dma_start(V1[0:64, vt, :], vb_d[s0:s0 + 64, cs]).then_inc(S["v1_loaded"], 16)
                    sp.dma_start(V1[0:64, vt + nb, :], vb_d[s0 + L - 64:s0 + L, cs])\
                      .then_inc(S["v1_loaded"], 16)

            def load_v2(i):
                cs = bass.ds(i * P, P)
                sp.dma_start(V2[:, 0:4, :], vb_d[0:512, cs].rearrange("(s r) c -> s r c", r=4))\
                  .then_inc(S["v2_loaded"], 16)
                for b in range(2):
                    sp.dma_start(V2[:, 4 + b:12:2, :],
                                 vb_d[512 + 512 * b:1024 + 512 * b, cs].rearrange("(s r) c -> s r c", r=4))\
                      .then_inc(S["v2_loaded"], 16)

            def load_x(t, s):
                sp.wait_ge(S["xt_made"], t - 1)
                sp.dma_start(xin[:, s, :], x_t[t]).then_inc(x_ld[s], 16)

            def store_v(t, s):
                sp.wait_ge(S["v_ready"], t + 1)
                sp.dma_start(vb_t[t], vst[:, s, :]).then_inc(vb_st[s], 16)

            load_w(0, KA0, KA0 + HD, wait=False)
            with sp.Fori(0, TILES // 2 - 1) as i:
                for s in range(2):
                    load_x(2 * i + 2 + s, s)
                    store_v(2 * i + s, s)
            load_qa(0)
            for s in range(2):
                store_v(TILES - 2 + s, s)
            for s in range(2):
                sp.wait_ge(vb_st[s], 16 * (TILES // 2) + 16)
            sp.wait_ge(S["xt_made"], TILES)
            sp.dma_start(tA, tab_a[0]).then_inc(S["ta_loaded"], 16)
            load_qb(0)
            sp.dma_start(t1, tab_1[0]).then_inc(S["t1_loaded"], 16)
            sp.dma_start(t2, tab_2[0]).then_inc(S["t2_loaded"], 16)
            load_v1(0)
            load_v2(0)
            load_kb(0)
            sp.dma_start(w_rt, w_router.rearrange("(k p) e -> p k e", p=P)).then_inc(S["wr_loaded"], 16)
            sp.dma_start(rbias, router_bias.partition_broadcast(P)).then_inc(S["wr_loaded"], 16)
            for c in range(2):
                sp.dma_start(nsink[:, c:8:2], sink[4 * c:4 * c + 4].partition_broadcast(P),
                             allow_slow_non_contiguous=True).then_inc(S["wr_loaded"], 16)
            for c in range(2):
                sp.dma_start(gains[HD * c:HD * c + HD, 0:4],
                             norm_a[256 * c:256 * c + 256].rearrange("(i p) -> p i", p=HD),
                             allow_slow_non_contiguous=True).then_inc(S["wo_loaded"], 16)
            sp.dma_start(gains[:, 4:8], norm_b.rearrange("(k p) -> p k", p=P),
                         allow_slow_non_contiguous=True).then_inc(S["wo_loaded"], 16)
            sp.wait_ge(S["ones_ready"], 1)
            def zero_y(n):
                rest = (SLOT_TILES * ST - 2 * TOKENS) // ZERO_PARTS
                sp.dma_start(y_d[bass.ds(n * rest + 2 * TOKENS, rest), :]
                             .rearrange("(p a) (h d) -> p (a h) d", p=P, d=256),
                             zeros.unsqueeze(1).to_broadcast([P, 4 * rest // P, 256]))\
                  .then_inc(S["y_zeroed"], 16)

            def store_o_prompt(i):
                cs = bass.ds(i * (2 * OW) + 4 * PAIRS * OW, 2 * OW)
                sp.dma_start(o_d[0:512, cs].rearrange("(s r) e -> s r e", r=4),
                             ost[2].rearrange("p t h e -> p t (h e)")[:, 0:4, :]).then_inc(S["o2_st0"], 16)

            def store_o(kind, i):
                c0 = (2 * PAIRS * kind) * OW
                sem = S[("oA_st", "o1_st", "o2_st1")[kind]]
                cs = bass.ds(i * (2 * OW) + c0, 2 * OW)
                flat = ost[kind].rearrange("p t h e -> p t (h e)")
                if kind < 2:
                    sp.dma_start(o_d[:, cs].rearrange("(t p) e -> p t e", p=P), flat).then_inc(sem, 16)
                    return
                for b in range(2):
                    sp.dma_start(o_d[512 + 512 * b:1024 + 512 * b, cs].rearrange("(s r) e -> s r e", r=4),
                                 flat[:, 4 + b:12:2, :]).then_inc(sem, 16)

            def pair(i, last):
                zero_y(i * 5)
                if not last:
                    load_qa(i + 1)
                    zero_y(i * 5 + 1)
                    load_qb(i + 1)
                    zero_y(i * 5 + 2)
                    sp.wait_ge(S["biased"], i * UNITS + 24)
                    sp.dma_start(tA, tab_a[i + 1]).then_inc(S["ta_loaded"], 16)
                else:
                    sp.wait_ge(S["proj_made"], 12 + i * 9)
                    for c, part in enumerate((w_out[0:256], w_out[256:512])):
                        sp.dma_start(raw_o[HD * c:HD * c + HD, 0:4, :],
                                     part.rearrange("(i p) n -> p i n", p=HD)).then_inc(S["wo_loaded"], 16)
                    sp.dma_start(raw_o[:, 4:8, :], w_out[512:1024].rearrange("(k p) n -> p k n", p=P))\
                      .then_inc(S["wo_loaded"], 16)
                    sp.dma_start(ln1g, ln1_g.partition_broadcast(P)).then_inc(S["wr_loaded"], 16)
                    sp.dma_start(ln1b, ln1_b.partition_broadcast(P)).then_inc(S["wr_loaded"], 16)
                sp.wait_ge(S["o_ready"], i * 18 + 6)
                store_o(0, i)
                if not last:
                    zero_y(i * 5 + 3)
                    load_kb(i + 1)
                    zero_y(i * 5 + 4)
                    sp.wait_ge(S["biased"], i * UNITS + 48)
                    sp.dma_start(t1, tab_1[i + 1]).then_inc(S["t1_loaded"], 16)
                sp.wait_ge(S["o_ready"], i * 18 + 12)
                store_o(1, i)
                if not last:
                    load_v1(i + 1)
                    sp.wait_ge(S["biased"], i * UNITS + 72)
                    sp.dma_start(t2, tab_2[i + 1]).then_inc(S["t2_loaded"], 16)
                sp.wait_ge(S["o_ready"], i * 18 + 14)
                store_o_prompt(i)
                sp.wait_ge(S["o_ready"], i * 18 + 18)
                store_o(2, i)
                if not last:
                    load_v2(i + 1)

            with sp.Fori(0, PAIRS - 1) as i:
                pair(i, False)
            pair(PAIRS - 1, True)

            sp.wait_ge(S["oA_st"], 16 * PAIRS + 16)
            sp.wait_ge(S["o1_st"], 16 * PAIRS + 16)
            sp.wait_ge(S["o2_st0"], 16 * PAIRS + 16)
            od_ld, xr_ld = (S["od_ld0"], S["od_ld1"]), (S["xr_ld0"], S["xr_ld1"])
            sp.wait_ge(S["o_ready"], 18 * PAIRS)
            sp.wait_ge(S["pT_ready"], UNITS * PAIRS)
            sp.dma_start(odt[:, 0, :], od_t[0]).then_inc(od_ld[0], 16)
            sp.dma_start(xr[:, 0, :], x_t[0]).then_inc(xr_ld[0], 16)
            sp.wait_ge(S["o2_st1"], 32 * PAIRS + 32)
            sp.dma_start(odt[:, 1, :], od_t[1]).then_inc(od_ld[1], 16)

            def load_raw_gu(gate_w, up_w):
                sp.dma_start(raw_gu[:, :, 0:DE], gate_w.rearrange("(k p) f -> p k f", p=P)).then_inc(S["wg_ld"], 16)
                sp.dma_start(raw_gu[:, :, DE:2 * DE], up_w.rearrange("(k p) f -> p k f", p=P))\
                  .then_inc(S["wg_ld"], 16)

            def load_raw_d(w):
                sp.dma_start(raw_d, w.rearrange("(k p) n -> p k n", p=P)).then_inc(S["wd_ld"], 16)

            def c_step(t, s, ok):
                if ok(2):
                    sp.wait_ge(S["merged"], t + 1)
                    sp.dma_start(odt[:, s, :], od_t[t + 2]).then_inc(od_ld[s], 16)
                if ok(1):
                    if not isinstance(t, int) or t > 0:
                        sp.wait_ge(S["res_done"], t)
                    sp.dma_start(xr[:, 1 - s, :], x_t[t + 1]).then_inc(xr_ld[1 - s], 16)

            for t in range(2):
                c_step(t, t, lambda d: True)
                if t == 0:
                    sp.wait_ge(S["wo_lo"], KD)
                    load_raw_gu(ws_gate, ws_up)
                    load_raw_d(ws_down)
            with sp.Fori(0, TILES // 2 - 2) as i:
                for s in range(2):
                    c_step(2 * i + 2 + s, s, lambda d: True)
            for t in range(TILES - 2, TILES):
                c_step(t, t % 2, lambda d, t=t: 0 <= t + d < TILES)

            x1_two = x1_d.rearrange("(q h p) d -> q p h d", h=2, p=P)
            for q in range(SHARED_TILES):
                for h in range(2):
                    sp.wait_ge(S[f"x1_st{h}"], 16 * (q + 1))
                if q > 0:
                    sp.wait_ge(S["base_set"], 2 * q)
                    sp.wait_ge(S["xgT_made"], 2 * q)
                sp.dma_start(slab, x1_two[q]).then_inc(S["rows_ld"], 16)
                if q == 4:
                    sp.wait_ge(S["ej_ready"], 1)
                    sp.wait_ge(S["wg_lo"], KD)
                    first = sp.value_load(ej_i[0:1, 0:1], min_val=0, max_val=NE - 1)
                    load_raw_gu(w_gate[first], w_up[first])
            sp.wait_ge(S["table_ready"], 1)
            more = sp.value_load(more_i[0:1, 0:1], min_val=MIN_PAIRS - 2, max_val=SLOT_TILES // 2 - 2)

            def load_d(j):
                e = sp.value_load(ej_i[0:1, bass.ds(j, 1)], min_val=0, max_val=NE - 1)
                sp.wait_ge(S["wd_lo"], j * 4 + 4)
                load_raw_d(w_down[e])

            def load_gu(j):
                e = sp.value_load(ej_i[0:1, bass.ds(j, 1)], min_val=0, max_val=NE - 1)
                sp.wait_ge(S["wg_lo"], j * KD + KD)
                load_raw_gu(w_gate[e], w_up[e])

            with sp.Fori(0, more * 2 + 3) as j:
                load_gu(j + 1)
                load_d(j)
            load_d(more * 2 + 3)

            sp.wait_ge(S["wg_lo"], (more * 2 + 5) * KD)
            sp.dma_start(ln2g, ln2_g.partition_broadcast(P)).then_inc(S["ln2_loaded"], 16)
            sp.dma_start(ln2b, ln2_b.partition_broadcast(P)).then_inc(S["ln2_loaded"], 16)
            out_st = (S["out_st0"], S["out_st1"])
            for t in range(TILES):
                sp.wait_ge(S["fin_ready"], t + 1)
                sp.dma_start(out_t[t], ob[:, t % 2, :]).then_inc(out_st[t % 2], 16)
            for s in range(2):
                sp.wait_ge(out_st[s], 16 * (TILES // 2))

        @block.tensor
        def _(pe):
            def transposes(src, banks, sem):
                for c in range(KD):
                    last = nc.tensor.transpose(banks[c // 4][:, P * (c % 4):P * (c % 4) + P],
                                               src[:, P * c:P * c + P], ident)
                last.then_inc(sem, 1)

            def three(o, w_hi, w_lo, x_hi, x_lo, first, last):
                nc.tensor.matmul(o, w_hi, x_hi, start=first, stop=False)
                nc.tensor.matmul(o, w_hi, x_lo, start=False, stop=False)
                return nc.tensor.matmul(o, w_lo, x_hi, start=False, stop=last)

            x_ld = (S["x_ld0"], S["x_ld1"])
            pe.wait_ge(S["c_loaded"], 16)

            def xt(t, s, n):
                pe.wait_ge(x_ld[s], 16 * n)
                transposes(xin[:, s, :], bank[2 * s:2 * s + 2], S["xt_made"])

            def vproj(t, s, first=False):
                pe.wait_ge(S["xts_ready"], t + 1)
                for o, c0, c1 in ((bank[4 + s][:, 0:384], 0, 384), (bank[6 + s][:, 0:256], 384, 640)):
                    for k in range(KD):
                        if first and c0 == 0:
                            pe.wait_ge(S["wv_made"], k + 1)
                        a = s * D + k * P
                        last = three(o, xs_hi[:, a:a + P], xs_lo[:, a:a + P], whole(wv_hi, 640)[:, k, c0:c1],
                                     whole(wv_lo, 640)[:, k, c0:c1], k == 0, k == KD - 1)
                last.then_inc(S["v_made"], 1)

            xt(0, 0, 1)
            xt(1, 1, 1)
            vproj(0, 0, True)
            with pe.Fori(0, TILES // 2 - 1) as i:
                xt(2 * i + 2, 0, i + 2)
                vproj(2 * i + 1, 1)
                xt(2 * i + 3, 1, i + 2)
                vproj(2 * i + 2, 0)
            vproj(TILES - 1, 1)

            def proj(w, g, k, n):
                last = three(pslot(n)[:], w[0][:, k * P:k * P + P], w[1][:, k * P:k * P + P],
                             whole(xT_hi, TOKENS)[:, k, 512 * g:512 * g + 512],
                             whole(xT_lo, TOKENS)[:, k, 512 * g:512 * g + 512], k == 0, k == KD - 1)
                if k == KD - 1:
                    last.then_inc(S["proj_made"], 1)

            pe.wait_ge(S["xts_ready"], TILES)
            pe.wait_ge(S["v_ready"], TILES)
            for n in range(6):
                if n % 3 == 0:
                    pe.wait_ge(S["wq_lo"], 2 + 2 * n // 3)
                if n >= 2:
                    pe.wait_ge(S["proj_ready"], n - 1)
                for k in range(KD):
                    proj(w_qb if n < 3 else w_qa, n % 3, k, n)

            def qk(u, i):
                kind, half, tile, q, k, n, tab, v = kinds[u]
                if u == 0:
                    pe.wait_ge(S["proj_ready"], 6 + i * 9)
                if u == 24:
                    pe.wait_ge(S["proj_ready"], 12 + i * 9)
                nc.tensor.matmul(sbank[ring(u)][:, 0:n], q, k, start=True, stop=True).then_inc(S["qk_made"], 1)

            def pT(u, i):
                kind, half, tile, q, k, n, tab, v = kinds[u]
                pe.wait_ge(S["exp_done"], i * UNITS + u + 1)
                at = [sum(r for r, _ in v[:c]) for c in range(len(v))]
                for c in sorted(range(len(v)), key=lambda c: -v[c][0]):
                    r = v[c][0]
                    last = nc.tensor.transpose(bank[2 + u % 2][0:r, P * c:P * c + P],
                                               prob[:, ring(u), at[c]:at[c] + r], ident)
                last.then_inc(S["pT_made"], 1)

            def pv(u, i):
                kind, half, tile, q, k, n, tab, v = kinds[u]
                if u == 24:
                    pe.wait_ge(S["v1_loaded"], (i + 1) * 96)
                if u == 48:
                    pe.wait_ge(S["v2_loaded"], (i + 1) * 48)
                pe.wait_ge(S["pT_ready"], i * UNITS + u + 1)
                o = bank[4 + (u // 4) % 2][:, HD * (u % 4):HD * (u % 4) + HD]
                for c, (r, rows) in enumerate(v):
                    last = nc.tensor.matmul(o, probT[0:r, u % 2, P * c:P * c + P], rows,
                                            start=c == 0, stop=c == len(v) - 1)
                if u % 4 == 3:
                    last.then_inc(S["pv_made"], 1)

            def pair(i, last):
                for g in range(UNITS):
                    for u in ahead(g):
                        if u < UNITS:
                            qk(u, i)
                        elif not last:
                            qk(u - UNITS, i + 1)
                    todo = [m for m in PLAN.get(g, []) if m[0] < 6 or not last]
                    for j, (n, k) in enumerate(todo):
                        if k == 0:
                            pe.wait_ge(S["proj_ready"], i * 9 + (6 if n == 0 else 5 + n if n < 6 else 6 + n))
                            if n == 0:
                                pe.wait_ge(S["wq_lo"], i * 6 + 8)
                            if n == 6:
                                pe.wait_ge(S["wq_lo"], i * 6 + 10)
                        proj((w_qb, w_kb, w_qa)[n // 3], n % 3, k, n)
                    if g + 1 < UNITS:
                        pT(g + 1, i)
                    elif not last:
                        pT(0, i + 1)
                    pv(g, i)

            qk(0, 0)
            qk(1, 0)
            pT(0, 0)
            with pe.Fori(0, PAIRS - 1) as i:
                pair(i, False)
            pair(PAIRS - 1, True)

            pe.wait_ge(S["o_ready"], 18 * PAIRS)
            pe.wait_ge(S["pT_ready"], UNITS * PAIRS)
            pe.wait_ge(S["wr_loaded"], 96)

            def dxt(src, half, q, n):
                if n >= SHARED_TILES:
                    pe.wait_ge(S["g_ld"], (q - (SHARED_TILES - 1)) * 32)
                else:
                    pe.wait_ge(S["rows_ld"], 16 * (q + 1))
                if n > 0 or half:
                    pe.wait_ge(S["xg_lo"], 2 * q + half)
                else:
                    pe.wait_ge(S["oT_lo"], TILES)
                if n == 4 and half == 0:
                    pe.wait_ge(S["cum_read"], 1)
                if n == 6 and half == 0:
                    pe.wait_ge(S["table_ready"], 1)
                transposes(src[:, half, :], bank[5:7] if n == 0 else bank[2:4], S["xgT_made"])

            def op(t, s, first=False, between=None):
                pe.wait_ge(S["oT_lo"], t + 1)
                if first:
                    pe.wait_ge(S["wo_lo"], KD)
                else:
                    pe.wait_ge(S["res_done"], t)
                order = [(k, c) for k in range(KD) for c in range(2)]
                if between is not None:
                    order.sort(key=lambda kc: kc[1])
                for k, c in order:
                    if between is not None and (k, c) == (0, 1):
                        between()
                    a, b = s * D + k * P, k * D + 512 * c
                    last = three(bank[c][:], oT_hi[:, a:a + P], oT_lo[:, a:a + P],
                                 wo_hi[:, b:b + 512], wo_lo[:, b:b + 512], k == 0, k == KD - 1)
                last.then_inc(S["op_made"], 1)

            def x1t(t, s, first=False, banks=bank[2:4]):
                pe.wait_ge(S["x1_ready"], t + 1)
                if not first:
                    pe.wait_ge(S["x1T_ready"], t)
                transposes(x1s[:, s, :], banks, S["x1T_made"])

            def ot(t, s, first=False):
                pe.wait_ge(S["om_ready"], t + 1)
                if not first:
                    pe.wait_ge(S["oT_lo"], t)
                transposes(om[:, s, :], bank[5:7], S["oT_made"])

            def rt(t, first=False):
                pe.wait_ge(S["x1T_ready"], t + 1)
                if not first:
                    pe.wait_ge(S["lg_ready"], t)
                for k in range(KD):
                    last = nc.tensor.matmul(bank[4][:, 0:NE], x1T[:, k, :], w_rt[:, k, :],
                                            start=k == 0, stop=k == KD - 1)
                last.then_inc(S["lg_made"], 1)

            def c_step(t, s, ok, n):
                op(t, s, n == 0, (lambda: dxt(slab, 1, 0, 0)) if n == TILES - 1 else None)
                if ok(-2):
                    x1t(t - 2, s, n == 2)
                if n == 0:
                    ot(1, 1)
                if ok(2):
                    ot(t + 2, s)
                if n == TILES - 2:
                    dxt(slab, 0, 0, 0)
                if ok(-3):
                    rt(t - 3, n == 3)

            ot(0, 0, True)
            for t in range(4):
                c_step(t, t % 2, lambda d, t=t: 0 <= t + d < TILES, t)
            with pe.Fori(0, TILES // 2 - 3) as i:
                for s in range(2):
                    c_step(2 * i + 4 + s, s, lambda d: True, 4)
            for t in range(TILES - 2, TILES):
                c_step(t, t % 2, lambda d, t=t: 0 <= t + d < TILES, t)

            def dgu(q, s, n):
                pe.wait_ge(S["xg_lo"], 2 * q + 2)
                if n == 0 or n >= SHARED_TILES:
                    pe.wait_ge(S["wg_lo"], KD if n == 0 else (q - (SHARED_TILES - 2)) * KD)
                if n > 0:
                    pe.wait_ge(S["hx_made"], q)
                else:
                    pe.wait_ge(S["res_done"], TILES)
                w_hi, w_lo = (whole(w, 2 * DE) for w in w_gu[1 if n < SHARED_TILES else s])
                x_hi, x_lo = whole(xg_hi, 2 * P), whole(xg_lo, 2 * P)
                for f in range(4):
                    o = bank[f // 2][:, 256 * (f % 2):256 * (f % 2) + 256]
                    for k in range(KD):
                        last = three(o, w_hi[:, k, P * f:P * f + P], w_lo[:, k, P * f:P * f + P],
                                     x_hi[:, k, :], x_lo[:, k, :], k == 0, k == KD - 1)
                last.then_inc(S["gx_made"], 1)

            def ddn(q, s, half, n, hi=wd_hi, lo=wd_lo):
                if half == 0:
                    pe.wait_ge(S["h_lo"], q + 1)
                    if n == 0 or n >= SHARED_TILES:
                        pe.wait_ge(S["wd_lo"], 4 if n == 0 else (q - (SHARED_TILES - 2)) * 4)
                if n > 0:
                    pe.wait_ge(S["y_read0" if half == 0 else "y_read1"], q)
                else:
                    pe.wait_ge(S["lg_ready"], TILES)
                for k in range(2):
                    for c in range(2):
                        a, b = s * 512 + k * 256 + half * P, k * D + 512 * c
                        last = three(bank[4 + 2 * half + c][:], h_hi[:, a:a + P], h_lo[:, a:a + P],
                                     hi[:, b:b + 512], lo[:, b:b + 512], k == 0, k == 1)
                last.then_inc(S["dx_made"], 1)

            def d_step(q, s, n, last=False):
                dgu(q, s, n)
                src = slab if n + 1 < SHARED_TILES else xg
                if not last:
                    dxt(src, 0, q + 1, n + 1)
                if n == 0:
                    rt(TILES - 2)
                    x1t(TILES - 1, 1, banks=bank[5:7])
                if n > 0:
                    ddn(q - 1, 1 - s, 0, n - 1)
                if not last:
                    dxt(src, 1, q + 1, n + 1)
                if n == 0:
                    rt(TILES - 1)
                if n > 0:
                    ddn(q - 1, 1 - s, 1, n - 1)

            pe.wait_ge(S["xg_lo"], 2)
            x1t(TILES - 2, 0, banks=bank[5:7])
            rt(TILES - 3)
            for q in range(SHARED_TILES + 3):
                d_step(q, q % 2, q)
                if q == 2:
                    pe.wait_ge(S["cum_need"], 1)
                    pe.wait_ge(S["xg_lo"], 2 * q + 4)
                    cum = bank[2]
                    nc.tensor.matmul(cum[:, 0:(TILES + 1) * NE], tri, msk.rearrange("p t e -> p (t e)"),
                                     start=True, stop=False)
                    for t in range(TILES):
                        rest = TILES - t
                        last = nc.tensor.matmul(cum[:, (t + 1) * NE:(TILES + 1) * NE], ones,
                                                msk[:, t:t + 1, :].to_broadcast([P, rest, NE]),
                                                start=False, stop=t == TILES - 1)
                    last.then_inc(S["cum_made"], 1)
                if q == 4:
                    pe.wait_ge(S["id_need"], 1)
                    pe.wait_ge(S["xg_lo"], 2 * q + 4)
                    for c in range(2 * TILES):
                        last = nc.tensor.matmul(bank[2][:, 0:2 * COLS], oneA[:, c, :],
                                                oneB[:, c].rearrange("p a b -> p (a b)"),
                                                start=c == 0, stop=c == 2 * TILES - 1)
                    last.then_inc(S["idm_made"], 1)
            more = pe.value_load(more_i[0:1, 0:1], min_val=MIN_PAIRS - 2, max_val=SLOT_TILES // 2 - 2)
            with pe.Fori(0, more) as i:
                d_step(2 * i + (SHARED_TILES + 3), 1, SHARED_TILES + 3)
                d_step(2 * i + (SHARED_TILES + 4), 0, SHARED_TILES + 4)
            end = more * 2 + (SHARED_TILES + 3)
            d_step(end, 1, SHARED_TILES + 5, last=True)
            ddn(end, 1, 0, SHARED_TILES + 5, *gu0)
            ddn(end, 1, 1, SHARED_TILES + 5, *gu0)

        @block.scalar
        def _(act):
            def copy(o, i):
                return nc.scalar.activation(o, i, ACT.Copy)

            def two_banks(dst, banks, sem):
                copy(dst[:, 0:4, :], banks[0][:].rearrange("p (k c) -> p k c", c=P))
                copy(dst[:, 4:8, :], banks[1][:].rearrange("p (k c) -> p k c", c=P)).then_inc(sem, 1)

            vb_st = (S["vb_st0"], S["vb_st1"])
            for n, c in (("vb_st0", 16), ("vb_st1", 16), ("oA_st", 16), ("o1_st", 16), ("o2_st0", 16), ("o2_st1", 32),
                         ("y_st0", 16), ("y_st1", 16)):
                act.sem_inc(S[n], c)

            def xt(t, s):
                act.wait_ge(S["xt_made"], t + 1)
                for dst, sem in ((whole(xT_hi, TOKENS)[:, :, bass.ds(t * P, P)], None),
                                 (whole(xs_hi, P)[:, KD * s:KD * s + KD, :], S["xs_hi"])):
                    copy(dst[:, 0:4, :], bank[2 * s][:].rearrange("p (k c) -> p k c", c=P))
                    last = copy(dst[:, 4:8, :], bank[2 * s + 1][:].rearrange("p (k c) -> p k c", c=P))
                last.then_inc(S["xs_hi"], 1)

            def vproj(t, s, n):
                act.wait_ge(S["v_made"], t + 1)
                act.wait_ge(vb_st[s], n * 16 + 16)
                copy(vst[:, s, 0:384], bank[4 + s][:, 0:384])
                copy(vst[:, s, 384:512], bank[6 + s][:, 0:P])
                copy(Va[:, t, :], bank[6 + s][:, P:2 * P]).then_inc(S["v_ready"], 1)

            def w_split(n, w, free=None):
                act.wait_ge(S["wraw_ld"], n * 32 + 32)
                if free is not None:
                    act.wait_ge(S["proj_made"], free)
                for c in range(2):
                    copy(w[0][:, 512 * c:512 * c + 512], raw_w_t[:, 512 * c:512 * c + 512])\
                      .then_inc(S["wq_hi"], 1)

            for k in range(KD):
                act.wait_ge(S[f"wv_ld{k // 4}"], 32)
                copy(wv_hi[:, 640 * k:640 * k + 640], raw_v[:, k, :]).then_inc(S["wv_hi"], 1)
                if k == 0:
                    xt(0, 0)
            with act.Fori(0, TILES // 2 - 1) as i:
                xt(2 * i + 1, 1)
                vproj(2 * i, 0, i)
                xt(2 * i + 2, 0)
                vproj(2 * i + 1, 1, i)
            xt(TILES - 1, 1)
            w_split(0, w_qb)
            vproj(TILES - 2, 0, TILES // 2 - 1)
            w_split(1, w_qa)
            vproj(TILES - 1, 1, TILES // 2 - 1)

            def proj(dst, g, n, count):
                act.wait_ge(S["proj_made"], count)
                copy(dst[:, 512 * g:512 * g + 512], pslot(n)[:]).then_inc(S["proj_ready"], 1)

            for n in range(6):
                proj(KA if n < 3 else QA, n % 3, n, n + 1)
                if n == 2:
                    w_split(2, w_qb, 3)
                if n == 3:
                    w_split(3, w_kb)

            def exps(u, i):
                kind, half, tile, q, k, n, tab, v = kinds[u]
                act.wait_ge(S["biased"], i * UNITS + u + 1)
                nc.scalar.activation(prob[:, ring(u), 0:n], prob[:, ring(u), 0:n], ACT.Exp, scale=-1.0,
                                     bias=ost[kind][:, tile, half, HD:HD + 1],
                                     accum_out=ost[kind][:, tile, half, HD + 1:HD + 2])\
                  .then_inc(S["exp_done"], 1)

            def results(q, i):
                kind, half, tile = kinds[4 * q][0:3]
                act.wait_ge(S["pv_made"], i * 18 + q + 1)
                copy(ost[kind][:, tile:tile + 4, half, 0:HD],
                     bank[4 + q % 2][:, 0:4 * HD].rearrange("p (t e) -> p t e", e=HD)).then_inc(S["o_ready"], 1)

            def pair(i, last):
                for g in range(UNITS):
                    if not last and g in SPLITS:
                        m = SPLITS.index(g)
                        w_split(3 * i + (4 + m), (w_qa, w_qb, w_kb)[m], i * 9 + (6, 9, 12)[m])
                    if last and g >= WO_UNIT and (g - WO_UNIT) % 2 == 0:
                        k, c = (g - WO_UNIT) // 4, (g - WO_UNIT) // 2 % 2
                        act.wait_ge(S["wo_scaled"], k + 1)
                        copy(wo_hi[:, k * D + 512 * c:k * D + 512 * c + 512],
                             raw_o[:, k, 512 * c:512 * c + 512]).then_inc(S["wo_hi"], 1)
                    for n in range(9):
                        if GROUP_END[n] == g - 1 and (n < 6 or not last):
                            proj((QB, KB, QA)[n // 3], n % 3, n, i * 9 + n + 7)
                    for u in ahead(g):
                        if u < UNITS:
                            exps(u, i)
                        elif not last:
                            exps(u - UNITS, i + 1)
                    if g % 4 == 3:
                        results(g // 4, i)

            exps(0, 0)
            exps(1, 0)
            with act.Fori(0, PAIRS - 1) as i:
                pair(i, False)
            pair(PAIRS - 1, True)

            act.wait_ge(S["o_ready"], 18 * PAIRS)
            act.wait_ge(S["oA_st"], 16 * PAIRS + 16)
            act.wait_ge(S["o1_st"], 16 * PAIRS + 16)
            act.wait_ge(S["o2_st1"], 32 * PAIRS + 32)

            def merge_exp(t):
                act.wait_ge(S["merge_need"], t + 1)
                nc.scalar.activation(mD, mD, ACT.Exp).then_inc(S["merge_exp"], 1)

            def squares(t, s):
                act.wait_ge(S["merged"], t + 1)
                for h in range(2):
                    last = nc.scalar.activation(bank[7][:], om[:, s, 512 * h:512 * h + 512], ACT.Square,
                                                scale=512 ** -0.5, accum_out=ssq[:, s, h:h + 1])
                    if h == 0:
                        act.drain()
                last.then_inc(S["squares"], 1)

            def scaled(t, s):
                act.wait_ge(S["rms_rstd"], t + 1)
                for h in range(2):
                    last = nc.scalar.activation(om[:, s, 512 * h:512 * h + 512], om[:, s, 512 * h:512 * h + 512],
                                                ACT.Copy, scale=rms[:, s, h:h + 1])
                last.then_inc(S["om_ready"], 1)

            def norm(t, s):
                squares(t, s)
                scaled(t, s)

            def high(dst, at, step, banks, sem):
                view = dst[:].rearrange("p (k c) -> p k c", c=step)[:, at // step:at // step + KD,
                                                                  at % step:at % step + P]
                copy(view[:, 0:4, :], banks[0][:].rearrange("p (k c) -> p k c", c=P))
                copy(view[:, 4:8, :], banks[1][:].rearrange("p (k c) -> p k c", c=P)).then_inc(sem, 1)

            def oT_high(t, s):
                act.wait_ge(S["oT_made"], t + 1)
                high(oT_hi, s * D, P, bank[5:7], S["oT_hi"])

            def lg(t):
                act.wait_ge(S["lg_made"], t + 1)
                copy(logits[:, t, :], bank[4][:, 0:NE]).then_inc(S["lg_ready"], 1)

            def x1t(t, banks=bank[2:4]):
                act.wait_ge(S["x1T_made"], t + 1)
                two_banks(x1T, banks, S["x1T_ready"])

            def store_x1(t, s):
                act.wait_ge(S["x1_ready"], t + 1)
                act.dma_start(x1_t[t], x1s[:, s, :]).then_inc(S["x1_st1" if s else "x1_st0"], 16)

            def xg_high(q, half, banks=bank[2:4]):
                act.wait_ge(S["xgT_made"], 2 * q + half + 1)
                high(xg_hi, half * P, 2 * P, banks, S["xg_hi"])

            def c_step(t, s, ok, n=4):
                if n == 0:
                    merge_exp(2)
                    norm(2, 0)
                if ok(1):
                    oT_high(t + 1, 1 - s)
                if ok(2) and n > 0:
                    merge_exp(t + 2)
                if ok(-4):
                    lg(t - 4)
                if ok(-3):
                    x1t(t - 3)
                if ok(2) and n > 0:
                    norm(t + 2, s)
                if n == TILES - 1:
                    xg_high(0, 0, bank[5:7])
                if ok(-1) and ok(0):
                    store_x1(t - 1, 1 - s)

            def gu_high(n_k, k, w):
                nc.scalar.activation(w[0][:, bass.ds(k * 512, 512)], raw_gu.rearrange("p k f -> p (k f)")
                                     [:, bass.ds(k * 512, 512)], ACT.Copy).then_inc(S["wg_hi"], 1)

            x1_t = x1_d.rearrange("(t p) d -> t p d", p=P)
            merge_exp(0)
            squares(0, 0)
            merge_exp(1)
            scaled(0, 0)
            oT_high(0, 0)
            norm(1, 1)
            for t in range(2):
                c_step(t, t % 2, lambda d, t=t: 0 <= t + d < TILES, t)
            act.wait_ge(S["wg_ld"], 32)
            act.wait_ge(S["y_zeroed"], 16 * ZERO_PARTS)
            for t in range(2, 4):
                c_step(t, t % 2, lambda d, t=t: 0 <= t + d < TILES)
                gu_high(0, t - 2, gu1)
            with act.Fori(0, TILES // 2 - 3) as i:
                for s in range(2):
                    c_step(2 * i + 4 + s, s, lambda d: True)
                    gu_high(0, 2 * i + 2 + s, gu1)
            for t in range(TILES - 2, TILES):
                c_step(t, t % 2, lambda d, t=t: 0 <= t + d < TILES, t)

            y_t = y_d.rearrange("(t p) d -> t p d", p=P)

            def gu_split(q, s, n):
                act.wait_ge(S["wg_ld"], (q - 4) * 32)
                if n == SHARED_TILES:
                    act.wait_ge(S["idm_made"], 1)
                    act.wait_ge(S["table_ready"], 1)
                act.wait_ge(S["gx_made"], q - 1)
                for k in range(KD):
                    gu_high(0, k, w_gu[s])

            def dn_split(q, n, dst=wd_hi):
                if dst is not wd_hi:
                    act.wait_ge(S["wd_ld"], (q - 4) * 16)
                    act.wait_ge(S["gx_made"], q)
                elif n == 0:
                    act.wait_ge(S["wd_ld"], 16)
                    act.wait_ge(S["op_made"], TILES)
                else:
                    act.wait_ge(S["wd_ld"], (q - 4) * 16)
                    act.wait_ge(S["dx_made"], 2 * q)
                flat = raw_d.rearrange("p k n -> p (k n)")
                for c in range(4):
                    copy(dst[:, 512 * c:512 * c + 512], flat[:, 512 * c:512 * c + 512]).then_inc(S["wd_hi"], 1)

            def y_rows(q, half, n):
                act.wait_ge(S["dx_made"], 2 * q + half + 1)
                if half == 0:
                    act.wait_ge(S["gcol_ready"], q - (SHARED_TILES - 1))
                act.wait_ge(S["y_st0" if half == 0 else "y_st1"], (q - (SHARED_TILES - 1)) * 16)
                for c in range(2):
                    last = nc.scalar.activation(slab[:, half, 512 * c:512 * c + 512], bank[4 + 2 * half + c][:],
                                                ACT.Copy, scale=gcol[:, half:half + 1])
                last.then_inc(S["y_read0" if half == 0 else "y_read1"], 1)
                act.wait_ge(S["y_read0" if half == 0 else "y_read1"], q + 1)
                act.dma_start(y_t[2 * q + (half - 2 * SHARED_TILES)], slab[:, half, :])\
                   .then_inc(S["y_st0" if half == 0 else "y_st1"], 16)

            def base_set(q):
                for h in range(2):
                    nc.scalar.activation(base[:, 2 * q + h, :], slab[:, h, :], ACT.Copy, scale=ALPHA)\
                      .then_inc(S["base_set"], 1)

            def d_step(q, s, n, last=False):
                if n - 2 >= SHARED_TILES:
                    y_rows(q - 2, 1, n - 2)
                if n - 1 >= SHARED_TILES:
                    dn_split(q - 1, n - 1)
                if last:
                    dn_split(q, n, gu0[0])
                elif n + 1 >= SHARED_TILES:
                    gu_split(q + 1, 1 - s, n + 1)
                if n == 0:
                    dn_split(0, 0)
                if n == 1:
                    for h in range(2):
                        act.wait_ge(S[f"x1_st{h}"], 16 * (TILES // 2))
                if n < SHARED_TILES:
                    act.wait_ge(S["rows_ld"], 16 * (q + 1))
                    base_set(q)
                act.wait_ge(S["gx_made"], q + 1)
                nc.scalar.activation(sg[:, s, :], bank[0][:], ACT.Silu).then_inc(S["sg_ready"], 1)
                if not last:
                    xg_high(q + 1, 0)
                if n == 0:
                    lg(TILES - 2)
                    x1t(TILES - 1, banks=bank[5:7])
                act.wait_ge(S["hx_made"], q + 1)
                copy(h_hi[:, s * 512:s * 512 + 512], hx[:, s, :]).then_inc(S["h_hi"], 1)
                if not last:
                    xg_high(q + 1, 1)
                if n - 1 >= SHARED_TILES:
                    y_rows(q - 1, 0, n - 1)
                if n == 0:
                    lg(TILES - 1)
                    act.wait_ge(S["lg_ready"], TILES)
                    nc.scalar.activation(score.rearrange("p t e -> p (t e)"), logits.rearrange("p t e -> p (t e)"),
                                         ACT.Exp, scale=-1.0).then_inc(S["lgexp_done"], 1)

            xg_high(0, 1, bank[5:7])
            lg(TILES - 4)
            x1t(TILES - 3)
            lg(TILES - 3)
            x1t(TILES - 2, banks=bank[5:7])
            store_x1(TILES - 1, 1)
            for q in range(SHARED_TILES + 3):
                d_step(q, q % 2, q)
            act.wait_ge(S["table_ready"], 1)
            more = act.value_load(more_i[0:1, 0:1], min_val=MIN_PAIRS - 2, max_val=SLOT_TILES // 2 - 2)
            with act.Fori(0, more) as i:
                d_step(2 * i + (SHARED_TILES + 3), 1, SHARED_TILES + 3)
                d_step(2 * i + (SHARED_TILES + 4), 0, SHARED_TILES + 4)
            end = more * 2 + (SHARED_TILES + 3)
            d_step(end, 1, SHARED_TILES + 5, last=True)
            y_rows(end - 1, 1, SHARED_TILES + 4)
            y_rows(end, 0, SHARED_TILES + 5)
            y_rows(end, 1, SHARED_TILES + 5)
            for half in range(2):
                act.wait_ge(S["y_st0" if half == 0 else "y_st1"], more * 32 + 80)
            act.sem_inc(S["y_all"], 1)

            for t in range(TILES):
                c = slice(t, t + 1)
                act.wait_ge(S[f"e_add{t}"], 32)
                act.drain()
                nc.scalar.activation(xg[:, 0, :], base[:, t, :], ACT.Copy, accum_out=zsum[:, c])
                act.drain()
                nc.scalar.activation(minus_mean[:, c], zsum[:, c], ACT.Copy, scale=-1.0 / D)
                nc.scalar.activation(mean_32[:, c], zsum[:, c], ACT.Copy, scale=-1.0 / D / 32)
                act.drain()
                nc.scalar.activation(xg[:, 1, :], base[:, t, :], ACT.Square, scale=1.0 / 32,
                                     bias=mean_32[:, c], accum_out=zvar[:, c]).then_inc(S["z_var"], 1)

        @block.vector
        def _(dve):
            V = nc.vector

            V.memset(ones, 1.0)
            V.memset(eps_ln, LN_EPS)
            V.memset(eps_rms, RMS_EPS)
            V.memset(minus_half, -0.5)

            def xt(t, s):
                dve.wait_ge(S["xs_hi"], t + 1)
                hi = plain(whole(xs_hi, P)[:, KD * s:KD * s + KD, :])
                for dst in (whole(xT_lo, TOKENS)[:, :, bass.ds(t * P, P)],
                            whole(xs_lo, P)[:, KD * s:KD * s + KD, :]):
                    for c in range(2):
                        last = V.tensor_tensor(dst[:, 4 * c:4 * c + 4, :],
                                               bank[2 * s + c][:].rearrange("p (k c) -> p k c", c=P),
                                               hi[:, 4 * c:4 * c + 4, :], ALU.subtract)
                last.then_inc(S["xts_ready"], 1)

            def w_split(n, w):
                for c in range(2):
                    dve.wait_ge(S["wq_hi"], n * 2 + (c + 1))
                    V.tensor_tensor(w[1][:, 512 * c:512 * c + 512], raw_w_t[:, 512 * c:512 * c + 512],
                                    plain(w[0][:, 512 * c:512 * c + 512]), ALU.subtract).then_inc(S["wq_lo"], 1)

            for k in range(KD):
                dve.wait_ge(S["wv_hi"], k + 1)
                V.tensor_tensor(wv_lo[:, 640 * k:640 * k + 640], raw_v[:, k, :],
                                plain(wv_hi[:, 640 * k:640 * k + 640]), ALU.subtract).then_inc(S["wv_made"], 1)
                if k == 0:
                    xt(0, 0)
            dve.drain()
            V.memset(zeros, 0.0).then_inc(S["ones_ready"], 1)
            with dve.Fori(0, TILES // 2 - 1) as i:
                xt(2 * i + 1, 1)
                xt(2 * i + 2, 0)
            xt(TILES - 1, 1)
            w_split(0, w_qb)
            w_split(1, w_qa)
            w_split(2, w_qb)
            w_split(3, w_kb)

            def bias(u, i):
                kind, half, tile, q, k, n, tab, v = kinds[u]
                if u % 24 == 0:
                    dve.wait_ge(S[("ta_loaded", "t1_loaded", "t2_loaded")[kind]], i * 16 + 16)
                    if kind == 2:
                        dve.wait_ge(S["o2_st0"], i * 16 + 16)
                        dve.wait_ge(S["o2_st1"], i * 32 + 32)
                    else:
                        dve.wait_ge(S[("oA_st", "o1_st")[kind]], i * 16 + 16)
                dve.wait_ge(S["qk_made"], i * UNITS + u + 1)
                dve.sem_inc(S["units_begun"], 1)
                V.tensor_tensor_reduce(out=prob[:, ring(u), 0:n], in0=sbank[ring(u)][:, 0:n], in1=tab,
                                       scale=-(HD ** -0.5), scalar=BIG, op0=ALU.add, op1=ALU.min,
                                       accum_out=ost[kind][:, tile, half, HD:HD + 1]).then_inc(S["biased"], 1)

            def pT(u, i):
                kind, half, tile, q, k, n, tab, v = kinds[u]
                dve.wait_ge(S["pT_made"], i * UNITS + u + 1)
                if all(r == P for r, _ in v):
                    last = V.tensor_copy(probT[:, u % 2, 0:n], bank[2 + u % 2][:, 0:n])
                else:
                    for c, (r, _) in enumerate(v):
                        last = V.tensor_copy(probT[0:r, u % 2, P * c:P * c + P],
                                             bank[2 + u % 2][0:r, P * c:P * c + P])
                last.then_inc(S["pT_ready"], 1)

            def pair(i, last):
                for g in range(UNITS):
                    if not last and g in SPLITS:
                        m = SPLITS.index(g)
                        w_split(3 * i + (4 + m), (w_qa, w_qb, w_kb)[m])
                    for u in ahead(g):
                        if u < UNITS:
                            bias(u, i)
                        elif not last:
                            bias(u - UNITS, i + 1)
                    if g + 1 < UNITS:
                        pT(g + 1, i)
                    elif not last:
                        pT(0, i + 1)

            bias(0, 0)
            bias(1, 0)
            pT(0, 0)
            with dve.Fori(0, PAIRS - 1) as i:
                pair(i, False)
            pair(PAIRS - 1, True)

            dve.wait_ge(S["wr_loaded"], 96)
            dve.wait_ge(S["o_ready"], 18 * PAIRS)
            dve.wait_ge(S["oA_st"], 16 * PAIRS + 16)
            dve.wait_ge(S["o1_st"], 16 * PAIRS + 16)
            V.tensor_scalar(nsink, nsink, -1.0, None, ALU.mult)
            dve.drain()
            od_ld, xr_ld, x1_st = (S["od_ld0"], S["od_ld1"]), (S["xr_ld0"], S["xr_ld1"]), (S["x1_st0"], S["x1_st1"])

            def low(dst, hi, at, step, banks, sem):
                dv, hv = (a[:].rearrange("p (k c) -> p k c", c=step)[:, at // step:at // step + KD,
                                                                   at % step:at % step + P]
                          for a in (dst, hi))
                for c in range(2):
                    last = V.tensor_tensor(dv[:, 4 * c:4 * c + 4, :],
                                           banks[c][:].rearrange("p (k c) -> p k c", c=P),
                                           plain(hv[:, 4 * c:4 * c + 4, :]), ALU.subtract)
                last.then_inc(sem, 1)

            def oT_low(t, s):
                dve.wait_ge(S["oT_hi"], t + 1)
                low(oT_lo, oT_hi, s * D, P, bank[5:7], S["oT_lo"])

            def residual(t, s, n):
                dve.drain()
                dve.wait_ge(S["op_made"], t + 1)
                dve.wait_ge(xr_ld[s], n)
                for c in range(2):
                    last = V.scalar_tensor_tensor(res[:, 512 * c:512 * c + 512], xr[:, s, 512 * c:512 * c + 512],
                                                  ALPHA, bank[c][:], ALU.mult, ALU.add)
                last.then_inc(S["res_done"], 1)

            def ln1_stats(t, s):
                dve.drain()
                for c in range(2):
                    V.bn_stats(bst[:, c, :], res[:, 512 * c:512 * c + 512])
                dve.drain()
                V.bn_aggr(mv[:, s, :], bst.rearrange("p a b -> p (a b)")).then_inc(S["ln_var"], 1)

            def ln1_apply(t, s, n):
                dve.wait_ge(S["ln_rstd"], t + 1)
                if n is not None:
                    dve.wait_ge(x1_st[s], n)
                    dve.wait_ge(S["x1T_made"], t - 1)
                V.scalar_tensor_tensor(res, res, mv[:, s, 0:1], ln1g, ALU.subtract, ALU.mult)
                dve.drain()
                V.scalar_tensor_tensor(x1s[:, s, :], res, rstd[:, s, :], ln1b, ALU.mult, ALU.add)\
                 .then_inc(S["x1_ready"], 1)

            def heads(s):
                return odt[:, s, :].rearrange("p (k h e) -> p k h e", k=3, e=OW)

            def merge_max(t, s, n):
                dve.wait_ge(od_ld[s], n)
                nm = heads(s)[:, :, :, HD]
                V.tensor_tensor(mM[:, 0, :], nm[:, 0, :], nsink, ALU.min)
                V.tensor_tensor(mM[:, 1, :], nm[:, 1, :], nm[:, 2, :], ALU.min)
                dve.drain()
                V.tensor_tensor(mD[:, 0:2, :], mM, nm[:, 0:2, :], ALU.subtract)
                V.tensor_tensor(mD[:, 2, :], mM[:, 1, :], nm[:, 2, :], ALU.subtract)
                V.tensor_tensor(mD[:, 3, :], mM[:, 0, :], nsink, ALU.subtract).then_inc(S["merge_need"], 1)

            def merge_factors(t, s):
                dve.wait_ge(S["merge_exp"], t + 1)
                V.tensor_tensor(mL, mD[:, 0:3, :], heads(s)[:, :, :, HD + 1], ALU.mult)
                dve.drain()
                V.tensor_tensor(mR[:, 0, :], mL[:, 0, :], mD[:, 3, :], ALU.add)
                V.tensor_tensor(mR[:, 1, :], mL[:, 1, :], mL[:, 2, :], ALU.add)
                dve.drain()
                V.reciprocal(mR, mR)
                dve.drain()
                V.tensor_tensor(mW[:, 0:2, :], mD[:, 0:2, :], mR, ALU.mult)
                V.tensor_tensor(mW[:, 2, :], mD[:, 2, :], mR[:, 1, :], ALU.mult)
                dve.drain()

            def merge_rows(t, s):
                o2 = junk2.rearrange("p (h e) -> p h e", e=HD)
                V.tensor_tensor(om[:, s, 512:1024].rearrange("p (h e) -> p h e", e=HD), heads(s)[:, 1, :, 0:HD],
                                mW[:, 1, :].unsqueeze(2).to_broadcast([P, 8, HD]), ALU.mult)
                V.tensor_tensor(o2, heads(s)[:, 2, :, 0:HD],
                                mW[:, 2, :].unsqueeze(2).to_broadcast([P, 8, HD]), ALU.mult)
                V.tensor_tensor(om[:, s, 0:512].rearrange("p (h e) -> p h e", e=HD), heads(s)[:, 0, :, 0:HD],
                                mW[:, 0, :].unsqueeze(2).to_broadcast([P, 8, HD]), ALU.mult)
                dve.drain()
                V.tensor_tensor(om[:, s, 512:1024], om[:, s, 512:1024], junk2, ALU.add).then_inc(S["merged"], 1)

            def xg_low(q, half, banks=bank[2:4]):
                dve.wait_ge(S["xg_hi"], 2 * q + half + 1)
                low(xg_lo, xg_hi, half * P, 2 * P, banks, S["xg_lo"])

            def c_step(t, s, m, ok, n=4):
                if ok(-1):
                    residual(t - 1, 1 - s, (m + s) * 16)
                if ok(2):
                    merge_max(t + 2, s, m * 16 + 32)
                if ok(1) and n > 0:
                    oT_low(t + 1, 1 - s)
                if ok(2):
                    merge_factors(t + 2, s)
                    merge_rows(t + 2, s)
                if ok(1) and n == 0:
                    oT_low(t + 1, 1 - s)
                if n == TILES - 1:
                    xg_low(0, 0, bank[5:7])
                if ok(-1):
                    ln1_stats(t - 1, 1 - s)
                    ln1_apply(t - 1, 1 - s, None if isinstance(t, int) and t < 3 else (m + s - 1) * 16)

            for t in range(2):
                merge_max(t, t, 16)
                merge_factors(t, t)
                if t == 0:
                    dve.wait_ge(S["o2_st1"], 32 * PAIRS + 32)
                merge_rows(t, t)
            oT_low(0, 0)
            for t in range(4):
                c_step(t, t % 2, t // 2, lambda d, t=t: 0 <= t + d < TILES, t)
            with dve.Fori(0, TILES // 2 - 3) as i:
                for s in range(2):
                    c_step(2 * i + 4 + s, s, i + 2, lambda d: True)
            for t in range(TILES - 2, TILES):
                c_step(t, t % 2, t // 2, lambda d, t=t: 0 <= t + d < TILES, t)

            def gu_split(q, s, n):
                flat = raw_gu.rearrange("p k f -> p (k f)")
                w_hi, w_lo = w_gu[s]
                for k in range(KD):
                    w = slice(512 * k, 512 * k + 512)
                    dve.wait_ge(S["wg_hi"], (q - 5) * KD + (k + 1))
                    V.tensor_tensor(w_lo[:, w], flat[:, w], plain(w_hi[:, w]), ALU.subtract)\
                     .then_inc(S["wg_lo"], 1)

            def dn_split(q, n, hi=wd_hi, lo=wd_lo):
                flat = raw_d.rearrange("p k n -> p (k n)")
                for c in range(4):
                    w = slice(512 * c, 512 * c + 512)
                    dve.wait_ge(S["wd_hi"], c + 1 if n == 0 else (q - 5) * 4 + (c + 1))
                    V.tensor_tensor(lo[:, w], flat[:, w], plain(hi[:, w]), ALU.subtract)\
                     .then_inc(S["wd_lo"], 1)

            def add_shared(q, half):
                dve.wait_ge(S["dx_made"], 2 * q + half + 1)
                dve.wait_ge(S["base_set"], 2 * q + half + 1)
                for c in range(2):
                    b = base[:, 2 * q + half, 512 * c:512 * c + 512]
                    last = V.tensor_tensor(b, b, bank[4 + 2 * half + c][:], ALU.add)
                last.then_inc(S["y_read0" if half == 0 else "y_read1"], 1)

            def d_step(q, s, n, last=False):
                if 0 <= n - 2 < SHARED_TILES:
                    add_shared(q - 2, 1)
                if n - 1 >= SHARED_TILES:
                    dn_split(q - 1, n - 1)
                if last:
                    dn_split(q, n, *gu0)
                elif n + 1 >= SHARED_TILES:
                    gu_split(q + 1, 1 - s, n + 1)
                if n == 0:
                    dn_split(0, 0)
                if n < len(routing):
                    routing[n]()
                dve.wait_ge(S["sg_ready"], q + 1)
                V.tensor_tensor(hx[:, s, :], sg[:, s, :], bank[1][:], ALU.mult).then_inc(S["hx_made"], 1)
                if not last:
                    xg_low(q + 1, 0)
                dve.wait_ge(S["h_hi"], q + 1)
                V.tensor_tensor(h_lo[:, s * 512:s * 512 + 512], hx[:, s, :],
                                plain(h_hi[:, s * 512:s * 512 + 512]), ALU.subtract).then_inc(S["h_lo"], 1)
                if not last:
                    xg_low(q + 1, 1)
                if 0 <= n - 1 < SHARED_TILES:
                    add_shared(q - 1, 0)

            def ranks(val, tmp, rk, start):
                n = val.shape[1] * val.shape[2] // 4
                v4, c4, r4_ = (a.rearrange("p t e -> p (t e)").rearrange("p (n f) -> p n f", f=4)
                               for a in (val, tmp, rk))
                V.tensor_copy(r4_, start.unsqueeze(1).to_broadcast([P, n, 4]))
                for d in range(1, 4):
                    dve.drain()
                    V.tensor_tensor(c4[:, :, 0:4 - d], v4[:, :, 0:4 - d], v4[:, :, d:4], ALU.is_ge)
                    dve.drain()
                    V.tensor_tensor(r4_[:, :, d:4], r4_[:, :, d:4], c4[:, :, 0:4 - d], ALU.add)
                    dve.drain()
                    V.tensor_tensor(r4_[:, :, 0:4 - d], r4_[:, :, 0:4 - d], c4[:, :, 0:4 - d], ALU.subtract)
                dve.drain()

            def flat(a):
                return a.rearrange("p t e -> p (t e)")

            def route_scores():
                V.memset(msk[:, TILES, :], 0.0)
                dve.wait_ge(S["lgexp_done"], 1)
                V.tensor_scalar(flat(score), flat(score), 1.0, None, ALU.add)
                dve.drain()
                V.reciprocal(flat(score), flat(score))
                dve.drain()
                V.tensor_tensor(bia, score, rbias.unsqueeze(1).to_broadcast([P, TILES, NE]), ALU.add)
                dve.drain()
                ranks(bia, cmp_, rank, rank0)

            def route_groups():
                V.tensor_scalar(flat(rank), flat(rank), 1.5, None, ALU.is_lt)
                dve.drain()
                V.tensor_tensor(flat(cmp_), flat(rank), flat(bia), ALU.mult)
                dve.drain()
                V.tensor_reduce(flat(gsc), flat(cmp_).rearrange("p (n f) -> p n f", f=4), AX.X, ALU.add)
                dve.drain()
                ranks(gsc, gcmp, grank, rank0)
                V.scalar_tensor_tensor(flat(msk[:, 0:TILES, :]).rearrange("p (n f) -> p n f", f=4),
                                       flat(grank).unsqueeze(2).to_broadcast([P, TILES * NGRP, 4]), 0.5,
                                       flat(rank).rearrange("p (n f) -> p n f", f=4),
                                       ALU.is_lt, ALU.mult).then_inc(S["cum_need"], 1)
                dve.drain()
                V.tensor_tensor(flat(msc), flat(msk[:, 0:TILES, :]), flat(score), ALU.mult)
                dve.drain()
                V.tensor_reduce(den, msc, AX.X, ALU.add)
                dve.drain()
                V.reciprocal(den, den)

            def route_slots():
                dve.wait_ge(S["cum_made"], 1)
                V.tensor_scalar(ntil_i[:], bank[2][:, TILES * NE:(TILES + 1) * NE], float(ST - 1), None, ALU.add)
                V.tensor_copy(slot, bank[2][:, 0:TILES * NE].rearrange("p (t e) -> p t e", e=NE))\
                 .then_inc(S["cum_read"], 1)
                dve.drain()
                V.tensor_scalar(ntil_i[:], ntil_i[:], ST.bit_length() - 1, None, ALU.arith_shift_right)
                dve.drain()
                V.tensor_copy(ntil, ntil_i[:])
                dve.drain()
                V.tensor_tensor_scan(tend, ones[:, 0:NE], ntil, 0.0, ALU.mult, ALU.add)
                dve.drain()
                V.tensor_tensor(ntil, tend, ntil, ALU.subtract)
                V.tensor_tensor(cmpj, iota_j[:, 0:SLOT_TILES].unsqueeze(2).to_broadcast([P, SLOT_TILES, NE]),
                                tend.unsqueeze(1).to_broadcast([P, SLOT_TILES, NE]), ALU.is_ge)
                V.tensor_scalar(more_i[:, 0:1], tend[:, NE - 1:NE], -3.0, None, ALU.add)
                dve.drain()
                V.tensor_reduce(ej, cmpj, AX.X, ALU.add)
                V.tensor_scalar(ntil, ntil, float(ST), None, ALU.mult)
                V.tensor_scalar(more_i[:, 0:1], more_i[:, 0:1], 1, None, ALU.arith_shift_right)
                dve.drain()
                V.tensor_scalar(ej_i[:], ej, float(NE - 1), None, ALU.min).then_inc(S["ej_ready"], 1)
                V.tensor_tensor(slot, slot, ntil.unsqueeze(1).to_broadcast([P, TILES, NE]), ALU.add)
                dve.drain()
                V.tensor_tensor(flat(slot), flat(slot), flat(msk[:, 0:TILES, :]), ALU.mult)
                dve.drain()
                V.tensor_reduce(two[:, :, 1], slot, AX.X, ALU.max)
                V.tensor_reduce(two[:, :, 0], slot, AX.X, ALU.add)
                dve.drain()
                V.tensor_tensor(two[:, :, 0], two[:, :, 0], two[:, :, 1], ALU.subtract)
                V.tensor_tensor(cmp_, slot, two[:, :, 1:2].to_broadcast([P, TILES, NE]), ALU.is_equal)
                dve.drain()
                V.tensor_copy(two_i[:], two)
                V.tensor_tensor(flat(cmp_), flat(cmp_), flat(msc), ALU.mult)
                dve.drain()
                V.tensor_reduce(gate[:, :, 1], cmp_, AX.X, ALU.add)
                V.tensor_tensor(flat(msc), flat(msc), flat(cmp_), ALU.subtract)
                V.tensor_scalar(rq_i[:, 0, :], flat(two_i[:]), P - 1, None, ALU.bitwise_and)
                V.tensor_scalar(rq_i[:, 1, :], flat(two_i[:]), 7, None, ALU.arith_shift_right)
                dve.drain()
                V.tensor_reduce(gate[:, :, 0], msc, AX.X, ALU.add)
                V.tensor_copy(flat(rq), flat(rq_i[:]))
                dve.drain()
                V.tensor_tensor(gate, gate, den.unsqueeze(2).to_broadcast([P, TILES, 2]), ALU.mult)

            def route_tables():
                V.tensor_tensor(oneA, rq[:, 0, :].unsqueeze(2).to_broadcast([P, 2 * TILES, P]),
                                iota_p.unsqueeze(1).to_broadcast([P, 2 * TILES, P]), ALU.is_equal)
                V.tensor_tensor(oneB[:, :, 0, :], rq[:, 1, :].unsqueeze(2).to_broadcast([P, 2 * TILES, COLS]),
                                iota_j.unsqueeze(1).to_broadcast([P, 2 * TILES, COLS]), ALU.is_equal)
                dve.drain()
                V.tensor_tensor(oneB[:, :, 1, :], oneB[:, :, 0, :],
                                flat(gate).unsqueeze(2).to_broadcast([P, 2 * TILES, COLS]), ALU.mult)
                dve.drain()
                for h in range(2):
                    last = V.tensor_tensor(oneB[:, h::2, 0, :], oneB[:, h::2, 0, :],
                                           token_id.unsqueeze(2).to_broadcast([P, TILES, COLS]), ALU.mult)
                last.then_inc(S["id_need"], 1)

            def route_done():
                dve.wait_ge(S["idm_made"], 1)
                V.tensor_copy(gtab, bank[2][:, COLS:2 * COLS])
                V.tensor_copy(idtab[:], bank[2][:, 0:COLS]).then_inc(S["table_ready"], 1)

            routing = [lambda: None, route_scores, route_groups, route_slots, route_tables]
            xg_low(0, 1, bank[5:7])
            residual(TILES - 1, 1, 16 * (TILES // 2))
            ln1_stats(TILES - 1, 1)
            ln1_apply(TILES - 1, 1, 16 * (TILES // 2 - 1))
            for q in range(SHARED_TILES + 3):
                if q == SHARED_TILES - 1:
                    route_done()
                d_step(q, q % 2, q)
            more = dve.value_load(more_i[0:1, 0:1], min_val=MIN_PAIRS - 2, max_val=SLOT_TILES // 2 - 2)
            with dve.Fori(0, more) as i:
                d_step(2 * i + (SHARED_TILES + 3), 1, SHARED_TILES + 3)
                d_step(2 * i + (SHARED_TILES + 4), 0, SHARED_TILES + 4)
            end = more * 2 + (SHARED_TILES + 3)
            d_step(end, 1, SHARED_TILES + 5, last=True)

            dve.wait_ge(S["ln2_loaded"], 32)
            out_st = (S["out_st0"], S["out_st1"])

            def z_out(t, s):
                dve.wait_ge(S["z_rstd"], t + 1)
                if t > 1:
                    dve.wait_ge(out_st[s], t // 2 * 16)
                dve.drain()
                V.scalar_tensor_tensor(zb, base[:, t, :], minus_mean[:, t:t + 1], ln2g, ALU.add, ALU.mult)
                dve.drain()
                V.scalar_tensor_tensor(ob[:, s, :], zb, rstd2[:, t:t + 1], ln2b, ALU.mult, ALU.add)\
                 .then_inc(S["fin_ready"], 1)

            for t in range(TILES):
                z_out(t, t % 2)

        @block.gpsimd
        def _(pool):
            G = nc.gpsimd

            pool.wait_ge(S["wo_loaded"], 96)
            for k in range(KD):
                G.tensor_scalar(raw_o[:, k, :], raw_o[:, k, :], gains[:, k:k + 1], None, ALU.mult)\
                 .then_inc(S["wo_scaled"], 1)
            pool.wait_ge(S["pv_made"], 18 * (PAIRS - 1) + 12)
            pool.wait_ge(S["oA_st"], 16 * PAIRS + 16)
            for k in range(KD):
                w = slice(k * D, k * D + D)
                pool.wait_ge(S["wo_hi"], 2 * k + 2)
                G.tensor_tensor(wo_lo[:, w], raw_o[:, k, :], plain(wo_hi[:, w]), ALU.subtract)\
                 .then_inc(S["wo_lo"], 1)

            def rsqrt(dst, src, eps):
                G.tensor_tensor(dst, src, eps.to_broadcast([P, dst.shape[1]]), ALU.add)
                pool.drain()
                return G.tensor_tensor(dst, dst, minus_half.to_broadcast([P, dst.shape[1]]), ALU.pow)

            def c_step(t, s, ok, k=None):
                if ok(2):
                    pool.wait_ge(S["squares"], t + 3)
                    rsqrt(rms[:, s, :], ssq[:, s, :], eps_rms).then_inc(S["rms_rstd"], 1)
                if ok(-1):
                    pool.wait_ge(S["ln_var"], t)
                    rsqrt(rstd[:, 1 - s, :], mv[:, 1 - s, 1:2], eps_ln).then_inc(S["ln_rstd"], 1)
                if k is not None:
                    pool.wait_ge(S["wg_hi"], k + 1)
                    w = bass.ds(k * 512, 512)
                    G.tensor_tensor(gu1[1][:, w], raw_gu.rearrange("p k f -> p (k f)")[:, w],
                                    plain(gu1[0][:, w]), ALU.subtract).then_inc(S["wg_lo"], 1)

            for t in range(-2, 4):
                c_step(t, t % 2, lambda d, t=t: 0 <= t + d < TILES, t - 2 if t >= 2 else None)
            with pool.Fori(0, TILES // 2 - 3) as i:
                for s in range(2):
                    c_step(2 * i + 4 + s, s, lambda d: True, 2 * i + 2 + s)
            for t in range(TILES - 2, TILES + 1):
                c_step(t, t % 2, lambda d, t=t: 0 <= t + d < TILES)

            pool.wait_ge(S["table_ready"], 1)
            for h in range(2):
                pool.wait_ge(S[f"x1_st{h}"], 16 * (TILES // 2))

            def gather(q, s):
                pool.wait_ge(S["xgT_made"], q * 2)
                G.tensor_copy(idc[:], idtab[:, bass.ds((q - SHARED_TILES) * 2, 2)]).then_inc(S["ids_col"], 1)
                pool.wait_ge(S["ids_col"], q - (SHARED_TILES - 1))
                pool.sem_inc(S["gathers_begun"], 1)
                for h in range(2):
                    G.indirect_dma_start(out=xg[:, h, :], out_offset=None, in_=x1_d,
                                         in_offset=bass.IndirectOffsetOnAxis(ap=idc[:, h:h + 1].bitcast(U32),
                                                                             axis=0)).then_inc(S["g_ld"], 16)

            def weights(q):
                pool.wait_ge(S["y_read1"], q)
                G.tensor_copy(gcol, gtab[:, bass.ds((q - SHARED_TILES) * 2, 2)]).then_inc(S["gcol_ready"], 1)

            gather(SHARED_TILES, 0)
            gather(SHARED_TILES + 1, 1)
            more = pool.value_load(more_i[0:1, 0:1], min_val=MIN_PAIRS - 2, max_val=SLOT_TILES // 2 - 2)
            with pool.Fori(0, more * 2 + 2) as i:
                weights(i + SHARED_TILES)
                gather(i + (SHARED_TILES + 2), None)
            end = more * 2 + (SHARED_TILES + 3)
            weights(end - 1)
            weights(end)

            pool.wait_ge(S["y_all"], 1)

            def add_rows(t, c):
                if c:
                    pool.wait_ge(S[f"e_add{t}"], 16)
                G.indirect_dma_start(out=base[:, t, :], out_offset=None, in_=y_d,
                                     in_offset=bass.IndirectOffsetOnAxis(ap=two_i[:, t, c:c + 1].bitcast(U32),
                                                                         axis=0),
                                     compute_op=ALU.add).then_inc(S[f"e_add{t}"], 16)

            def z_rsqrt(t, s):
                pool.wait_ge(S["z_var"], t + 1)
                G.tensor_tensor(rstd2[:, t:t + 1], zvar[:, t:t + 1], eps_ln, ALU.add).then_inc(S["z_eps"], 1)
                pool.wait_ge(S["z_eps"], t + 1)
                G.tensor_tensor(rstd2[:, t:t + 1], rstd2[:, t:t + 1], minus_half, ALU.pow).then_inc(S["z_rstd"], 1)

            LAG = 2
            for t in range(TILES + 2 * LAG):
                if t < TILES:
                    add_rows(t, 0)
                if LAG <= t < TILES + LAG:
                    add_rows(t - LAG, 1)
                if t >= 2 * LAG:
                    z_rsqrt(t - 2 * LAG, t % 2)


_WEIGHTS = ["w_in", "sink_a", "norm_a", "norm_b", "w_out", "ln1_g", "ln1_b", "w_router", "router_bias",
            "w_gate", "w_up", "w_down", "ws_gate", "ws_up", "ws_down", "ln2_g", "ln2_b"]
_WHOLE = {"w_router", "router_bias"}


def kernel(**inputs):
    import concourse.bacc as _bacc
    from concourse.bass_utils import run_bass_kernel_spmd as _run

    nc = _bacc.Bacc("TRN2", target_bir_lowering=False, num_devices=1)
    arrays, args = {}, []

    def give(name, a):
        a = np.ascontiguousarray(a)
        arrays[f"in_{name}"] = a
        args.append(nc.dram_tensor(f"in_{name}", a.shape, mybir.dt.from_np(a.dtype), kind="ExternalInput").ap())

    give("x", np.concatenate([np.asarray(inputs["x_prompt"])[0], np.asarray(inputs["x_sample"])[0]], 0))
    for name in _WEIGHTS:
        a = np.asarray(inputs[name])
        give(name, a if name in _WHOLE else a[0])
    for name, a in constants().items():
        give(name, a)
    args.append(nc.dram_tensor("out_y", (TOKENS, D), FP32, kind="ExternalOutput").ap())
    encoder_layer(nc, *args)
    r = _run(nc, [arrays], core_ids=[0])
    y = r.results[0]["out_y"]
    return y[0:512].reshape(1, 512, D), y[512:TOKENS].reshape(1, 1024, D)
```
